# Optimizing a Trainium2 kernel written in Bass

```python
import jax
import jax.numpy as jnp
from jax import lax
import numpy as np

D_MODEL = 1024
BATCH = 1
SEQ = 256
DEPTH = 2

HEAD_DIM = 64
RWKV_W = D_MODEL // 4
RWKV_H = RWKV_W // HEAD_DIM
ATT_W = 3 * D_MODEL // 8
ATT_H = ATT_W // HEAD_DIM
GLA_W = D_MODEL - RWKV_W - ATT_W
GLA_H = GLA_W // HEAD_DIM
RWKV_DECAY_RANK = 32
RWKV_AAA_RANK = 32
RWKV_GATE_RANK = 64
RWKV_VRES_RANK = 16
RWKV_GN_EPS = 64e-5
GLA_GATE_RANK = 16
GLA_GATE_TAU = 16.0
GLA_CHUNK = 64
DILATED_BRANCHES = ((128, 1), (512, 4), (2048, 16))
ATT_BLOCK = 128
ROPE_THETA = 500000.0
ROPE_DIMS = HEAD_DIM // 4
FFN_DENSE = 2816
N_EXPERTS = 8
TOP_K = 2
FFN_EXPERT = 3584
RMS_EPS = 1e-5
NEG_INF = -1e30

RWKV_SPLITS = (RWKV_W, RWKV_W, RWKV_W, RWKV_DECAY_RANK, RWKV_AAA_RANK, RWKV_GATE_RANK)
ATT_SPLITS = (ATT_W, ATT_W, ATT_W)
GLA_SPLITS = (GLA_W, GLA_W, GLA_W, GLA_GATE_RANK, GLA_W)
RWKV_COLS = 3 * RWKV_W + RWKV_DECAY_RANK + RWKV_AAA_RANK + RWKV_GATE_RANK
ATT_COLS = 3 * ATT_W
GLA_COLS = 4 * GLA_W + GLA_GATE_RANK
IN_COLS = RWKV_COLS + ATT_COLS + GLA_COLS

kernel_name = 'hybrid_rwkv7_dilated_gla_moe_trunk'

def rms_norm(x, g):
    xf = x.astype(jnp.float32)
    y = xf * lax.rsqrt(jnp.mean(xf * xf, axis=-1, keepdims=True) + RMS_EPS)
    return (y * g.astype(jnp.float32)).astype(x.dtype)

def _split(t, sizes):
    parts, start = [], 0
    for size in sizes:
        parts.append(t[..., start:start + size])
        start += size
    return parts

def _heads(t):
    return t.reshape(t.shape[:-1] + (t.shape[-1] // HEAD_DIM, HEAD_DIM))

def token_shift(y):
    return jnp.pad(y, ((0, 0), (1, 0), (0, 0)))[:, :-1]

def partial_rotary(t, positions):
    half = ROPE_DIMS // 2
    inv_freq = ROPE_THETA ** (-jnp.arange(half, dtype=jnp.float32) / half)
    ang = positions.astype(jnp.float32)[..., None] * inv_freq
    cos = jnp.cos(ang)[:, :, None, :]
    sin = jnp.sin(ang)[:, :, None, :]
    rot = t[..., :ROPE_DIMS].astype(jnp.float32)
    x1, x2 = rot[..., :half], rot[..., half:]
    rot = jnp.concatenate([x1 * cos - x2 * sin, x2 * cos + x1 * sin], axis=-1)
    return jnp.concatenate([rot.astype(t.dtype), t[..., ROPE_DIMS:]], axis=-1)

def _rwkv7_scan(r, w, k, v, a, b):
    B, S, H, N = r.shape

    def step(state, inp):
        r_t, w_t, k_t, v_t, a_t, b_t = inp
        sa = jnp.einsum('bhvk,bhk->bhv', state, a_t)
        state = (state * w_t[:, :, None, :] + sa[..., None] * b_t[:, :, None, :]
                 + v_t[..., None] * k_t[:, :, None, :])
        return state, jnp.einsum('bhvk,bhk->bhv', state, r_t)

    xs = tuple(t.transpose(1, 0, 2, 3) for t in (r, w, k, v, a, b))
    _, out = lax.scan(step, jnp.zeros((B, H, N, N), jnp.float32), xs)
    return out.transpose(1, 0, 2, 3)

def rwkv7_group(y, mu, w0, w2, a0, a2, g2, k_k, k_a, r_k, ln_g, ln_b, v_first, vres):
    B, S, _ = y.shape
    yf = y.astype(jnp.float32)
    ym = yf + (token_shift(yf) - yf) * mu
    r, k, v, xw, xa, xg = _split(ym, RWKV_SPLITS)
    w_log = -jax.nn.softplus(-(w0 + jnp.tanh(xw) @ w2)) - 0.5
    decay = jnp.exp(-jnp.exp(w_log))
    a = jax.nn.sigmoid(a0 + xa @ a2)
    g = jax.nn.sigmoid(xg) @ g2
    if vres is None:
        v_first = v
    else:
        v0, v1, v2 = vres
        v = v + (v_first - v) * jax.nn.sigmoid(v0 + (v @ v1) @ v2)
    r, k, v, decay, a = (_heads(t) for t in (r, k, v, decay, a))
    kk = k * _heads(k_k)
    kk = kk * lax.rsqrt(jnp.maximum(jnp.sum(kk * kk, axis=-1, keepdims=True), 1e-24))
    k = k * (1.0 + (a - 1.0) * _heads(k_a))
    o = _rwkv7_scan(r, decay, k, v, -kk, kk * a)
    mean = jnp.mean(o, axis=-1, keepdims=True)
    var = jnp.mean(jnp.square(o - mean), axis=-1, keepdims=True)
    o = ((o - mean) * lax.rsqrt(var + RWKV_GN_EPS)).reshape(B, S, RWKV_W) * ln_g + ln_b
    bonus = (jnp.sum(r * k * r_k, axis=-1, keepdims=True) * v).reshape(B, S, RWKV_W)
    return (o + bonus) * g, v_first

def _to_residue_blocks(t, dil, n_blk):
    B, S, H, Dh = t.shape
    L = S // dil
    t = t.reshape(B, L, dil, H, Dh).transpose(0, 2, 1, 3, 4)
    t = jnp.pad(t, ((0, 0), (0, 0), (0, n_blk * ATT_BLOCK - L), (0, 0), (0, 0)))
    return t.reshape(B, dil, n_blk, ATT_BLOCK, H, Dh)

def _with_previous_block(t):
    prev = jnp.pad(t, ((0, 0), (0, 0), (1, 0), (0, 0), (0, 0), (0, 0)))[:, :, :-1]
    return jnp.concatenate([prev, t], axis=3)

def dilated_branch(q, k, v, window, dil):
    B, S, H, Dh = q.shape
    L = S // dil
    n_blk = -(-L // ATT_BLOCK)
    span = window // dil
    qb = _to_residue_blocks(q, dil, n_blk)
    kb = _with_previous_block(_to_residue_blocks(k, dil, n_blk))
    vb = _with_previous_block(_to_residue_blocks(v, dil, n_blk)).astype(jnp.float32)
    qi = jnp.arange(ATT_BLOCK)[:, None]
    kc = jnp.arange(2 * ATT_BLOCK)[None, :]
    rel = qi + ATT_BLOCK - kc
    key_idx = jnp.arange(n_blk)[:, None, None] * ATT_BLOCK + kc[None] - ATT_BLOCK
    valid = (rel >= 0) & (rel <= span) & (key_idx >= 0)
    s = jnp.einsum('brnqhd,brnkhd->brnhqk', qb, kb, preferred_element_type=jnp.float32)
    s = jnp.where(valid[None, None, :, None], s, NEG_INF)
    m = jnp.max(s, axis=-1, keepdims=True)
    p = jnp.exp(s - m)
    den = jnp.sum(p, axis=-1)
    o = jnp.einsum('brnhqk,brnkhd->brnqhd', p, vb) / den.transpose(0, 1, 2, 4, 3)[..., None]
    lse = (m[..., 0] + jnp.log(den)).transpose(0, 1, 2, 4, 3)
    o = o.reshape(B, dil, n_blk * ATT_BLOCK, H, Dh)[:, :, :L]
    o = o.transpose(0, 2, 1, 3, 4).reshape(B, S, H, Dh)
    lse = lse.reshape(B, dil, n_blk * ATT_BLOCK, H)[:, :, :L]
    lse = lse.transpose(0, 2, 1, 3).reshape(B, S, H)
    return o, lse

def dilated_attention_group(y, positions):
    B, S, _ = y.shape
    q, k, v = (_heads(t) for t in _split(y, ATT_SPLITS))
    q = partial_rotary(q, positions) * HEAD_DIM ** -0.5
    k = partial_rotary(k, positions)
    outs, lses = [], []
    for window, dil in DILATED_BRANCHES:
        o, lse = dilated_branch(q, k, v, window, dil)
        outs.append(o)
        lses.append(lse)
    alpha = jax.nn.softmax(jnp.stack(lses), axis=0)
    out = jnp.einsum('gbsh,gbshd->bshd', alpha, jnp.stack(outs))
    return out.reshape(B, S, ATT_W)

def _gla_chunked(q, k, v, lg):
    B, S, H, K = q.shape
    V = v.shape[-1]
    C = GLA_CHUNK
    N = S // C
    q, k, v, lg = (t.reshape(B, N, C, H, t.shape[-1]) for t in (q, k, v, lg))
    b = jnp.cumsum(lg, axis=2)
    b_last = b[:, :, -1]
    q_in = q * jnp.exp(b)
    k_in = k * jnp.exp(-b)
    k_end = k * jnp.exp(b_last[:, :, None] - b)
    causal = jnp.tril(jnp.ones((C, C), dtype=bool))
    att = jnp.where(causal, jnp.einsum('bnihk,bnjhk->bnhij', q_in, k_in), 0.0)
    o_intra = jnp.einsum('bnhij,bnjhv->bnihv', att, v)
    kv = jnp.einsum('bnjhk,bnjhv->bnhkv', k_end, v)

    def step(state, inp):
        kv_n, decay_n = inp
        return state * decay_n[..., None] + kv_n, state

    _, s_before = lax.scan(step, jnp.zeros((B, H, K, V), jnp.float32),
                           (kv.transpose(1, 0, 2, 3, 4), jnp.exp(b_last).transpose(1, 0, 2, 3)))
    o_inter = jnp.einsum('bnihk,nbhkv->bnihv', q_in, s_before)
    return (o_intra + o_inter).reshape(B, S, H, V)

def gla_group(y, gate_up, gate_b, norm_g):
    B, S, _ = y.shape
    yf = y.astype(jnp.float32)
    q, k, v, gd, og = _split(yf, GLA_SPLITS)
    lg = jax.nn.log_sigmoid(gd @ gate_up + gate_b) / GLA_GATE_TAU
    o = _gla_chunked(_heads(q) * HEAD_DIM ** -0.5, _heads(k), _heads(v), _heads(lg))
    o = o * lax.rsqrt(jnp.mean(o * o, axis=-1, keepdims=True) + RMS_EPS) * norm_g
    return o.reshape(B, S, GLA_W) * jax.nn.silu(og)

def swiglu(h, w_gate, w_up, w_down):
    return (jax.nn.silu(h @ w_gate) * (h @ w_up)) @ w_down

def moe_swiglu(h, w_router, w_gate, w_up, w_down):
    logits = jnp.einsum('bsd,de->bse', h, w_router, preferred_element_type=jnp.float32)
    top_val, top_idx = lax.top_k(logits, TOP_K)
    gates = jax.nn.softmax(top_val, axis=-1)
    combine = jnp.sum(jax.nn.one_hot(top_idx, N_EXPERTS, dtype=jnp.float32) * gates[..., None], axis=-2)
    combine = combine.astype(h.dtype)
    out = jnp.zeros_like(h)
    for e in range(N_EXPERTS):
        out = out + combine[..., e:e + 1] * swiglu(h, w_gate[e], w_up[e], w_down[e])
    return out

def setup_inputs(seed: int = 0) -> dict:
    key = jax.random.key(seed)
    ks = jax.random.split(key, 32)

    def nrm(i, shape, scale):
        return jax.random.normal(ks[i], shape, jnp.float32) * scale

    L = DEPTH
    n_dense = (DEPTH + 1) // 2
    n_moe = DEPTH // 2
    D = D_MODEL
    x = nrm(0, (BATCH, SEQ, D), 1.0)
    positions = (jax.random.randint(ks[1], (BATCH, 1), 0, 8192, dtype=jnp.int32)
                 + jnp.arange(SEQ, dtype=jnp.int32)[None, :])
    return {
        'x': x,
        'positions': positions,
        'mix_norm_g': 1.0 + nrm(2, (L, D), 0.02),
        'w_in': nrm(3, (L, D, IN_COLS), D ** -0.5),
        'rwkv_mu': jax.random.uniform(ks[4], (L, RWKV_COLS), jnp.float32),
        'rwkv_w0': nrm(5, (L, RWKV_W), 0.5),
        'rwkv_w2': nrm(6, (L, RWKV_DECAY_RANK, RWKV_W), 0.1),
        'rwkv_a0': nrm(7, (L, RWKV_W), 0.1),
        'rwkv_a2': nrm(8, (L, RWKV_AAA_RANK, RWKV_W), RWKV_AAA_RANK ** -0.5),
        'rwkv_g2': nrm(9, (L, RWKV_GATE_RANK, RWKV_W), RWKV_GATE_RANK ** -0.5),
        'rwkv_k_k': 0.85 + nrm(10, (L, RWKV_W), 0.05),
        'rwkv_k_a': 1.0 + nrm(11, (L, RWKV_W), 0.05),
        'rwkv_r_k': nrm(12, (L, RWKV_H, HEAD_DIM), 0.1),
        'rwkv_ln_g': 1.0 + nrm(13, (L, RWKV_W), 0.02),
        'rwkv_ln_b': nrm(14, (L, RWKV_W), 0.02),
        'rwkv_v0': 1.0 + nrm(15, (L - 1, RWKV_W), 0.1),
        'rwkv_v1': nrm(16, (L - 1, RWKV_W, RWKV_VRES_RANK), RWKV_W ** -0.5),
        'rwkv_v2': nrm(17, (L - 1, RWKV_VRES_RANK, RWKV_W), 0.1 * RWKV_VRES_RANK ** -0.5),
        'gla_gate_up': nrm(18, (L, GLA_GATE_RANK, GLA_W), GLA_GATE_RANK ** -0.5),
        'gla_gate_b': nrm(19, (L, GLA_W), 0.1),
        'gla_norm_g': 1.0 + nrm(20, (L, HEAD_DIM), 0.02),
        'w_out': nrm(21, (L, D, D), D ** -0.5),
        'ffn_norm_g': 1.0 + nrm(22, (L, D), 0.02),
        'ffn_w_gate': nrm(23, (n_dense, D, FFN_DENSE), D ** -0.5),
        'ffn_w_up': nrm(24, (n_dense, D, FFN_DENSE), D ** -0.5),
        'ffn_w_down': nrm(25, (n_dense, FFN_DENSE, D), FFN_DENSE ** -0.5),
        'moe_router': nrm(26, (n_moe, D, N_EXPERTS), D ** -0.5),
        'moe_w_gate': nrm(27, (n_moe, N_EXPERTS, D, FFN_EXPERT), D ** -0.5),
        'moe_w_up': nrm(28, (n_moe, N_EXPERTS, D, FFN_EXPERT), D ** -0.5),
        'moe_w_down': nrm(29, (n_moe, N_EXPERTS, FFN_EXPERT, D), FFN_EXPERT ** -0.5),
        'final_norm_g': 1.0 + nrm(30, (D,), 0.02),
    }

def reference(x, positions, mix_norm_g, w_in, rwkv_mu, rwkv_w0, rwkv_w2, rwkv_a0, rwkv_a2, rwkv_g2,
              rwkv_k_k, rwkv_k_a, rwkv_r_k, rwkv_ln_g, rwkv_ln_b, rwkv_v0, rwkv_v1, rwkv_v2,
              gla_gate_up, gla_gate_b, gla_norm_g, w_out, ffn_norm_g, ffn_w_gate, ffn_w_up, ffn_w_down,
              moe_router, moe_w_gate, moe_w_up, moe_w_down, final_norm_g):
    h = x
    v_first = None
    for layer in range(DEPTH):
        u = rms_norm(h, mix_norm_g[layer])
        proj = u @ w_in[layer]
        y_rwkv = proj[..., :RWKV_COLS]
        y_att = proj[..., RWKV_COLS:RWKV_COLS + ATT_COLS]
        y_gla = proj[..., RWKV_COLS + ATT_COLS:]
        vres = None if layer == 0 else (rwkv_v0[layer - 1], rwkv_v1[layer - 1], rwkv_v2[layer - 1])
        o_rwkv, v_first = rwkv7_group(y_rwkv, rwkv_mu[layer], rwkv_w0[layer], rwkv_w2[layer],
                                      rwkv_a0[layer], rwkv_a2[layer], rwkv_g2[layer], rwkv_k_k[layer],
                                      rwkv_k_a[layer], rwkv_r_k[layer], rwkv_ln_g[layer], rwkv_ln_b[layer],
                                      v_first, vres)
        o_att = dilated_attention_group(y_att, positions)
        o_gla = gla_group(y_gla, gla_gate_up[layer], gla_gate_b[layer], gla_norm_g[layer])
        mixed = jnp.concatenate([o_rwkv, o_att, o_gla], axis=-1).astype(h.dtype)
        h = h + mixed @ w_out[layer]
        u = rms_norm(h, ffn_norm_g[layer])
        i = layer // 2
        if layer % 2 == 0:
            h = h + swiglu(u, ffn_w_gate[i], ffn_w_up[i], ffn_w_down[i])
        else:
            h = h + moe_swiglu(u, moe_router[i], moe_w_gate[i], moe_w_up[i], moe_w_down[i])
    return rms_norm(h, final_norm_g)


_drawn_inputs = setup_inputs


def setup_inputs(seed=0):
    import zlib

    import numpy as np

    out = dict(_drawn_inputs(seed))
    spreads = {}
    factors = {'rwkv_k_k': 4.521,
     'rwkv_ln_b': 3.483,
     'rwkv_v0': 3.897,
     'rwkv_v1': 8.0,
     'rwkv_v2': 8.0,
     'final_norm_g': 2.778}
    for name, (base, spread) in spreads.items():
        noise = np.random.default_rng([zlib.crc32(name.encode()), seed]).standard_normal(out[name].shape)
        drawn = base * np.exp(spread * noise) if base else spread * noise
        out[name] = jnp.asarray(drawn.astype(out[name].dtype))
    for name, factor in factors.items():
        out[name] = (out[name] * factor).astype(out[name].dtype)
    return out
```

```python
from contextlib import ExitStack

import concourse.bass as bass
from concourse import mybir

F32 = mybir.dt.float32
I32 = mybir.dt.int32
ALU = mybir.AluOpType
ACT = mybir.ActivationFunctionType
AX = mybir.AxisListType

P = 128
D = 1024
KB = D // P
T = 256
NT = T // P
HD = 64
CH = 64
NCH = T // CH
RP, AP3, GP = 2, 3, 3
AW = GW = 384
FFN, FEXP, NE = 2816, 3584, 8
FT, ET = FFN // P, FEXP // P
NM = NE * ET
DECAY = 0.6065306597126334
RMS_EPS, GN_EPS = 1e-5, 64e-5
PI = 3.14159265358979
ROUND = 12582912.0
C1, C2, C3 = 6.28125, 1.9350051879882812e-03, 3.0198680390e-07

CAP = 96
RING = 4
SLOT = 3072

CHUNKS = (("r0", "r1", "k0"), ("k1", "v0", "v1"), ("wag", "aq0", "aq1"), ("aq2", "ak0", "ak1"), ("ak2", "gd"),
          ("av",), ("gq0", "gq1", "gq2"), ("gk0", "gk1", "gk2"), ("gv",), ("og0", "og1", "og2"))
WIDTH = {"gd": 16, "av": AW, "gv": GW}
UNITS = (("r0", "r1"), ("k0", "k1"), ("v0", "v1"), ("wag",), ("aq0", "aq1"), ("aq2", "ak0"), ("ak1", "ak2"), ("gd",),
         ("av", 0), ("av", 1), ("gq0", "gq1"), ("gq2", "gk0"), ("gk1", "gk2"), ("gv", 0), ("gv", 1), ("og0", "og1"),
         ("og2",))
NU = len(UNITS)
CHUNK_OF, COL_OF, CHUNK_W = {}, {}, []
for _c, _tiles in enumerate(CHUNKS):
    _at = 0
    for _n in _tiles:
        CHUNK_OF[_n], COL_OF[_n] = _c, _at
        _at += WIDTH.get(_n, P)
    CHUNK_W.append(_at)
LAST_UNIT = [max(u for u, unit in enumerate(UNITS) if any(n in CHUNKS[c] for n in unit)) for c in range(len(CHUNKS))]
OUT_K = (3, 3, 2)
NCI, NCO = len(CHUNKS), len(OUT_K)
LAYER_LOADS = (NCI + NCO + FT, NCI + NCO)
LAYER0 = (0, LAYER_LOADS[0])
MOE0 = sum(LAYER_LOADS)
assert MOE0 % RING == 0 and ET % RING == 0

PCOL, _at = {}, 0
for _n, _w in (("mix_g", 8), ("ffn_g", 8), ("mu", 7), ("w0", 2), ("a0", 2), ("kk", 2), ("ka", 2), ("rk", 2),
               ("lng", 2), ("lnb", 2), ("v0", 2), ("gb", 3), ("gn", 1), ("fin", 8)):
    PCOL[_n] = _at
    _at += _w
NPAR = _at
CCOL, _at = {}, 0
for _n, _w in (("ident", 128), ("ones", 128), ("strict", 128), ("incl", 128), ("lev", 6 * 128), ("rot", 128),
               ("blk", 128), ("lnw", 384), ("reset", 768), ("freq", 1), ("tri8", 64), ("before", 128),
               ("slot", CAP)):
    CCOL[_n] = _at
    _at += _w
NCON = _at


def constants():
    import numpy as np
    c = np.zeros((P, NCON), np.float32)

    def put(name, a):
        c[:a.shape[0], CCOL[name]:CCOL[name] + a.shape[1]] = a

    j, i = np.arange(P)[:, None], np.arange(P)[None, :]
    same = j // CH == i // CH
    put("ident", j == i)
    put("ones", np.ones((P, P)))
    put("strict", (j < i) & same)
    put("incl", (j <= i) & same)
    put("lev", np.concatenate([(j >> (n + 1) == i >> (n + 1)) & ((j >> n) % 2 == 0) & ((i >> n) % 2 == 1)
                               for n in range(6)], axis=1))
    dj, di = j % HD, i % HD
    head = j // HD == i // HD
    put("rot", head * (1.0 * ((di >= 8) & (di < 16) & (dj == di - 8)) - 1.0 * ((di < 8) & (dj == di + 8))))
    put("blk", head)
    w = np.zeros((T, T))
    qi, kj = np.arange(T)[:, None], np.arange(T)[None, :]
    for window, dil in ((128, 1), (512, 4), (2048, 16)):
        w += (qi >= kj) & (qi % dil == kj % dil) & (qi // dil - kj // dil <= window // dil)
    lw = np.where(w > 0, np.log(np.maximum(w, 1)), -1e30)
    put("lnw", np.concatenate([lw[:P, :P], lw[P:, :]], axis=1))
    put("reset", np.broadcast_to((np.arange(768) % CH != 0)[None, :], (P, 768)))
    half = 8
    inv = np.float32(500000.0) ** (-np.arange(half, dtype=np.float32) / np.float32(half))
    f = np.zeros((P, 1), np.float32)
    for p in range(P):
        if p % HD < 16:
            f[p] = inv[p % 8]
    put("freq", f)
    e = np.arange(8)
    put("before", j < i)
    put("slot", np.broadcast_to(np.arange(CAP)[None, :], (P, CAP)))
    put("tri8", np.broadcast_to((e[None, :] < e[:, None]).reshape(1, 64), (P, 64)))
    return c


def build_trunk(nc, xT, pos, con, par, lora, small, v1, router, w_in, w_out, w_ffn, w_moe, out):
    with ExitStack() as ctx:
        def sb(name, shape, dt=F32):
            return ctx.enter_context(nc.sbuf_tensor(name, shape, dt))

        sems = {}

        def S(name):
            if name not in sems:
                sems[name] = ctx.enter_context(nc.semaphore(name))
            return sems[name]

        ring = sb("ring", [P, RING, SLOT])
        hT = sb("hT", [P, KB, T])
        uT = sb("uT", [P, KB, T])
        mixT = sb("mixT", [P, KB, T])
        vfirst = sb("vfirst", [P, RP, T])
        cst = sb("cst", [P, NCON])
        prm = sb("prm", [P, 2, NPAR])
        lor = sb("lor", [P, 2, 256])
        sml = sb("sml", [16, 2, 640])
        v1s = sb("v1s", [P, RP, 16])
        rts = sb("rts", [P, KB, NE])
        cosT = sb("cosT", [P, T])
        sinT = sb("sinT", [P, T])
        std = sb("std", [P, T])
        rstd = sb("rstd", [P, T])
        epsr = sb("epsr", [P, 2])
        sttmp = sb("sttmp", [P, GP, P])

        ypad = sb("ypad", [P, 7, T + 1])
        ym = sb("ym", [P, 7, T])
        aqk = sb("aqk", [P, 6, T])
        av = sb("av", [P, NT, AW])
        gqk = sb("gqk", [P, 6, T])
        gv = sb("gv", [P, NT, GW])
        gd = sb("gd", [16, T])
        og = sb("og", [P, 3, T])

        tw = sb("tw", [P, T])
        sw = sb("sw", [P, RP, T])
        aa = sb("aa", [P, RP, T])
        gg = sb("gg", [P, RP, T])
        At = sb("At", [P, RP, T])
        kk = sb("kk", [P, RP, T])
        Kt = sb("Kt", [P, RP, T])
        Bt = sb("Bt", [P, RP, T])
        bonus = sb("bonus", [P, RP, T])
        lc = sb("lc", [P, RP, NCH])
        tmpA = sb("tmpA", [P, RP, T])
        tmpB = sb("tmpB", [P, RP, T])
        tmpC = sb("tmpC", [P, RP, T])
        tokm = sb("tokm", [P, 4, NT, 256])
        MT = sb("MT", [P, 2, 4, P])
        X = sb("X", [P, 2, 4, P])
        Y = sb("Y", [P, 2, 4, P])
        T1 = sb("T1", [P, 2, 4, P])
        ML = sb("ML", [P, 2, 4, P])
        wt = sb("wt", [P, RP, T])
        st = sb("st", [P, GP, P])

        bank = [ctx.enter_context(nc.psum_tensor(f"bank{i}", [P, 512], F32)) for i in range(8)]

        L_, Li, cs = tmpA, tmpB, tmpC
        nv, c0, uu = tmpA, tmpB, kk
        gE = MT[:, :, :, :].rearrange("p a b c -> p (a b c)")[:, 0:768]
        gEi = X[:, :, :, :].rearrange("p a b c -> p (a b c)")[:, 0:768]
        gS = Y[:, :, :, :].rearrange("p a b c -> p (a b c)")[:, 0:768]
        gU = T1[:, :, :, :].rearrange("p a b c -> p (a b c)")[:, 0:768]
        gM = ML[:, :, :, :].rearrange("p a b c -> p (a b c)")[:, 0:768]
        ktok = tokm[:, :, :, :].rearrange("p a b c -> p (a b c)")[:, 0:768].rearrange("p (t c) -> p t c", t=NT)
        gatt = ym[:, :, :].rearrange("p a b -> p (a b)")[:, 0:1536].rearrange("p (g m c) -> p g m c", g=2, m=6)
        sc = ypad[:, :, :].rearrange("p a b -> p (a b)")[:, 0:768].rearrange("p (b c) -> p b c", b=2)
        pt = ypad[:, :, :].rearrange("p a b -> p (a b)")[:, 768:1536].rearrange("p (b c) -> p b c", b=2)
        lgc = sb("lgc", [P, GP, NCH])
        mxn = sb("mxn", [P, 2, NT])
        den = sb("den", [P, 2, NT])
        rden = sb("rden", [P, 2, NT])
        sil = gE[:, 0:512].rearrange("p (b t) -> p b t", b=2)
        hac = gEi[:, 0:512].rearrange("p (b t) -> p b t", b=2)
        hraw = gS[:, 0:512].rearrange("p (b t) -> p b t", b=2)
        rt = sb("rt", [P, NT, 2, 64])
        lgt = sb("lgt", [P, NT, NE])
        sel = sb("sel", [P, NT, NE])
        posn = sb("posn", [P, NT, NE])
        nmax = sb("nmax", [P, NT])
        rsum = sb("rsum", [P, NT])
        count = sb("count", [P, 1])
        countI = sb("countI", [P, 1], I32)
        cT = tw[0:NE, :]
        combB = sb("combB", [P, NE, T])
        gT = combB
        xg = aqk[:, :, :].rearrange("p a b -> p (a b)")[:, 0:KB * CAP].rearrange("p (k s) -> p k s", k=KB)
        ycol = aqk[:, :, :].rearrange("p a b -> p (a b)")[:, 768:768 + KB * CAP].rearrange("p (k s) -> p k s", k=KB)
        yrow = X[:, :, :, :].rearrange("p a b c -> p (a b c)")
        utok = tokm[:, :, :, :].rearrange("p a b c -> p (a b c)").rearrange("p (t c) -> p t c", t=NT)
        pick = gqk[:, :, :].rearrange("p a b -> p (a b)").rearrange("p (t e s) -> p t e s", t=NT, e=NE)
        pickw = ypad[:, :, :].rearrange("p a b -> p (a b)")[:, 0:NT * NE * CAP]\
            .rearrange("p (t e s) -> p t e s", t=NT, e=NE)
        silg = gE[:, 0:2 * CAP].rearrange("p (b t) -> p b t", b=2)
        hacg = gE[:, 256:256 + 2 * CAP].rearrange("p (b t) -> p b t", b=2)

        def C(name, n=P, at=0):
            return cst[:, CCOL[name] + at:CCOL[name] + at + n]

        def PR(l, name, i=0):
            a = PCOL[name] + i
            return prm[:, l, a:a + 1]

        ident, ones, blk = C("ident"), C("ones"), C("blk")

        def flat(a):
            return a[:, :, :].rearrange("p a b -> p (a b)")

        def loaded(eng, j):
            eng.wait_ge(S(f"slot{j % RING}_loaded"), 16 * (j // RING + 1))

        def wslot(j, w):
            return ring[:, j % RING, 0:KB * w].rearrange("p (k c) -> p k c", k=KB)

        def gu_slot(s):
            return ring[:, s, 0:2 * D].rearrange("p (m k c) -> p m k c", m=2, k=KB)

        def dn_slot(s):
            return ring[:, s, 2 * D:3 * D].rearrange("p (k c) -> p k c", k=KB)

        pb, bs = bank[0:2], bank
        hm = [(t, p) for t in range(NT) for p in range(RP)]
        block = ctx.enter_context(nc.Block())

        @block.sync
        def _(sp):
            sp.dma_start(hT[:, :, :], xT).then_inc(S("x_loaded"), 16)
            sp.dma_start(cst[:, :], con).then_inc(S("par_loaded"), 16)
            sp.dma_start(prm[:, :, :], par).then_inc(S("par_loaded"), 16)
            sp.dma_start(lor[:, :, :], lora).then_inc(S("par_loaded"), 16)
            sp.dma_start(sml[:, :, :], small).then_inc(S("par_loaded"), 16)
            sp.dma_start(v1s[:, :, :], v1).then_inc(S("par_loaded"), 16)
            sp.dma_start(rts[:, :, :], router).then_inc(S("par_loaded"), 16)

            def used(j):
                l = 0 if j < LAYER0[1] else 1
                i = j - LAYER0[l]
                if i < NCI:
                    sp.wait_ge(S("proj_done"), l * NU + LAST_UNIT[i] + 1)
                elif i < NCI + NCO:
                    sp.wait_ge(S("wout_used"), l * NCO + i - NCI + 1)
                else:
                    sp.wait_ge(S("down_done"), i - NCI - NCO + 1)

            def load(j, src, n):
                if j >= RING:
                    used(j - RING)
                sp.dma_start(ring[:, j % RING, 0:n], src).then_inc(S(f"slot{j % RING}_loaded"), 16)

            for l in range(2):
                at = 0
                for c in range(NCI):
                    load(LAYER0[l] + c, w_in[l, :, at:at + KB * CHUNK_W[c]], KB * CHUNK_W[c])
                    at += KB * CHUNK_W[c]
                at = 0
                for c in range(NCO):
                    load(LAYER0[l] + NCI + c, w_out[l, :, at:at + OUT_K[c] * D], OUT_K[c] * D)
                    at += OUT_K[c] * D
                if l == 0:
                    first = NCI + NCO
                    for c in range(RING):
                        load(first + c, w_ffn[c], SLOT)
                    with sp.Fori(0, FT // RING - 1) as it:
                        for s in range(RING):
                            sl = (first + s) % RING
                            sp.wait_ge(S("down_done"), it * RING + (s + 1))
                            sp.dma_start(ring[:, sl, :],
                                         w_ffn[bass.ds(it * RING + (RING + s), 1)].rearrange("a p n -> p (a n)"))\
                              .then_inc(S(f"slot{sl}_loaded"), 16)
                    for c in range(FT // RING * RING, FT):
                        load(first + c, w_ffn[c], SLOT)
            for c in range(RING):
                load(MOE0 + c, w_moe[c], SLOT)
            with sp.Fori(0, NM // RING - 1) as it:
                for s in range(RING):
                    sp.wait_ge(S("down_done"), it * RING + (FT + s + 1))
                    sp.dma_start(ring[:, s, :], w_moe[bass.ds(it * RING + (RING + s), 1)].rearrange("a p n -> p (a n)"))\
                      .then_inc(S(f"slot{s}_loaded"), 16)
            sp.wait_ge(S("final_ready"), 1)
            sp.dma_start(out, uT[:, :, :]).then_inc(S("stored"), 16)
            sp.wait_ge(S("stored"), 16)

        @block.gpsimd
        def _(pool):
            pool.dma_start(tmpA[:, 0, :].bitcast(I32), pos.partition_broadcast(P)).then_inc(S("pos_loaded"), 16)
            pool.wait_ge(S("par_loaded"), 96)
            for l in range(2):
                for lev in range(1, 6):
                    for g in range(2):
                        if lev == 1:
                            pool.wait_ge(S("mt_ready"), 2 * l + g + 1)
                        else:
                            pool.wait_ge(S("t1_done"), l * 10 + (lev - 2) * 2 + g + 1)
                        for m in range(4):
                            last = nc.gpsimd.tensor_tensor(ML[:, g, m, :], MT[:, g, m, :], C("lev", P, lev * P),
                                                           ALU.mult)
                        last.then_inc(S("level_part"), 1)

        @block.tensor
        def _(pe):
            mm = nc.tensor.matmul

            def norm(n):
                pe.wait_ge(S("sq_ready"), n + 1)
                for k in range(KB):
                    last = mm(bank[7][:, 0:T], ones, uT[:, k, :], start=(k == 0), stop=(k == KB - 1))
                last.then_inc(S("norm_summed"), 1)

            def project(l, u):
                unit = UNITS[u]
                i = l * NU + u
                b = pb[u % 2]
                if u >= 2:
                    pe.wait_ge(S("proj_taken"), i - 1)
                if u == 0:
                    pe.wait_ge(S("u_ready"), 2 * l + 1)
                if unit[0] in ("av", "gv"):
                    c = CHUNK_OF[unit[0]]
                    loaded(pe, LAYER0[l] + c)
                    w = wslot(LAYER0[l] + c, AW)
                    t = unit[1]
                    for k in range(KB):
                        last = mm(b[:, 0:AW], uT[:, k, t * P:(t + 1) * P], w[:, k, :], start=(k == 0),
                                  stop=(k == KB - 1))
                else:
                    for i2, name in enumerate(unit):
                        c = CHUNK_OF[name]
                        loaded(pe, LAYER0[l] + c)
                        w = wslot(LAYER0[l] + c, CHUNK_W[c])
                        m = WIDTH.get(name, P)
                        for k in range(KB):
                            last = mm(b[0:m, i2 * T:(i2 + 1) * T], w[:, k, COL_OF[name]:COL_OF[name] + m], uT[:, k, :],
                                      start=(k == 0), stop=(k == KB - 1))
                last.then_inc(S("proj_done"), 1)

            def lora_up(l):
                pe.wait_ge(S("tw_ready"), l + 1)
                for b, (lo, hi) in ((2, (0, 32)), (3, (32, 64)), (4, (64, 128))):
                    for p in range(RP):
                        last = mm(bank[b][:, p * T:(p + 1) * T], lor[lo:hi, l, p * P:(p + 1) * P], tw[lo:hi, :],
                                  start=True, stop=True)
                    last.then_inc(S("lora_done"), 1)

            def value_residual():
                pe.wait_ge(S("v_mixed"), 2)
                for p in range(RP):
                    last = mm(bank[5][0:16, 0:T], v1s[:, p, :], ym[:, 4 + p, :], start=(p == 0), stop=(p == RP - 1))
                last.then_inc(S("v1_done"), 1)
                pe.wait_ge(S("v1_taken"), 1)
                for p in range(RP):
                    last = mm(bank[5][:, p * T:(p + 1) * T], sml[:, 1, p * P:(p + 1) * P], tmpA[0:16, 0, :],
                              start=True, stop=True)
                last.then_inc(S("v2_done"), 1)

            def head_sum(sig, val, done, b, src, n=512):
                pe.wait_ge(S(sig), val)
                mm(bank[b][:, 0:n], blk, src, start=True, stop=True).then_inc(S(done), 1)

            def rwkv_products(l):
                for q, (name, src) in enumerate((("a_ready", At), ("b_ready", Bt), ("k_ready", Kt), ("v_ready", ym))):
                    pe.wait_ge(S(name), l + 1)
                    if q == 0:
                        pe.wait_ge(S("sw_ready"), l + 1)
                        pe.wait_ge(S("bonus_ready"), l + 1)
                    if q == 2:
                        pe.wait_ge(S("gg_ready"), l + 1)
                    if q == 3 and l == 1:
                        pe.wait_ge(S("v_gate"), 1)
                    for t in range(NT):
                        for p in range(RP):
                            x = src[:, p, t * P:(t + 1) * P] if q < 3 else ym[:, 4 + p, t * P:(t + 1) * P]
                            last = nc.tensor.transpose(bank[2 + q][:, t * T + p * P:t * T + (p + 1) * P], x, ident)
                    last.then_inc(S("tok_done"), 1)

            def pairwise(l, n, sig, lhs, rhs):
                for g in range(2):
                    if n:
                        pe.wait_ge(S("pair_taken"), l * 8 + 2 * n + g - 1)
                    for m, (t, p) in enumerate(hm):
                        a = lhs[g * HD:(g + 1) * HD, p, t * P:(t + 1) * P]
                        b = rhs[g * HD:(g + 1) * HD, p, t * P:(t + 1) * P]
                        last = mm(bank[2 + g][:, m * P:(m + 1) * P], a, b, start=True, stop=True)
                    last.then_inc(S("pair_done"), 1)

            def level0(l):
                for g in range(2):
                    pe.wait_ge(S("y0_ready"), 2 * l + g + 1)
                    pe.wait_ge(S("tok_taken"), 4 * l + 4)
                    for m in range(4):
                        last = nc.tensor.transpose(bank[4 + g][:, m * P:(m + 1) * P], T1[:, g, m, :], ident)
                    last.then_inc(S("m0_done"), 1)

            def invert(l):
                for lev in range(1, 6):
                    for g in range(2):
                        i = l * 10 + (lev - 1) * 2 + g
                        pe.wait_ge(S("level_part"), i + 1)
                        if lev == 1:
                            pe.wait_ge(S("x0_ready"), 2 * l + g + 1)
                        else:
                            pe.wait_ge(S("x_updated"), l * 8 + (lev - 2) * 2 + g + 1)
                            pe.wait_ge(S("y_updated"), i - 1)
                        for m in range(4):
                            last = mm(bank[2 + g][:, m * P:(m + 1) * P], ML[:, g, m, :], X[:, g, m, :], start=True,
                                      stop=True)
                        last.then_inc(S("t1_done"), 1)
                    for g in range(2):
                        i = l * 10 + (lev - 1) * 2 + g
                        pe.wait_ge(S("t1_taken"), i + 1)
                        if lev < 5:
                            for m in range(4):
                                last = mm(bank[4 + g][:, m * P:(m + 1) * P], Y[:, g, m, :], T1[:, g, m, :], start=True,
                                          stop=True)
                            last.then_inc(S("xd_done"), 1)
                        for m in range(4):
                            last = mm(bank[2 + g][:, m * P:(m + 1) * P], T1[:, g, m, :], Y[:, g, m, :], start=True,
                                      stop=True)
                        last.then_inc(S("yd_done"), 1)

            def rwkv_solve(l):
                for g in range(2):
                    pe.wait_ge(S("pair_taken"), l * 8 + 4)
                    for m, (t, p) in enumerate(hm):
                        c = p * P + g * HD
                        last = mm(bank[4][:, t * T + c:t * T + c + HD], MT[:, g, m, :], tokm[:, 3, t, c:c + HD],
                                  start=True, stop=True)
                last.then_inc(S("nv_done"), 1)
                for g in range(2):
                    for m, (t, p) in enumerate(hm):
                        c = p * P + g * HD
                        last = mm(bank[5][g * HD:(g + 1) * HD, p * T + t * P:p * T + (t + 1) * P],
                                  tokm[:, 0, t, c:c + HD], Y[:, g, m, :], start=True, stop=True)
                last.then_inc(S("wt_done"), 1)
                pe.wait_ge(S("r_ready"), l + 1)
                pairwise(l, 2, None, Bt, ym_r)
                pairwise(l, 3, None, Kt, ym_r)
                pe.wait_ge(S("nv_taken"), l + 1)
                for g in range(2):
                    for m, (t, p) in enumerate(hm):
                        c = p * P + g * HD
                        last = mm(bank[4][:, t * T + c:t * T + c + HD], Y[:, g, m, :], nv[:, t, c:c + HD],
                                  start=True, stop=True)
                last.then_inc(S("c_done"), 1)

            def rwkv_scan(l):
                ob = bank[5]
                pe.wait_ge(S("wt_taken"), l + 1)
                pe.wait_ge(S("c_taken"), l + 1)
                for n in range(NCH):
                    t, q = n // 2, n % 2
                    rows = slice(q * CH, (q + 1) * CH)
                    tk = slice(n * CH, (n + 1) * CH)
                    pe.wait_ge(S("state_ready"), l * (NCH + 1) + n + 1)
                    for p in range(RP):
                        last = mm(bank[4][rows, p * P:(p + 1) * P], wt[:, p, tk], st[:, p, :], start=True, stop=True)
                    last.then_inc(S("us_done"), 1)
                    for p in range(RP):
                        mm(ob[:, p * T + n * CH:p * T + (n + 1) * CH], st[:, p, :], ym[:, p, tk],
                           start=(n == 0 and p == 0), stop=False, skip_group_check=True)
                    pe.wait_ge(S("u_chunk"), l * NCH + n + 1)
                    for p in range(RP):
                        cc = slice(p * P, (p + 1) * P)
                        mm(bank[4][:, cc], tokm[rows, 1, t, cc], uu[rows, t, cc], start=True, stop=False)
                        last = mm(bank[4][:, cc], tokm[rows, 2, t, cc], tokm[rows, 3, t, cc], start=False, stop=True)
                    last.then_inc(S("ds_done"), 1)
                pe.wait_ge(S("pair_taken"), l * 8 + 8)
                for g in range(2):
                    for m, (t, p) in enumerate(hm):
                        c = p * P + g * HD
                        o = ob[g * HD:(g + 1) * HD, p * T + t * P:p * T + (t + 1) * P]
                        mm(o, uu[:, t, c:c + HD], T1[:, g, m, :], start=False, stop=False, skip_group_check=True)
                        last = mm(o, tokm[:, 3, t, c:c + HD], X[:, g, m, :], start=False, stop=True,
                                  skip_group_check=True)
                last.then_inc(S("ro_done"), 1)

            def group_norm(l):
                head_sum("ro_taken", l + 1, "mean_done", 2, flat(tmpC))
                head_sum("cen_ready", l + 1, "var_done", 3, flat(tmpB))

            def rotary(l):
                for i in range(3):
                    j = l * 3 + i
                    pe.wait_ge(S("proj_taken"), l * NU + 7)
                    if i == 0:
                        pe.wait_ge(S("proj_taken"), l * NU + NU)
                    if i > 0:
                        pe.wait_ge(S("rot_taken"), j)
                    for s in range(2):
                        last = mm(bank[6][:, s * T:(s + 1) * T], C("rot"), aqk[:, 2 * i + s, :], start=True, stop=True)
                    last.then_inc(S("rot_done"), 1)

            def scores(l, h):
                p, g = h // 2, h % 2
                i = l * 6 + h
                r = slice(g * HD, (g + 1) * HD)
                pe.wait_ge(S("qk_ready"), 3 * l + 3)
                if h >= 2:
                    pe.wait_ge(S("score_taken"), i - 1)
                for t in range(NT):
                    n = (t + 1) * P
                    last = mm(bank[g][:, t * P:t * P + n], aqk[r, p, t * P:(t + 1) * P], aqk[r, 3 + p, 0:n],
                              start=True, stop=True)
                last.then_inc(S("score_done"), 1)

            def attend(l, h):
                p, g = h // 2, h % 2
                i = l * 6 + h
                pe.wait_ge(S("prob_ready"), i + 1)
                if h == 0:
                    pe.wait_ge(S("qk_ready"), 3 * l + 3)
                if h >= 1:
                    pe.wait_ge(S("pt_taken"), i)
                for b in range(3):
                    last = nc.tensor.transpose(bank[6][:, b * P:(b + 1) * P], sc[:, h % 2, b * P:(b + 1) * P], ident)
                last.then_inc(S("pt_done"), 1)
                pe.wait_ge(S("pt_taken"), i + 1)
                if g == 0 and h > 0:
                    pe.wait_ge(S("ao_taken"), l * 3 + p)
                r = slice(g * HD, (g + 1) * HD)
                v = slice(h * HD, (h + 1) * HD)
                mm(bank[7][r, 0:P], av[:, 0, v], pt[:, h % 2, 0:P], start=True, stop=True)
                mm(bank[7][r, P:T], av[:, 0, v], pt[:, h % 2, P:2 * P], start=True, stop=False)
                mm(bank[7][r, P:T], av[:, 1, v], pt[:, h % 2, 2 * P:3 * P], start=False, stop=True)\
                    .then_inc(S("ao_done"), 1)

            def gla(l):
                pe.wait_ge(S("score_taken"), 6 * l + 6)
                pe.wait_ge(S("proj_taken"), l * NU + 8)
                for p in range(GP):
                    b = bank[p // 2]
                    last = mm(b[:, (p % 2) * T:(p % 2 + 1) * T], sml[:, l, 256 + p * P:256 + (p + 1) * P], gd[:, :],
                              start=True, stop=True)
                last.then_inc(S("gz_done"), 1)
                pe.wait_ge(S("gk_ready"), l + 1)
                pe.wait_ge(S("pt_taken"), 6 * l + 6)
                pe.wait_ge(S("ao_taken"), 3 * l + 3)
                for t in range(NT):
                    for p in range(GP):
                        last = nc.tensor.transpose(bank[6 + t][:, p * P:(p + 1) * P], gqk[:, 3 + p, t * P:(t + 1) * P],
                                                   ident)
                last.then_inc(S("ktok_done"), 1)
                for g in range(2):
                    r = slice(g * HD, (g + 1) * HD)
                    for m in range(6):
                        t, p = m // 3, m % 3
                        b = bank[2 + g + 2 * (m // 4)]
                        last = mm(b[:, (m % 4) * P:(m % 4 + 1) * P], gqk[r, 3 + p, t * P:(t + 1) * P],
                                  gqk[r, p, t * P:(t + 1) * P], start=True, stop=True)
                    last.then_inc(S("gatt_done"), 1)
                pe.wait_ge(S("ktok_taken"), l + 1)
                for n in range(NCH):
                    t, q = n // 2, n % 2
                    rows = slice(q * CH, (q + 1) * CH)
                    pe.wait_ge(S("gstate_ready"), l * (NCH + 1) + n + 1)
                    for p in range(GP):
                        mm(bank[p // 2][:, (p % 2) * T + n * CH:(p % 2) * T + (n + 1) * CH], st[:, p, :],
                           gqk[:, p, n * CH:(n + 1) * CH], start=(n == 0 and p != 1), stop=False,
                           skip_group_check=True)
                    for p in range(GP):
                        cc = slice(p * P, (p + 1) * P)
                        last = mm(bank[6][:, cc], ktok[rows, t, cc], gv[rows, t, cc], start=True, stop=True)
                    last.then_inc(S("gds_done"), 1)
                pe.wait_ge(S("gatt_taken"), l + 1)
                for g in range(2):
                    for m in range(6):
                        t, p = m // 3, m % 3
                        c = p * P + g * HD
                        last = mm(bank[p // 2][g * HD:(g + 1) * HD, (p % 2) * T + t * P:(p % 2) * T + (t + 1) * P],
                                  gv[:, t, c:c + HD], gatt[:, g, m, :], start=False, stop=True, skip_group_check=True)
                last.then_inc(S("go_done"), 1)
                pe.wait_ge(S("go_squared"), l + 1)
                mm(bank[2][:, :], blk, gS[:, 0:512], start=True, stop=True)
                mm(bank[3][:, 0:T], blk, gS[:, 512:768], start=True, stop=True).then_inc(S("gvar_done"), 1)

            def out_projection(l):
                pe.wait_ge(S("gmix_ready"), l + 1)
                pe.wait_ge(S("rmix_ready"), l + 1)
                pe.wait_ge(S("ao_taken"), 3 * l + 3)
                k = 0
                for c in range(NCO):
                    j = LAYER0[l] + NCI + c
                    loaded(pe, j)
                    w = ring[:, j % RING, 0:OUT_K[c] * D].rearrange("p (k c) -> p k c", k=OUT_K[c])
                    for kk_ in range(OUT_K[c]):
                        for m in range(KB):
                            last = mm(bank[m // 2][:, (m % 2) * T:(m % 2 + 1) * T], w[:, kk_, m * P:(m + 1) * P],
                                      mixT[:, k, :], start=(k == 0 and m % 2 == 0), stop=(k == KB - 1),
                                      skip_group_check=True)
                        k += 1
                    last.then_inc(S("wout_used"), 1)

            def gate_up(slot, par):
                w = gu_slot(slot)
                for m in range(2):
                    for k in range(KB):
                        last = mm(bank[4 + par][:, m * T:(m + 1) * T], w[:, m, k, :], uT[:, k, :], start=(k == 0),
                                  stop=(k == KB - 1))
                last.then_inc(S("gate_up_done"), 1)

            def down(slot, par, first):
                w = dn_slot(slot)
                for m in range(KB):
                    last = mm(bank[m // 2][:, (m % 2) * T:(m % 2 + 1) * T], w[:, m, :], hac[:, par, :],
                              start=(first and m % 2 == 0), stop=False, skip_group_check=True)
                last.then_inc(S("down_done"), 1)

            def channel_mixer(n_chunks, load0, base):
                def gu(c, slot):
                    pe.wait_ge(S(f"slot{slot}_loaded"), 16 * ((load0 + c) // RING + 1) if isinstance(c, int) else c)
                first_slot = load0 % RING
                body = (n_chunks - 1) // RING * RING

                def step_gu(c, s, static):
                    slot = (first_slot + s) % RING
                    wrap = (first_slot + s) // RING
                    turn = (c - s) // RING if static else None
                    return slot, wrap, turn

                loaded(pe, load0)
                pe.wait_ge(S("act_ready"), base) if base else None
                gate_up(first_slot, 0)
                loaded(pe, load0 + 1)
                gate_up((first_slot + 1) % RING, 1)
                pe.wait_ge(S("act_ready"), base + 1)
                down(first_slot, 0, True)
                rounds = (n_chunks - 2) // RING

                def pair(gc, s, slot_load_value):
                    sg = (first_slot + 2 + s) % RING
                    sd = (first_slot + 1 + s) % RING
                    pe.wait_ge(S(f"slot{sg}_loaded"), slot_load_value)
                    pe.wait_ge(S("act_ready"), gc + (base - 1))
                    gate_up(sg, s % 2)
                    pe.wait_ge(S("act_ready"), gc + base)
                    down(sd, (s + 1) % 2, False)

                with pe.Fori(0, rounds) as it:
                    for s in range(RING):
                        n0 = (load0 + 2 + s) // RING + 1
                        pair(it * RING + (2 + s), s, (it + n0) * 16)
                for gc in range(2 + rounds * RING, n_chunks):
                    s = (gc - 2) % RING
                    pair(gc, s, 16 * ((load0 + gc) // RING + 1))
                pe.wait_ge(S("act_ready"), base + n_chunks)
                down((first_slot + n_chunks - 1) % RING, (n_chunks - 1) % 2, False)

            def route():
                pe.wait_ge(S("u_ready"), 4)
                for t in range(NT):
                    for k in range(KB):
                        last = mm(bank[6][:, t * NE:(t + 1) * NE], uT[:, k, t * P:(t + 1) * P], rts[:, k, :],
                                  start=(k == 0), stop=(k == KB - 1))
                last.then_inc(S("logits_done"), 1)
                pe.wait_ge(S("sel_ready"), 1)
                mm(bank[7][:, 0:NE], C("before"), sel[:, 0, :], start=True, stop=True)
                mm(bank[7][:, NE:2 * NE], ones, sel[:, 0, :], start=True, stop=False)
                mm(bank[7][:, NE:2 * NE], C("before"), sel[:, 1, :], start=False, stop=True)
                mm(bank[7][:, 2 * NE:3 * NE], ones, sel[:, 0, :], start=True, stop=False)
                mm(bank[7][:, 2 * NE:3 * NE], ones, sel[:, 1, :], start=False, stop=True)\
                    .then_inc(S("queues_done"), 1)

            def spread_weights():
                pe.wait_ge(S("comb_ready"), 1)
                for t in range(NT):
                    last = nc.tensor.transpose(bank[7][0:NE, t * P:(t + 1) * P], lgt[:, t, :], ident)
                last.then_inc(S("combT_done"), 1)
                pe.wait_ge(S("combT_taken"), 1)
                for e in range(NE):
                    if e >= 2:
                        pe.wait_ge(S("combB_taken"), e - 1)
                    mm(bank[6 + e % 2][:, 0:T], ident[0:NE, e:e + 1].to_broadcast([NE, P]), cT[:, :], start=True,
                       stop=True).then_inc(S("combB_done"), 1)

            def gathered_experts():
                for t in range(NT):
                    for k in range(KB):
                        last = nc.tensor.transpose(bank[2 * t + k // 4][:, (k % 4) * P:(k % 4 + 1) * P],
                                                   uT[:, k, t * P:(t + 1) * P], ident)
                    last.then_inc(S("utok_done"), 1)
                for e in range(NE):
                    pe.wait_ge(S("pick_ready"), e + 1)
                    if e >= 2:
                        pe.wait_ge(S("gt_taken"), e - 1)
                    for t in range(NT):
                        last = nc.tensor.transpose(bank[6 + e % 2][0:CAP, t * P:(t + 1) * P], pickw[:, t, e, :], ident)
                    last.then_inc(S("gt_done"), 1)
                pe.wait_ge(S("utok_taken"), NT)
                pe.wait_ge(S("gt_taken"), NE)

                def gate_up_g(slot, par):
                    w = gu_slot(slot)
                    for m in range(2):
                        for k in range(KB):
                            last = mm(bank[4 + par][:, m * CAP:(m + 1) * CAP], w[:, m, k, :], xg[:, k, :],
                                      start=(k == 0), stop=(k == KB - 1))
                    last.then_inc(S("gate_up_done"), 1)

                def down_g(slot, par, first):
                    w = dn_slot(slot)
                    for m in range(KB):
                        last = mm(bank[6 + m // 4][:, (m % 4) * CAP:(m % 4 + 1) * CAP], w[:, m, :], hacg[:, par, :],
                                  start=(first and m % 4 == 0), stop=False, skip_group_check=True)
                    last.then_inc(S("down_done"), 1)

                with pe.Fori(0, NE) as e:
                    for k in range(KB):
                        for t in range(NT):
                            last = mm(bank[k // 4][:, (k % 4) * CAP:(k % 4 + 1) * CAP],
                                      utok[:, t, k * P:(k + 1) * P],
                                      pick[:, t, bass.ds(e, 1), :].rearrange("p a s -> p (a s)"), start=(t == 0),
                                      stop=(t == NT - 1))
                        if k % 4 == 3:
                            last.then_inc(S("gather_done"), 1)
                    pe.wait_ge(S("xg_first"), e + 1)
                    pe.wait_ge(S("xg_second"), e + 1)
                    for c in range(ET + 1):
                        if c < ET:
                            pe.wait_ge(S(f"slot{c % RING}_loaded"),
                                       e * (16 * ET // RING) + 16 * ((MOE0 + c) // RING + 1))
                            pe.wait_ge(S("act_ready"), e * ET + (FT + c - 1))
                            gate_up_g(c % RING, c % 2)
                        if c:
                            pe.wait_ge(S("act_ready"), e * ET + (FT + c))
                            down_g((c - 1) % RING, (c - 1) % 2, c == 1)
                    pe.wait_ge(S("ycol_ready"), e * 2 + 2)
                    for k in range(KB):
                        last = nc.tensor.transpose(bank[2 + k // 4][0:CAP, (k % 4) * P:(k % 4 + 1) * P],
                                                   ycol[:, k, :], ident)
                        if k % 4 == 3:
                            last.then_inc(S("yrow_done"), 1)
                    pe.wait_ge(S("yrow_ready"), e * 2 + 2)
                    for k in range(KB):
                        last = mm(bank[k // 2][:, (k % 2) * T:(k % 2 + 1) * T], yrow[0:CAP, k * P:(k + 1) * P],
                                  gT[0:CAP, bass.ds(e, 1), :].rearrange("p a t -> p (a t)"), start=True, stop=True)
                        if k % 2:
                            last.then_inc(S("scatter_done"), 1)
                    pe.wait_ge(S("h_added"), e * 4 + 2)

            ym_r = ym
            pe.wait_ge(S("par_loaded"), 96)
            for l in range(2):
                norm(2 * l)
                for u in range(7):
                    project(l, u)
                lora_up(l)
                if l == 1:
                    value_residual()
                project(l, 7)
                project(l, 8)
                pe.wait_ge(S("sw_ready"), l + 1)
                head_sum("kk2_ready", l + 1, "kksum_done", 2, flat(tmpA))
                project(l, 9)
                project(l, 10)
                project(l, 11)
                head_sum("rk_ready", l + 1, "rksum_done", 3, flat(bonus))
                for u in range(12, NU):
                    project(l, u)
                rwkv_products(l)
                pe.wait_ge(S("tok_taken"), 4 * l + 2)
                pairwise(l, 0, None, Bt, At)
                level0(l)
                invert(l)
                pe.wait_ge(S("y_updated"), l * 10 + 10)
                pairwise(l, 1, None, Kt, At)
                rwkv_solve(l)
                rwkv_scan(l)
                group_norm(l)
                rotary(l)
                scores(l, 0)
                for h in range(6):
                    if h < 5:
                        scores(l, h + 1)
                    attend(l, h)
                gla(l)
                out_projection(l)
                norm(2 * l + 1)
                if l == 0:
                    pe.wait_ge(S("u_ready"), 2)
                    channel_mixer(FT, NCI + NCO, 0)
                else:
                    route()
                    pe.wait_ge(S("count_ready"), 1)
                    most = pe.value_load(countI[0:1, 0:1], min_val=0, max_val=T)
                    with pe.If(most < CAP + 1):
                        gathered_experts()
                    with pe.Else():
                        spread_weights()
                        channel_mixer(NM, MOE0, FT)
            norm(4)

        @block.scalar
        def _(act):
            a = nc.scalar.activation
            chain = [0]

            def link(ins):
                chain[0] += 1
                ins.then_inc(S("act_step"), 1)
                act.wait_ge(S("act_step"), chain[0])

            def norm_std(n):
                act.wait_ge(S("norm_summed"), n + 1)
                a(std[:, :], bank[7][:, 0:T], ACT.Sqrt, scale=1.0 / D, bias=epsr[:, 0:1]).then_inc(S("std_ready"), 1)

            def take(l, u):
                unit = UNITS[u]
                act.wait_ge(S("proj_done"), l * NU + u + 1)
                b = pb[u % 2]
                n = len(unit)
                two = b[:, 0:n * T].rearrange("p (a t) -> p a t", a=n) if unit[0] not in ("av", "gv") else None
                if u < 4:
                    dst, src = ypad[:, 2 * u:2 * u + n, 1:T + 1], two
                elif u < 7:
                    dst, src = aqk[:, 2 * (u - 4):2 * (u - 4) + 2, :], two
                elif u == 7:
                    dst, src = gd[:, :], b[0:16, 0:T]
                elif unit[0] == "av":
                    dst, src = av[:, unit[1], :], b[:, 0:AW]
                elif u < 13:
                    dst, src = gqk[:, 2 * (u - 10):2 * (u - 10) + 2, :], two
                elif unit[0] == "gv":
                    dst, src = gv[:, unit[1], :], b[:, 0:GW]
                else:
                    dst, src = og[:, 2 * (u - 15):2 * (u - 15) + n, :], two
                a(dst, src, ACT.Copy).then_inc(S("proj_taken"), 1)

            act.wait_ge(S("par_loaded"), 96)
            act.wait_ge(S("eps_set"), 1)
            act.wait_ge(S("angles_ready"), 1)
            a(cosT[:, :], tmpB[:, 0, :], ACT.Sin)
            a(sinT[:, :], tmpB[:, 1, :], ACT.Sin).then_inc(S("rope_ready"), 1)
            for l in range(2):
                norm_std(2 * l)
                for u in range(4):
                    take(l, u)
                act.wait_ge(S("wag_mixed"), l + 1)
                a(tw[64:128, :], ym[64:128, 6, :], ACT.Sigmoid)
                a(tw[0:32, :], ym[0:32, 6, :], ACT.Tanh)
                a(tw[32:64, :], ym[32:64, 6, :], ACT.Copy).then_inc(S("tw_ready"), 1)
                for u in range(4, 7):
                    take(l, u)
                act.wait_ge(S("lora_done"), 3 * l + 1)
                for p in range(RP):
                    last = a(sw[:, p, :], bank[2][:, p * T:(p + 1) * T], ACT.Sigmoid, bias=PR(l, "w0", p))
                last.then_inc(S("sw_ready"), 1)
                act.wait_ge(S("lora_done"), 3 * l + 2)
                for p in range(RP):
                    last = a(aa[:, p, :], bank[3][:, p * T:(p + 1) * T], ACT.Sigmoid, bias=PR(l, "a0", p))
                last.then_inc(S("aa_ready"), 1)
                if l == 1:
                    act.wait_ge(S("v2_done"), 1)
                    for p in range(RP):
                        last = a(tmpB[:, p, :], bank[5][:, p * T:(p + 1) * T], ACT.Sigmoid, bias=PR(l, "v0", p))
                    last.then_inc(S("v_gate"), 1)
                take(l, 7)
                take(l, 8)
                act.wait_ge(S("kk_floor"), l + 1)
                a(flat(tmpB), flat(tmpB), ACT.Sqrt).then_inc(S("kk_norm"), 1)
                act.wait_ge(S("cs_ready"), l + 1)
                a(flat(tmpA), flat(tmpC), ACT.Exp, scale=-DECAY)
                a(flat(At), flat(sw), ACT.Exp, scale=-DECAY)
                a(flat(Kt), flat(tmpC), ACT.Exp, scale=DECAY).then_inc(S("decay_ready"), 1)
                for u in range(9, NU):
                    take(l, u)
                for q in range(4):
                    act.wait_ge(S("tok_done"), 4 * l + q + 1)
                    a(tokm[:, q, :, :].rearrange("p t c -> p (t c)"), bank[2 + q][:, :], ACT.Copy)\
                        .then_inc(S("tok_taken"), 1)
                for lev in range(1, 6):
                    for g in range(2):
                        i = l * 10 + (lev - 1) * 2 + g
                        act.wait_ge(S("t1_done"), i + 1)
                        if lev > 1:
                            act.wait_ge(S("yd_done"), i - 1)
                        a(T1[:, g, :, :].rearrange("p m c -> p (m c)"), bank[2 + g][:, :], ACT.Copy)\
                            .then_inc(S("t1_taken"), 1)
                act.wait_ge(S("nv_done"), l + 1)
                a(flat(nv), bank[4][:, :], ACT.Copy).then_inc(S("nv_taken"), 1)
                act.wait_ge(S("wt_done"), l + 1)
                a(flat(wt), bank[5][:, :], ACT.Copy).then_inc(S("wt_taken"), 1)
                act.wait_ge(S("c_done"), l + 1)
                a(flat(c0), bank[4][:, :], ACT.Copy).then_inc(S("c_taken"), 1)
                act.wait_ge(S("ro_done"), l + 1)
                a(flat(tmpC), bank[5][:, :], ACT.Copy).then_inc(S("ro_taken"), 1)
                act.wait_ge(S("var_done"), l + 1)
                a(flat(tmpA), bank[3][:, :], ACT.Sqrt, scale=1.0 / HD, bias=epsr[:, 1:2]).then_inc(S("gn_std"), 1)
                for h in range(6):
                    i = l * 6 + h
                    act.wait_ge(S("max_ready"), i + 1)
                    for t in range(NT):
                        n = (t + 1) * P
                        x = sc[:, h % 2, t * P:t * P + n]
                        last = a(x, x, ACT.Exp, bias=mxn[:, h % 2, t:t + 1], accum_out=den[:, h % 2, t:t + 1])
                    last.then_inc(S("exp_done"), 1)
                    act.wait_ge(S("pt_done"), i + 1)
                    if h >= 2:
                        act.wait_ge(S("ao_done"), i - 1)
                    a(pt[:, h % 2, :], bank[6][:, 0:384], ACT.Copy).then_inc(S("pt_taken"), 1)
                    if h % 2:
                        act.wait_ge(S("ao_done"), i + 1)
                        a(mixT[:, RP + h // 2, :], bank[7][:, 0:T], ACT.Copy).then_inc(S("ao_taken"), 1)
                act.wait_ge(S("gabs_ready"), l + 1)
                link(a(gS[:, :], gE[:, :], ACT.Exp, scale=-1.0))
                a(gS[:, :], gS[:, :], ACT.Ln, bias=1.0).then_inc(S("gln_ready"), 1)
                act.wait_ge(S("gcs_ready"), l + 1)
                a(gE[:, :], gM[:, :], ACT.Exp, scale=1.0 / 16)
                a(gEi[:, :], gM[:, :], ACT.Exp, scale=-1.0 / 16).then_inc(S("gdecay_ready"), 1)
                a(gU[:, :], og[:, :, :].rearrange("p a t -> p (a t)"), ACT.Silu).then_inc(S("og_ready"), 1)
                act.wait_ge(S("ktok_done"), l + 1)
                for t in range(NT):
                    last = a(ktok[:, t, :], bank[6 + t][:, 0:384], ACT.Copy)
                last.then_inc(S("ktok_taken"), 1)
                act.wait_ge(S("gvar_done"), l + 1)
                a(gE[:, 0:512], bank[2][:, :], ACT.Sqrt, scale=1.0 / HD, bias=epsr[:, 0:1])
                a(gE[:, 512:768], bank[3][:, 0:T], ACT.Sqrt, scale=1.0 / HD, bias=epsr[:, 0:1])\
                    .then_inc(S("gstd_ready"), 1)
                norm_std(2 * l + 1)

                def silu(c, par, guard=True):
                    act.wait_ge(S("gate_up_done"), c + 1)
                    if guard:
                        act.wait_ge(S("act_ready"), c - 1)
                    a(sil[:, par, :], bank[4 + par][:, 0:T], ACT.Silu).then_inc(S("silu_done"), 1)


                def all_tokens(base, n):
                    for c in range(2):
                        silu(base + c, c, base > 0)
                    with act.Fori(0, (n - 2) // RING) as it:
                        for s in range(RING):
                            silu(it * RING + (base + 2 + s), s % 2)
                    for c in range(2 + (n - 2) // RING * RING, n):
                        silu(base + c, c % 2)

                if l == 0:
                    all_tokens(0, FT)
            act.wait_ge(S("logit_max"), 1)
            for t in range(NT):
                last = a(lgt[:, t, :], lgt[:, t, :], ACT.Exp, bias=nmax[:, t:t + 1])
            last.then_inc(S("logit_exp"), 1)
            act.wait_ge(S("count_ready"), 1)
            most = act.value_load(countI[0:1, 0:1], min_val=0, max_val=T)
            with act.If(most < CAP + 1):
                for t in range(NT):
                    act.wait_ge(S("utok_done"), t + 1)
                    for b in range(2):
                        last = a(utok[:, t, b * 512:(b + 1) * 512], bank[2 * t + b][:, :], ACT.Copy)
                    last.then_inc(S("utok_taken"), 1)
                for e in range(NE):
                    act.wait_ge(S("gt_done"), e + 1)
                    a(gT[0:CAP, e, :], bank[6 + e % 2][0:CAP, 0:T], ACT.Copy).then_inc(S("gt_taken"), 1)
                with act.Fori(0, NE) as e:
                    act.wait_ge(S("gather_done"), e * 2 + 1)
                    a(xg[:, 0:4, :].rearrange("p k s -> p (k s)"), bank[0][:, 0:4 * CAP], ACT.Copy)\
                        .then_inc(S("xg_first"), 1)
                    for c in range(ET):
                        act.wait_ge(S("gate_up_done"), e * ET + (FT + c + 1))
                        act.wait_ge(S("act_ready"), e * ET + (FT + c - 1))
                        a(silg[:, c % 2, :], bank[4 + c % 2][:, 0:CAP], ACT.Silu).then_inc(S("silu_done"), 1)
                    act.wait_ge(S("down_done"), e * ET + (FT + ET))
                    for b in range(2):
                        a(ycol[:, 4 * b:4 * b + 4, :].rearrange("p k s -> p (k s)"), bank[6 + b][:, 0:4 * CAP],
                          ACT.Copy).then_inc(S("ycol_ready"), 1)
            with act.Else():
                all_tokens(FT, NM)
            norm_std(4)

        @block.vector
        def _(dve):
            v = nc.vector
            tt, stt, ts = v.tensor_tensor, v.scalar_tensor_tensor, v.tensor_scalar
            chain = [0]

            def link(ins):
                chain[0] += 1
                ins.then_inc(S("dve_step"), 1)
                dve.wait_ge(S("dve_step"), chain[0])

            def tell(ins, name, val):
                ins.then_inc(S(name), 1)
                dve.wait_ge(S(name), val)

            def square(n):
                v.tensor_tensor(flat(uT), flat(hT), flat(hT), ALU.mult).then_inc(S("sq_ready"), 1)

            def scale_rows(n, g, l):
                dve.wait_ge(S("std_ready"), n + 1)
                link(v.reciprocal(rstd[:, :], std[:, :]))
                for k in range(KB):
                    last = stt(uT[:, k, :], hT[:, k, :], PR(l, g, k), rstd[:, :], ALU.mult, ALU.mult)
                return last

            link(v.memset(epsr[:, 1:2], GN_EPS))
            v.memset(epsr[:, 0:1], RMS_EPS).then_inc(S("eps_set"), 1)
            dve.wait_ge(S("x_loaded"), 16)
            square(0)
            dve.wait_ge(S("pos_loaded"), 16)
            dve.wait_ge(S("par_loaded"), 96)
            link(v.tensor_copy(tmpA[:, 1, :], tmpA[:, 0, :].bitcast(I32)))
            link(ts(tmpA[:, 1, :], tmpA[:, 1, :], C("freq", 1), None, ALU.mult))
            for i, (turn, shift) in enumerate(((0.25, PI / 2), (0.0, 0.0))):
                r = tmpB[:, i, :]
                k = tmpC[:, i, :]
                link(ts(k, tmpA[:, 1, :], 1.0 / (2 * PI), turn, ALU.mult, ALU.add))
                link(ts(k, k, ROUND, -ROUND, ALU.add, ALU.add))
                link(stt(r, k, -C1, tmpA[:, 1, :], ALU.mult, ALU.add))
                link(stt(r, k, -C2, r, ALU.mult, ALU.add))
                link(stt(r, k, -C3, r, ALU.mult, ALU.add))
                link(ts(r, r, shift, None, ALU.add))
                link(ts(k, r, PI, -2 * PI, ALU.is_gt, ALU.mult))
                link(tt(r, r, k, ALU.add))
                link(ts(k, r, -PI, 2 * PI, ALU.is_lt, ALU.mult))
                link(tt(r, r, k, ALU.add))
                ins = ts(r, r, 3.1415925, -3.1415925, ALU.min, ALU.max)
                if i == 0:
                    link(ins)
                else:
                    ins.then_inc(S("angles_ready"), 1)

            for l in range(2):
                link(v.memset(ypad[:, :, 0:1], 0.0))
                scale_rows(2 * l, "mix_g", l).then_inc(S("u_ready"), 1)
                dve.wait_ge(S("proj_taken"), l * NU + 4)
                link(tt(ym[:, 6, :], ypad[:, 6, 0:T], ypad[:, 6, 1:T + 1], ALU.subtract))
                stt(ym[:, 6, :], ym[:, 6, :], PR(l, "mu", 6), ypad[:, 6, 1:T + 1], ALU.mult, ALU.add)\
                    .then_inc(S("wag_mixed"), 1)
                link(tt(ym[:, 0:6, :], ypad[:, 0:6, 0:T], ypad[:, 0:6, 1:T + 1], ALU.subtract))
                for i in range(6):
                    last = stt(ym[:, i, :], ym[:, i, :], PR(l, "mu", i), ypad[:, i, 1:T + 1], ALU.mult, ALU.add)
                tell(last, "v_mixed", l + 1)
                r_, k_, v_ = ym[:, 0:2, :], ym[:, 2:4, :], ym[:, 4:6, :]
                if l == 1:
                    dve.wait_ge(S("v1_done"), 1)
                    v.tensor_copy(tmpA[0:16, 0, :], bank[5][0:16, 0:T]).then_inc(S("v1_taken"), 1)
                    dve.wait_ge(S("v_gate"), 1)
                    link(tt(tmpC[:, :, :], vfirst[:, :, :], v_, ALU.subtract))
                    link(tt(tmpC[:, :, :], tmpC[:, :, :], tmpB[:, :, :], ALU.mult))
                    tell(tt(v_, v_, tmpC[:, :, :], ALU.add), "v_ready", 2)
                else:
                    tell(v.tensor_copy(vfirst[:, :, :], v_), "v_ready", 1)
                for p in range(RP):
                    last = ts(kk[:, p, :], k_[:, p, :], PR(l, "kk", p), None, ALU.mult)
                link(last)
                tt(tmpA[:, :, :], kk[:, :, :], kk[:, :, :], ALU.mult).then_inc(S("kk2_ready"), 1)
                dve.wait_ge(S("sw_ready"), l + 1)
                link(v.tensor_tensor_scan(flat(tmpC), C("reset", 512), flat(sw), 0.0, ALU.mult, ALU.add))
                dve.wait_ge(S("kksum_done"), l + 1)
                ts(flat(tmpB), bank[2][:, :], 1e-24, None, ALU.max).then_inc(S("kk_floor"), 1)
                tt(flat(sw), flat(tmpC), flat(sw), ALU.subtract).then_inc(S("cs_ready"), 1)
                dve.wait_ge(S("lora_done"), 3 * l + 3)
                v.tensor_copy(flat(gg), bank[4][:, :]).then_inc(S("gg_ready"), 1)
                dve.wait_ge(S("kk_norm"), l + 1)
                link(v.reciprocal(flat(tmpB), flat(tmpB)))
                link(tt(flat(kk), flat(kk), flat(tmpB), ALU.mult))
                dve.wait_ge(S("aa_ready"), l + 1)
                for p in range(RP):
                    last = ts(tmpB[:, p, :], aa[:, p, :], -1.0, PR(l, "ka", p), ALU.add, ALU.mult)
                link(last)
                link(stt(flat(tmpB), flat(tmpB), 1.0, ym[:, 2:4, :].rearrange("p a t -> p (a t)"), ALU.add, ALU.mult))
                for p in range(RP):
                    last = stt(bonus[:, p, :], r_[:, p, :], PR(l, "rk", p), tmpB[:, p, :], ALU.mult, ALU.mult)
                last.then_inc(S("rk_ready"), 1)
                dve.wait_ge(S("decay_ready"), l + 1)
                link(tt(flat(aa), flat(aa), flat(kk), ALU.mult))
                stt(flat(At), flat(kk), -1.0, flat(At), ALU.mult, ALU.mult).then_inc(S("a_ready"), 1)
                tt(flat(Bt), flat(aa), flat(Kt), ALU.mult).then_inc(S("b_ready"), 1)
                tt(flat(Kt), flat(tmpB), flat(Kt), ALU.mult).then_inc(S("k_ready"), 1)
                v.tensor_copy(lc[:, :, :], tmpA[:, :, CH - 1::CH])
                tt(r_, r_, tmpA[:, :, :], ALU.mult).then_inc(S("r_ready"), 1)
                dve.wait_ge(S("rksum_done"), l + 1)
                tt(bonus[:, :, :], bank[3][:, :].rearrange("p (a t) -> p a t", a=RP), v_, ALU.mult)\
                    .then_inc(S("bonus_ready"), 1)
                for g in range(2):
                    dve.wait_ge(S("pair_done"), l * 8 + g + 1)
                    b = bank[2 + g][:, :].rearrange("p (m c) -> p m c", m=4)
                    m4 = [P, 4, P]
                    dve.wait_ge(S("tok_taken"), 4 * l + 2)
                    tt(MT[:, g, :, :], b, C("strict").unsqueeze(1).to_broadcast(m4), ALU.mult)\
                        .then_inc(S("pair_taken"), 1)
                    dve.wait_ge(S("pair_taken"), l * 8 + g + 1)
                    tell(tt(T1[:, g, :, :], MT[:, g, :, :], C("lev").unsqueeze(1).to_broadcast(m4), ALU.mult),
                         "y0_ready", 2 * l + g + 1)
                    tt(Y[:, g, :, :], T1[:, g, :, :], ident.unsqueeze(1).to_broadcast(m4), ALU.add)\
                        .then_inc(S("mt_ready"), 1)
                for g in range(2):
                    dve.wait_ge(S("m0_done"), 2 * l + g + 1)
                    b = bank[4 + g][:, :].rearrange("p (m c) -> p m c", m=4)
                    tt(X[:, g, :, :], b, ident.unsqueeze(1).to_broadcast(m4), ALU.add).then_inc(S("x0_ready"), 1)
                for lev in range(1, 6):
                    for g in range(2):
                        i = l * 10 + (lev - 1) * 2 + g
                        if lev < 5:
                            dve.wait_ge(S("xd_done"), l * 8 + (lev - 1) * 2 + g + 1)
                            b = bank[4 + g][:, :].rearrange("p (m c) -> p m c", m=4)
                            tt(X[:, g, :, :], b, X[:, g, :, :], ALU.add).then_inc(S("x_updated"), 1)
                        dve.wait_ge(S("yd_done"), i + 1)
                        b = bank[2 + g][:, :].rearrange("p (m c) -> p m c", m=4)
                        tt(Y[:, g, :, :], b, Y[:, g, :, :], ALU.add).then_inc(S("y_updated"), 1)
                for n, (dst, mask) in ((1, (MT, "strict")), (2, (T1, "incl")), (3, (X, "incl"))):
                    for g in range(2):
                        dve.wait_ge(S("pair_done"), l * 8 + 2 * n + g + 1)
                        if n == 1:
                            dve.wait_ge(S("level_part"), l * 10 + 10)
                        b = bank[2 + g][:, :].rearrange("p (m c) -> p m c", m=4)
                        tt(dst[:, g, :, :], b, C(mask).unsqueeze(1).to_broadcast(m4), ALU.mult)\
                            .then_inc(S("pair_taken"), 1)
                v.memset(st[:, 0:RP, :], 0.0).then_inc(S("state_ready"), 1)
                dve.wait_ge(S("c_taken"), l + 1)
                for n in range(NCH):
                    t, q = n // 2, n % 2
                    rows = slice(q * CH, (q + 1) * CH)
                    dve.wait_ge(S("us_done"), l * NCH + n + 1)
                    tt(uu[rows, t, :], bank[4][rows, 0:T], c0[rows, t, :], ALU.add).then_inc(S("u_chunk"), 1)
                    dve.wait_ge(S("ds_done"), l * NCH + n + 1)
                    dve.wait_ge(S("state_ready"), l * (NCH + 1) + n + 1)
                    for p in range(RP):
                        last = stt(sttmp[:, p, :], bank[4][:, p * P:(p + 1) * P], lc[:, p, n:n + 1], blk, ALU.mult,
                                   ALU.mult)
                    link(last)
                    for p in range(RP):
                        last = stt(st[:, p, :], st[:, p, :], lc[:, p, n:n + 1], sttmp[:, p, :], ALU.mult, ALU.add)
                    last.then_inc(S("state_ready"), 1)
                dve.wait_ge(S("mean_done"), l + 1)
                link(stt(flat(tmpC), bank[2][:, :], -1.0 / HD, flat(tmpC), ALU.mult, ALU.add))
                tt(flat(tmpB), flat(tmpC), flat(tmpC), ALU.mult).then_inc(S("cen_ready"), 1)
                dve.wait_ge(S("gn_std"), l + 1)
                link(v.reciprocal(flat(tmpA), flat(tmpA)))
                link(tt(flat(tmpC), flat(tmpC), flat(tmpA), ALU.mult))
                for p in range(RP):
                    last = ts(tmpC[:, p, :], tmpC[:, p, :], PR(l, "lng", p), PR(l, "lnb", p), ALU.mult, ALU.add)
                link(last)
                link(tt(flat(tmpC), flat(tmpC), flat(bonus), ALU.add))
                tt(mixT[:, 0:RP, :], tmpC[:, :, :], gg[:, :, :], ALU.mult).then_inc(S("rmix_ready"), 1)
                dve.wait_ge(S("rope_ready"), 1)
                for i in range(3):
                    dve.wait_ge(S("rot_done"), 3 * l + i + 1)
                    x = aqk[:, 2 * i:2 * i + 2, :]
                    two = [P, 2, T]
                    tell(tt(tmpA[:, :, :], bank[6][:, :].rearrange("p (a t) -> p a t", a=2),
                            sinT[:, :].unsqueeze(1).to_broadcast(two), ALU.mult), "rot_taken", 3 * l + i + 1)
                    link(tt(x, x, cosT[:, :].unsqueeze(1).to_broadcast(two), ALU.mult))
                    tell(tt(x, x, tmpA[:, :, :], ALU.add), "qk_ready", 3 * l + i + 1)

                def soft_max(h):
                    i = l * 6 + h
                    b = h % 2
                    dve.wait_ge(S("score_done"), i + 1)
                    if h >= 2:
                        dve.wait_ge(S("pt_done"), i - 1)
                    tell(stt(sc[:, b, :], bank[b][:, 0:384], 0.125, C("lnw", 384), ALU.mult, ALU.add), "score_taken",
                         i + 1)
                    for t in range(NT):
                        last = v.tensor_reduce(mxn[:, b, t:t + 1], sc[:, b, t * P:t * P + (t + 1) * P], AX.X, ALU.max,
                                               negate=True)
                    last.then_inc(S("max_ready"), 1)

                def soft_scale(h):
                    i = l * 6 + h
                    b = h % 2
                    dve.wait_ge(S("exp_done"), i + 1)
                    link(v.reciprocal(rden[:, b, :], den[:, b, :]))
                    for t in range(NT):
                        x = sc[:, b, t * P:t * P + (t + 1) * P]
                        last = ts(x, x, rden[:, b, t:t + 1], None, ALU.mult)
                    last.then_inc(S("prob_ready"), 1)

                soft_max(0)
                for h in range(6):
                    if h < 5:
                        soft_max(h + 1)
                    soft_scale(h)
                dve.wait_ge(S("gz_done"), l + 1)
                for p in range(GP):
                    z = bank[p // 2][:, (p % 2) * T:(p % 2 + 1) * T]
                    c = slice(p * T, (p + 1) * T)
                    ts(gU[:, c], z, PR(l, "gb", p), None, ALU.add)
                link(v.memset(st[:, :, :], 0.0))
                link(ts(gE[:, :], gU[:, :], -1.0, None, ALU.mult))
                link(tt(gE[:, :], gE[:, :], gU[:, :], ALU.max))
                ts(gM[:, :], gU[:, :], 0.0, None, ALU.min).then_inc(S("gabs_ready"), 1)
                dve.wait_ge(S("gln_ready"), l + 1)
                link(tt(gS[:, :], gM[:, :], gS[:, :], ALU.subtract))
                v.tensor_tensor_scan(gM[:, :], C("reset", 768), gS[:, :], 0.0, ALU.mult, ALU.add)\
                    .then_inc(S("gcs_ready"), 1)
                link(v.memset(gatt[:, :, :, :], 0.0))
                dve.wait_ge(S("gdecay_ready"), l + 1)
                q3 = gqk[:, 0:3, :].rearrange("p a t -> p (a t)")
                k3 = gqk[:, 3:6, :].rearrange("p a t -> p (a t)")
                stt(q3, q3, 0.125, gE[:, :], ALU.mult, ALU.mult)
                tt(k3, k3, gEi[:, :], ALU.mult).then_inc(S("gk_ready"), 1)
                v.tensor_copy(lgc[:, :, :], gE[:, :].rearrange("p (a t) -> p a t", a=GP)[:, :, CH - 1::CH])\
                    .then_inc(S("gstate_ready"), 1)
                for g in range(2):
                    dve.wait_ge(S("gatt_done"), 2 * l + g + 1)
                    for lo, hi, b in ((0, 4, bank[2 + g]), (4, 6, bank[4 + g])):
                        last = v.copy_predicated(
                            gatt[:, g, lo:hi, :], C("incl").bitcast(I32).unsqueeze(1).to_broadcast([P, hi - lo, P]),
                            b[:, 0:(hi - lo) * P].rearrange("p (m c) -> p m c", m=hi - lo))
                last.then_inc(S("gatt_taken"), 1)
                dve.wait_ge(S("gstate_ready"), l * (NCH + 1) + 1)
                for n in range(NCH):
                    dve.wait_ge(S("gds_done"), l * NCH + n + 1)
                    if n:
                        dve.wait_ge(S("gstate_ready"), l * (NCH + 1) + n + 1)
                    for p in range(GP):
                        last = stt(sttmp[:, p, :], bank[6][:, p * P:(p + 1) * P], lgc[:, p, n:n + 1], blk, ALU.mult,
                                   ALU.mult)
                    link(last)
                    for p in range(GP):
                        last = stt(st[:, p, :], st[:, p, :], lgc[:, p, n:n + 1], sttmp[:, p, :], ALU.mult, ALU.add)
                    last.then_inc(S("gstate_ready"), 1)
                dve.wait_ge(S("go_done"), l + 1)
                v.tensor_copy(gEi[:, 0:512], bank[0][:, :])
                link(v.tensor_copy(gEi[:, 512:768], bank[1][:, 0:T]))
                tt(gS[:, :], gEi[:, :], gEi[:, :], ALU.mult).then_inc(S("go_squared"), 1)
                dve.wait_ge(S("gstd_ready"), l + 1)
                link(v.reciprocal(gE[:, :], gE[:, :]))
                link(tt(gEi[:, :], gEi[:, :], gE[:, :], ALU.mult))
                stt(mixT[:, 5:8, :].rearrange("p a t -> p (a t)"), gEi[:, :], PR(l, "gn"), gU[:, :], ALU.mult,
                    ALU.mult).then_inc(S("gmix_ready"), 1)

                def add_residual(name, val):
                    dve.wait_ge(S(name), val)
                    for b in range(4):
                        x = hT[:, 2 * b:2 * b + 2, :].rearrange("p a t -> p (a t)")
                        last = tt(x, bank[b][:, :], x, ALU.add)
                    link(last)

                add_residual("wout_used", NCO * (l + 1))
                square(2 * l + 1)
                tell(scale_rows(2 * l + 1, "ffn_g", l), "u_ready", 2 * l + 2)

                def times_up(c, par, e=None, guard=True):
                    dve.wait_ge(S("silu_done"), c + 1)
                    if guard:
                        dve.wait_ge(S("down_done"), c - 1)
                    up = bank[4 + par][:, T:2 * T]
                    if l == 0:
                        tt(hac[:, par, :], up, sil[:, par, :], ALU.mult).then_inc(S("act_ready"), 1)
                    else:
                        tt(hraw[:, par, :], up, sil[:, par, :], ALU.mult).then_inc(S("raw_ready"), 1)
                        dve.wait_ge(S("raw_ready"), c - (FT - 1))
                        tt(hac[:, par, :], hraw[:, par, :], combB[:, e, :], ALU.mult).then_inc(S("act_ready"), 1)

                if l == 0:
                    for c in range(2):
                        times_up(c, c, guard=False)
                    with dve.Fori(0, (FT - 2) // RING) as it:
                        for s in range(RING):
                            times_up(it * RING + (2 + s), s % 2)
                    for c in range(2 + (FT - 2) // RING * RING, FT):
                        times_up(c, c % 2)
                    add_residual("down_done", FT)
                    square(2)
            dve.wait_ge(S("logits_done"), 1)
            for t in range(NT):
                lg, first = lgt[:, t, :], sel[:, t, :]
                link(v.tensor_copy(lg, bank[6][:, t * NE:(t + 1) * NE]))
                v.tensor_reduce(nmax[:, t:t + 1], lg, AX.X, ALU.max, negate=True)
                other = lg.unsqueeze(1).to_broadcast([P, NE, NE])
                own = lg.unsqueeze(2).to_broadcast([P, NE, NE])
                gt = rt[:, t, 0, :].rearrange("p (a b) -> p a b", a=NE)
                eq = rt[:, t, 1, :].rearrange("p (a b) -> p a b", a=NE)
                tt(gt, other, own, ALU.is_gt)
                link(tt(eq, other, own, ALU.is_equal))
                link(tt(eq, eq, C("tri8", 64).rearrange("p (a b) -> p a b", a=NE), ALU.mult))
                link(tt(gt, gt, eq, ALU.add))
                link(v.tensor_reduce(first, gt, AX.X, ALU.add))
                link(ts(first, first, 2.0, None, ALU.is_lt))
            v.memset(count[:, :], 0.0).then_inc(S("sel_ready"), 1)
            dve.wait_ge(S("sel_ready"), 1)
            v.memset(st[:, :, 0:1], 0.0).then_inc(S("logit_max"), 1)
            dve.wait_ge(S("queues_done"), 1)
            v.tensor_reduce(count[:, :], bank[7][:, 2 * NE:3 * NE], AX.X, ALU.max)
            link(v.tensor_copy(posn[:, :, :].rearrange("p t e -> p (t e)"), bank[7][:, 0:2 * NE]))
            v.tensor_copy(countI[:, :], count[:, :]).then_inc(S("count_ready"), 1)
            dve.wait_ge(S("logit_exp"), 1)
            for t in range(NT):
                w8 = lgt[:, t, :]
                link(tt(w8, w8, sel[:, t, :], ALU.mult))
                link(v.tensor_reduce(rsum[:, t:t + 1], w8, AX.X, ALU.add))
                link(v.reciprocal(rsum[:, t:t + 1], rsum[:, t:t + 1]))
                last = ts(w8, w8, rsum[:, t:t + 1], None, ALU.mult)
            tell(last, "comb_ready", 1)
            dve.wait_ge(S("count_ready"), 1)
            most = dve.value_load(countI[0:1, 0:1], min_val=0, max_val=T)
            with dve.If(most < CAP + 1):
                for e in range(NE):
                    for t in range(NT):
                        ts(pick[:, t, e, :], C("slot", CAP), posn[:, t, e:e + 1], sel[:, t, e:e + 1], ALU.is_equal,
                           ALU.mult)
                        last = ts(pickw[:, t, e, :], C("slot", CAP), posn[:, t, e:e + 1], lgt[:, t, e:e + 1],
                                  ALU.is_equal, ALU.mult)
                    last.then_inc(S("pick_ready"), 1)
                with dve.Fori(0, NE) as e:
                    dve.wait_ge(S("gather_done"), e * 2 + 2)
                    v.tensor_copy(xg[:, 4:8, :].rearrange("p k s -> p (k s)"), bank[1][:, 0:4 * CAP])\
                        .then_inc(S("xg_second"), 1)
                    for c in range(ET):
                        dve.wait_ge(S("silu_done"), e * ET + (FT + c + 1))
                        dve.wait_ge(S("down_done"), e * ET + (FT + c - 1))
                        tt(hacg[:, c % 2, :], bank[4 + c % 2][:, CAP:2 * CAP], silg[:, c % 2, :], ALU.mult)\
                            .then_inc(S("act_ready"), 1)
                    for b in range(2):
                        dve.wait_ge(S("yrow_done"), e * 2 + (b + 1))
                        v.tensor_copy(yrow[0:CAP, b * 512:(b + 1) * 512], bank[2 + b][0:CAP, :])\
                            .then_inc(S("yrow_ready"), 1)
                    for b in range(4):
                        dve.wait_ge(S("scatter_done"), e * 4 + (b + 1))
                        x = hT[:, 2 * b:2 * b + 2, :].rearrange("p a t -> p (a t)")
                        tt(x, bank[b][:, :], x, ALU.add).then_inc(S("h_added"), 1)
                dve.wait_ge(S("h_added"), 4 * NE)
            with dve.Else():
                dve.wait_ge(S("combT_done"), 1)
                v.tensor_copy(cT[:, :], bank[7][0:NE, 0:T]).then_inc(S("combT_taken"), 1)
                for e in range(NE):
                    dve.wait_ge(S("combB_done"), e + 1)
                    v.tensor_copy(combB[:, e, :], bank[6 + e % 2][:, 0:T]).then_inc(S("combB_taken"), 1)
                dve.wait_ge(S("combB_taken"), NE)
                with dve.Fori(0, NE) as e:
                    with dve.Fori(0, ET // RING) as it:
                        for s in range(RING):
                            times_up(e * ET + it * RING + (FT + s), s % 2, bass.ds(e, 1))
                dve.wait_ge(S("down_done"), FT + NM)
                for b in range(4):
                    x = hT[:, 2 * b:2 * b + 2, :].rearrange("p a t -> p (a t)")
                    last = tt(x, bank[b][:, :], x, ALU.add)
                last.then_inc(S("h_general"), 1)
                dve.wait_ge(S("h_general"), 1)
            square(4)
            scale_rows(4, "fin", 0).then_inc(S("final_ready"), 1)


def kernel(**inputs):
    import numpy as np
    import concourse.bacc as bacc
    from concourse.bass_utils import run_bass_kernel_spmd as run

    a = {k: np.asarray(x) for k, x in inputs.items()}

    def cols(x):
        return np.swapaxes(x.reshape(x.shape[:-1] + (-1, P)), -1, -2)

    def rows(x):
        return x.reshape((-1, P) + x.shape[1:]).transpose(1, 0, 2)

    par = np.concatenate([
        cols(a["mix_norm_g"]), cols(a["ffn_norm_g"]), cols(a["rwkv_mu"]), cols(a["rwkv_w0"]), cols(a["rwkv_a0"]),
        cols(a["rwkv_k_k"]), cols(a["rwkv_k_a"]), cols(a["rwkv_r_k"].reshape(2, -1)), cols(a["rwkv_ln_g"]),
        cols(a["rwkv_ln_b"]), cols(np.concatenate([a["rwkv_v0"], a["rwkv_v0"]])), cols(a["gla_gate_b"]),
        cols(np.concatenate([a["gla_norm_g"], a["gla_norm_g"]], axis=1)),
        cols(np.stack([a["final_norm_g"], a["final_norm_g"]]))], axis=2).transpose(1, 0, 2)
    lora = np.concatenate([a["rwkv_w2"], a["rwkv_a2"], a["rwkv_g2"]], axis=1).transpose(1, 0, 2)
    small = np.stack([np.concatenate([a["rwkv_v2"][0], a["gla_gate_up"][l]], axis=1) for l in range(2)], axis=1)
    start = {"wag": 768, "av": 1664, "gv": 2816, "gd": 3200}
    for n, at in (("r", 0), ("k", 256), ("v", 512), ("aq", 896), ("ak", 1280), ("gq", 2048), ("gk", 2432),
                  ("og", 3216)):
        for i in range(3):
            start[f"{n}{i}"] = at + i * P
    w_in = np.stack([np.concatenate([rows(np.concatenate(
        [a["w_in"][l][:, start[n]:start[n] + WIDTH.get(n, P)] for n in tiles], axis=1)).reshape(P, -1)
        for tiles in CHUNKS], axis=1) for l in range(2)])
    w_out = np.stack([rows(a["w_out"][l]).reshape(P, -1) for l in range(2)])

    def mixer(g, u, d):
        n, _, f = g.shape
        gu = [x.reshape(n, KB, P, f // P, P).transpose(0, 3, 2, 1, 4).reshape(n * f // P, P, D) for x in (g, u)]
        return np.concatenate(gu + [d.reshape(n * f // P, P, D)], axis=2)

    arrays = {
        "in_x": rows(a["x"][0].T), "in_pos": a["positions"].reshape(-1), "in_const": constants(), "in_par": par,
        "in_lora": lora, "in_small": small, "in_v1": rows(a["rwkv_v1"][0]), "in_router": rows(a["moe_router"][0]),
        "in_w_in": w_in, "in_w_out": w_out,
        "in_ffn": mixer(a["ffn_w_gate"], a["ffn_w_up"], a["ffn_w_down"]),
        "in_moe": mixer(a["moe_w_gate"][0], a["moe_w_up"][0], a["moe_w_down"][0]),
    }
    arrays = {k: np.ascontiguousarray(x) for k, x in arrays.items()}
    nc = bacc.Bacc("TRN2", target_bir_lowering=False, num_devices=1)
    args = [nc.dram_tensor(k, x.shape, mybir.dt.from_np(x.dtype), kind="ExternalInput").ap()
            for k, x in arrays.items()]
    out = nc.dram_tensor("out_0", (P, KB, T), F32, kind="ExternalOutput").ap()
    build_trunk(nc, *args, out)
    r = run(nc, [arrays], core_ids=[0])
    o = r.results[0]["out_0"]
    return o.transpose(2, 1, 0).reshape(1, T, D)
```

```python
from contextlib import ExitStack

import concourse.bass as bass
from concourse import mybir

F32 = mybir.dt.float32
F32R = mybir.dt.float32r
I32 = mybir.dt.int32
ALU = mybir.AluOpType
ACT = mybir.ActivationFunctionType
AX = mybir.AxisListType

P = 128
D = 1024
KB = D // P
T = 256
NT = T // P
HD = 64
CH = 64
NCH = T // CH
RP, AP3, GP = 2, 3, 3
AW = GW = 384
FFN, FEXP, NE = 2816, 3584, 8
FT, ET = FFN // P, FEXP // P
NM = NE * ET
DECAY = 0.6065306597126334
RMS_EPS, GN_EPS = 1e-5, 64e-5
PI = 3.14159265358979
LN256 = 5.545177444479562
ROUND = 12582912.0
C1, C2, C3 = 6.28125, 1.9350051879882812e-03, 3.0198680390e-07

CAP = 96
RING = 4
MRING = 7
SLOT = 3072

CHUNKS = (("r0", "r1", "k0"), ("k1", "v0", "v1"), ("wag", "aq0", "aq1"), ("aq2", "ak0", "ak1"), ("ak2", "gd"),
          ("av",), ("gq0", "gq1", "gq2"), ("gk0", "gk1", "gk2"), ("gv",), ("og0", "og1", "og2"))
WIDTH = {"gd": 16, "av": AW, "gv": GW}
UNITS = (("r0", "r1"), ("k0", "k1"), ("v0", "v1"), ("wag",), ("aq0", "aq1"), ("aq2", "ak0"), ("ak1", "ak2"), ("gd",),
         ("av", 0), ("av", 1), ("gq0", "gq1"), ("gq2", "gk0"), ("gk1", "gk2"), ("gv", 0), ("gv", 1), ("og0", "og1"),
         ("og2",))
NU = len(UNITS)
CHUNK_OF, COL_OF, CHUNK_W = {}, {}, []
for _c, _tiles in enumerate(CHUNKS):
    _at = 0
    for _n in _tiles:
        CHUNK_OF[_n], COL_OF[_n] = _c, _at
        _at += WIDTH.get(_n, P)
    CHUNK_W.append(_at)
LAST_UNIT = [max(u for u, unit in enumerate(UNITS) if any(n in CHUNKS[c] for n in unit)) for c in range(len(CHUNKS))]
OUT_ORDER = (2, 3, 4, 5, 6, 7, 0, 1)
OUT_K = (3, 3, 2)
OUT_BANKS = (0, 1, 6, 7)
NCI, NCO = len(CHUNKS), len(OUT_K)
LAYER_LOADS = (NCI + NCO + FT, NCI + NCO)
LAYER0 = (0, LAYER_LOADS[0])
MOE0 = sum(LAYER_LOADS)
assert MOE0 % RING == 0 and ET % (2 * MRING) == 0 and ET % RING == 0

PCOL, _at = {}, 0
for _n, _w in (("mix_g", 8), ("ffn_g", 8), ("mu", 7), ("w0", 2), ("a0", 2), ("kk", 2), ("ka", 2), ("rk", 2),
               ("lng", 2), ("lnb", 2), ("v0", 2), ("gb", 3), ("gn", 1), ("fin", 8)):
    PCOL[_n] = _at
    _at += _w
NPAR = _at
CCOL, _at = {}, 0
for _n, _w in (("ident", 128), ("ones", 128), ("strict", 128), ("incl", 128), ("lev", 6 * 128), ("rot", 128),
               ("blk", 128), ("lnw", 384), ("reset", 768), ("freq", 1), ("tri8", 64), ("before", 128),
               ("slot", CAP)):
    CCOL[_n] = _at
    _at += _w
NCON = _at


def constants():
    import numpy as np
    c = np.zeros((P, NCON), np.float32)

    def put(name, a):
        c[:a.shape[0], CCOL[name]:CCOL[name] + a.shape[1]] = a

    j, i = np.arange(P)[:, None], np.arange(P)[None, :]
    same = j // CH == i // CH
    put("ident", j == i)
    put("ones", np.ones((P, P)))
    put("strict", (j < i) & same)
    put("incl", (j <= i) & same)
    put("lev", np.concatenate([(j >> (n + 1) == i >> (n + 1)) & ((j >> n) % 2 == 0) & ((i >> n) % 2 == 1)
                               for n in range(6)], axis=1))
    dj, di = j % HD, i % HD
    head = j // HD == i // HD
    put("rot", head * (1.0 * ((di >= 8) & (di < 16) & (dj == di - 8)) - 1.0 * ((di < 8) & (dj == di + 8))))
    put("blk", head)
    w = np.zeros((T, T))
    qi, kj = np.arange(T)[:, None], np.arange(T)[None, :]
    for window, dil in ((128, 1), (512, 4), (2048, 16)):
        w += (qi >= kj) & (qi % dil == kj % dil) & (qi // dil - kj // dil <= window // dil)
    lw = np.where(w > 0, np.log(np.maximum(w, 1)), -1e30)
    put("lnw", np.concatenate([lw[:P, :P], lw[P:, :]], axis=1))
    put("reset", np.broadcast_to((np.arange(768) % CH != 0)[None, :], (P, 768)))
    half = 8
    inv = np.float32(500000.0) ** (-np.arange(half, dtype=np.float32) / np.float32(half))
    f = np.zeros((P, 1), np.float32)
    for p in range(P):
        if p % HD < 16:
            f[p] = inv[p % 8]
    put("freq", f)
    e = np.arange(8)
    put("before", j < i)
    put("slot", np.broadcast_to(np.arange(CAP)[None, :], (P, CAP)))
    put("tri8", np.broadcast_to((e[None, :] < e[:, None]).reshape(1, 64), (P, 64)))
    return c


def build_trunk(nc, xT, pos, con, par, lora, small, v1, router, w_in, w_out, w_ffn, w_moe, out):
    with ExitStack() as ctx:
        address = {}

        def sb(name, shape, dt=F32):
            address[name] = (nc.sbuf_base + 31) // 32 * 32
            return ctx.enter_context(nc.sbuf_tensor(name, shape, dt))

        sems = {}

        def S(name):
            if name not in sems:
                sems[name] = ctx.enter_context(nc.semaphore(name))
            return sems[name]

        def rounded(name, x, shape):
            return nc.alloc_sbuf_tensor_at(name, shape, F32R, offset=address[x])

        ring = sb("ring", [P, RING, SLOT])
        hT = sb("hT", [P, KB, T])
        uT = sb("uT", [P, KB, T])
        mixT = sb("mixT", [P, KB, T])
        lent = sb("lent", [P, (MRING - RING) * SLOT])
        mats = sb("mats", [P, 5, 1024])
        vfirst = sb("vfirst", [P, RP, T])
        cst = sb("cst", [P, NCON])
        prm = sb("prm", [P, 2, NPAR])
        lor = sb("lor", [P, 2, 256])
        sml = sb("sml", [16, 2, 640])
        v1s = sb("v1s", [P, RP, 16])
        rts = sb("rts", [P, KB, NE])
        cosT = sb("cosT", [P, T])
        sinT = sb("sinT", [P, T])
        std = sb("std", [P, T])
        rstd = sb("rstd", [P, T])
        epsr = sb("epsr", [P, 3])
        sttmp = sb("sttmp", [P, RP, P])

        ypad = sb("ypad", [P, 7, T + 1])
        lent_at = [0]

        def part(n, *dims):
            at = lent_at[0]
            lent_at[0] += n
            x = lent[:, at:at + n]
            names = "abc"[:len(dims) + 1]
            if not dims:
                return x
            spec = " ".join(names)
            return x.rearrange(f"p ({spec}) -> p {spec}", **dict(zip(names, dims)))

        ym = part(7 * T, 7)
        aqk = sb("aqk", [P, 6, T])
        av = sb("av", [P, NT, AW])
        gqk = sb("gqk", [P, 6, T])
        gv = sb("gv", [P, NT, GW])
        gd = sb("gd", [16, T])
        og = sb("og", [P, 3, T])

        tw = part(T)
        sw, aa, gg, At, kk, Kt, Bt, bonus, wt = (part(RP * T, RP) for _ in range(9))
        tokm = part(4 * NT * 256, 4, NT)
        lc = sb("lc", [P, RP, NCH])
        tmpA = sb("tmpA", [P, RP, T])
        tmpB = sb("tmpB", [P, RP, T])
        tmpC = sb("tmpC", [P, RP, T])
        MT, X, ML, Y, T1 = (mats[:, i, :].rearrange("p (a b c) -> p a b c", a=2, b=4) for i in range(5))
        st = sb("st", [P, RP, P])

        bank = [ctx.enter_context(nc.psum_tensor(f"bank{i}", [P, 512], F32)) for i in range(8)]

        L_, Li, cs = tmpA, tmpB, tmpC
        nv, c0, uu = tmpA, tmpB, kk
        yp = ypad[:, :, :].rearrange("p a b -> p (a b)")
        qkf = aqk[:, :, :].rearrange("p a b -> p (a b)")
        combB = sb("combB", [P, NE, T])
        cbf = combB[:, :, :].rearrange("p a b -> p (a b)")
        sc = yp[:, 0:768].rearrange("p (b c) -> p b c", b=2)
        pt = yp[:, 768:1536].rearrange("p (b c) -> p b c", b=2)
        rtmp = yp[:, 0:512].rearrange("p (b c) -> p b c", b=2)
        gE, gEi, gU, gS = cbf[:, 0:768], cbf[:, 768:1536], yp[:, 0:768], yp[:, 768:1536]
        gatt = qkf.rearrange("p (g m c) -> p g m c", g=2, m=6)
        ktok = av
        gst = sb("gst", [P, GP, P])
        gtmp = sb("gtmp", [P, GP, P])
        lgc = sb("lgc", [P, GP, NCH])
        negb = sb("negb", [P, GP])
        mxn = sb("mxn", [P, 2, NT])
        den = sb("den", [P, 2, NT])
        rden = sb("rden", [P, 2, NT])
        sil = mats[:, 0, 0:512].rearrange("p (b t) -> p b t", b=2)
        hac = mats[:, 2, 0:512].rearrange("p (b t) -> p b t", b=2)
        hraw = mats[:, 4, 0:512].rearrange("p (b t) -> p b t", b=2)
        rt = sb("rt", [P, NT, 2, 64])
        lgt = sb("lgt", [P, NT, NE])
        sel = sb("sel", [P, NT, NE])
        posn = sb("posn", [P, NT, NE])
        nmax = sb("nmax", [P, NT])
        rsum = sb("rsum", [P, NT])
        count = sb("count", [P, 1])
        countI = sb("countI", [P, 1], I32)
        cT = cosT[0:NE, :]
        gT = combB
        ycol = aqk[:, :, :].rearrange("p a b -> p (a b)")[:, 768:768 + KB * CAP].rearrange("p (k s) -> p k s", k=KB)
        yrow = mats[:, 4, :]
        utok = mixT[:, :, :].rearrange("p k t -> p (k t)").rearrange("p (t d) -> p t d", t=NT)
        w_high = rounded("w_high", "mats", [P, 2, 2, D])
        ring_low = rounded("ring_low", "ring", [P, RING, SLOT])
        lent_low = rounded("lent_low", "lent", [P, MRING - RING, SLOT])
        x_high = rounded("x_high", "uT", [P, 2, KB * CAP])
        pick = gqk[:, :, :].rearrange("p a b -> p (a b)").rearrange("p (t e s) -> p t e s", t=NT, e=NE)
        pickw = ypad[:, :, :].rearrange("p a b -> p (a b)")[:, 0:NT * NE * CAP]\
            .rearrange("p (t e s) -> p t e s", t=NT, e=NE)
        silg = vfirst[:, 0, :].rearrange("p (b f) -> p b f", b=2)
        hrow = vfirst[:, 1, :].rearrange("p (b f) -> p b f", b=2)
        hcol = sinT[:, 0:2 * CAP].rearrange("p (b s) -> p b s", b=2)

        def C(name, n=P, at=0):
            return cst[:, CCOL[name] + at:CCOL[name] + at + n]

        def PR(l, name, i=0):
            a = PCOL[name] + i
            return prm[:, l, a:a + 1]

        ident, ones, blk = C("ident"), C("ones"), C("blk")

        def flat(a):
            return a[:, :, :].rearrange("p a b -> p (a b)")

        def loaded(eng, j):
            eng.wait_ge(S(f"slot{j % RING}_loaded"), 16 * (j // RING + 1))

        def wslot(j, w):
            return ring[:, j % RING, 0:KB * w].rearrange("p (k c) -> p k c", k=KB)

        def slot(s):
            return ring[:, s, :] if s < RING else lent[:, (s - RING) * SLOT:(s - RING + 1) * SLOT]

        def gu_slot(s):
            return slot(s)[:, 0:2 * D].rearrange("p (k m c) -> p m k c", m=2, k=KB)

        def half(x, q):
            return x[:, q * D:(q + 1) * D]

        def low_slot(s):
            return ring_low[:, s, :] if s < RING else lent_low[:, s - RING, :]

        def dn_slot(s):
            return slot(s)[:, 2 * D:3 * D].rearrange("p (k c) -> p k c", k=KB)

        pb, bs = bank[0:2], bank
        hm = [(t, p) for t in range(NT) for p in range(RP)]
        block = ctx.enter_context(nc.Block())

        @block.sync
        def _(sp):
            sp.dma_start(hT[:, :, :], xT).then_inc(S("x_loaded"), 16)
            sp.dma_start(cst[:, :], con).then_inc(S("par_loaded"), 16)
            sp.dma_start(prm[:, :, :], par).then_inc(S("par_loaded"), 16)
            sp.dma_start(lor[:, :, :], lora).then_inc(S("par_loaded"), 16)
            sp.dma_start(sml[:, :, :], small).then_inc(S("par_loaded"), 16)
            sp.dma_start(v1s[:, :, :], v1).then_inc(S("par_loaded"), 16)
            sp.dma_start(rts[:, :, :], router).then_inc(S("par_loaded"), 16)

            def used(j):
                l = 0 if j < LAYER0[1] else 1
                i = j - LAYER0[l]
                if i < NCI:
                    sp.wait_ge(S("proj_done"), l * NU + LAST_UNIT[i] + 1)
                elif i < NCI + NCO:
                    sp.wait_ge(S("wout_used"), l * NCO + i - NCI + 1)
                else:
                    sp.wait_ge(S("down_done"), i - NCI - NCO + 1)

            def load(j, src, n):
                if j >= RING:
                    used(j - RING)
                sp.dma_start(ring[:, j % RING, 0:n], src).then_inc(S(f"slot{j % RING}_loaded"), 16)

            for l in range(2):
                at = 0
                for c in range(NCI):
                    load(LAYER0[l] + c, w_in[l, :, at:at + KB * CHUNK_W[c]], KB * CHUNK_W[c])
                    at += KB * CHUNK_W[c]
                at = 0
                for c in range(NCO):
                    load(LAYER0[l] + NCI + c, w_out[l, :, at:at + OUT_K[c] * D], OUT_K[c] * D)
                    at += OUT_K[c] * D
                if l == 0:
                    first = NCI + NCO
                    for c in range(RING):
                        load(first + c, w_ffn[c], SLOT)
                    with sp.Fori(0, FT // RING - 1) as it:
                        for s in range(RING):
                            sl = (first + s) % RING
                            sp.wait_ge(S("down_done"), it * RING + (s + 1))
                            sp.dma_start(ring[:, sl, :],
                                         w_ffn[bass.ds(it * RING + (RING + s), 1)].rearrange("a p n -> p (a n)"))\
                              .then_inc(S(f"slot{sl}_loaded"), 16)
                    for c in range(FT // RING * RING, FT):
                        load(first + c, w_ffn[c], SLOT)
            for c in range(MRING):
                if c < RING:
                    used(MOE0 - RING + c)
                elif c == RING:
                    sp.wait_ge(S("rmix_ready"), 2)
                    sp.wait_ge(S("gmix_ready"), 2)
                sp.dma_start(slot(c), w_moe[c]).then_inc(S(f"moe{c}_loaded"), 16)
            with sp.Fori(0, NM // MRING - 1) as it:
                for s in range(MRING):
                    sp.wait_ge(S("down_done"), it * MRING + (FT + s + 1))
                    sp.dma_start(slot(s), w_moe[bass.ds(it * MRING + (MRING + s), 1)].rearrange("a p n -> p (a n)"))\
                      .then_inc(S(f"moe{s}_loaded"), 16)
            sp.wait_ge(S("final_ready"), 1)
            sp.dma_start(out, uT[:, :, :]).then_inc(S("stored"), 16)
            sp.wait_ge(S("stored"), 16)

        @block.gpsimd
        def _(pool):
            pool.dma_start(tmpA[:, 0, :].bitcast(I32), pos.partition_broadcast(P)).then_inc(S("pos_loaded"), 16)
            pool.wait_ge(S("par_loaded"), 96)
            for l in range(2):
                for lev in range(1, 6):
                    for g in range(2):
                        if lev == 1:
                            pool.wait_ge(S("mt_ready"), 2 * l + g + 1)
                        else:
                            pool.wait_ge(S("t1_done"), l * 10 + (lev - 2) * 2 + g + 1)
                        for m in range(4):
                            last = nc.gpsimd.tensor_tensor(ML[:, g, m, :], MT[:, g, m, :], C("lev", P, lev * P),
                                                           ALU.mult)
                        last.then_inc(S("level_part"), 1)

        @block.tensor
        def _(pe):
            mm = nc.tensor.matmul

            def norm(n):
                pe.wait_ge(S("sq_ready"), n + 1)
                for k in range(KB):
                    last = mm(bank[7][:, 0:T], ones, uT[:, k, :], start=(k == 0), stop=(k == KB - 1))
                last.then_inc(S("norm_summed"), 1)

            def project(l, u):
                unit = UNITS[u]
                i = l * NU + u
                b = pb[u % 2]
                if u >= 2:
                    pe.wait_ge(S("proj_taken"), i - 1)
                if u == 0:
                    pe.wait_ge(S("u_ready"), 2 * l + 1)
                if unit[0] in ("av", "gv"):
                    c = CHUNK_OF[unit[0]]
                    loaded(pe, LAYER0[l] + c)
                    w = wslot(LAYER0[l] + c, AW)
                    t = unit[1]
                    for k in range(KB):
                        last = mm(b[:, 0:AW], uT[:, k, t * P:(t + 1) * P], w[:, k, :], start=(k == 0),
                                  stop=(k == KB - 1))
                else:
                    for i2, name in enumerate(unit):
                        c = CHUNK_OF[name]
                        loaded(pe, LAYER0[l] + c)
                        w = wslot(LAYER0[l] + c, CHUNK_W[c])
                        m = WIDTH.get(name, P)
                        for k in range(KB):
                            last = mm(b[0:m, i2 * T:(i2 + 1) * T], w[:, k, COL_OF[name]:COL_OF[name] + m], uT[:, k, :],
                                      start=(k == 0), stop=(k == KB - 1))
                last.then_inc(S("proj_done"), 1)

            def lora_up(l):
                pe.wait_ge(S("tw_ready"), l + 1)
                for b, (lo, hi) in ((2, (0, 32)), (3, (32, 64)), (4, (64, 128))):
                    for p in range(RP):
                        last = mm(bank[b][:, p * T:(p + 1) * T], lor[lo:hi, l, p * P:(p + 1) * P], tw[lo:hi, :],
                                  start=True, stop=True)
                    last.then_inc(S("lora_done"), 1)

            def value_residual():
                pe.wait_ge(S("v_mixed"), 2)
                for p in range(RP):
                    last = mm(bank[5][0:16, 0:T], v1s[:, p, :], ym[:, 4 + p, :], start=(p == 0), stop=(p == RP - 1))
                last.then_inc(S("v1_done"), 1)
                pe.wait_ge(S("v1_taken"), 1)
                for p in range(RP):
                    last = mm(bank[5][:, p * T:(p + 1) * T], sml[:, 1, p * P:(p + 1) * P], tmpA[0:16, 0, :],
                              start=True, stop=True)
                last.then_inc(S("v2_done"), 1)

            def head_sum(sig, val, done, b, src, n=512):
                pe.wait_ge(S(sig), val)
                mm(bank[b][:, 0:n], blk, src, start=True, stop=True).then_inc(S(done), 1)

            def rwkv_products(l):
                pe.wait_ge(S("score_taken"), 6 * l + 6)
                for q, (name, src) in enumerate((("a_ready", At), ("b_ready", Bt), ("k_ready", Kt), ("v_ready", ym))):
                    pe.wait_ge(S(name), l + 1)
                    if q == 0:
                        pe.wait_ge(S("sw_ready"), l + 1)
                        pe.wait_ge(S("bonus_ready"), l + 1)
                    if q == 2:
                        pe.wait_ge(S("gg_ready"), l + 1)
                    if q == 3 and l == 1:
                        pe.wait_ge(S("v_gate"), 1)
                    for t in range(NT):
                        for p in range(RP):
                            x = src[:, p, t * P:(t + 1) * P] if q < 3 else ym[:, 4 + p, t * P:(t + 1) * P]
                            last = nc.tensor.transpose(bank[2 + q][:, t * T + p * P:t * T + (p + 1) * P], x, ident)
                    last.then_inc(S("tok_done"), 1)

            def pairwise(l, n, sig, lhs, rhs):
                for g in range(2):
                    if n:
                        pe.wait_ge(S("pair_taken"), l * 8 + 2 * n + g - 1)
                    for m, (t, p) in enumerate(hm):
                        a = lhs[g * HD:(g + 1) * HD, p, t * P:(t + 1) * P]
                        b = rhs[g * HD:(g + 1) * HD, p, t * P:(t + 1) * P]
                        last = mm(bank[2 + g][:, m * P:(m + 1) * P], a, b, start=True, stop=True)
                    last.then_inc(S("pair_done"), 1)

            def level0(l):
                for g in range(2):
                    pe.wait_ge(S("y0_ready"), 2 * l + g + 1)
                    pe.wait_ge(S("tok_taken"), 4 * l + 4)
                    for m in range(4):
                        last = nc.tensor.transpose(bank[4 + g][:, m * P:(m + 1) * P], T1[:, g, m, :], ident)
                    last.then_inc(S("m0_done"), 1)

            def invert_product(l, lev):
                for g in range(2):
                    i = l * 10 + (lev - 1) * 2 + g
                    pe.wait_ge(S("level_part"), i + 1)
                    if lev == 1:
                        pe.wait_ge(S("x0_ready"), 2 * l + g + 1)
                    else:
                        pe.wait_ge(S("x_updated"), l * 8 + (lev - 2) * 2 + g + 1)
                        pe.wait_ge(S("y_updated"), i - 1)
                    for m in range(4):
                        last = mm(bank[2 + g][:, m * P:(m + 1) * P], ML[:, g, m, :], X[:, g, m, :], start=True,
                                  stop=True)
                    last.then_inc(S("t1_done"), 1)

            def invert_update(l, lev):
                for g in range(2):
                    i = l * 10 + (lev - 1) * 2 + g
                    pe.wait_ge(S("t1_taken"), i + 1)
                    if lev < 5:
                        for m in range(4):
                            last = mm(bank[4 + g][:, m * P:(m + 1) * P], Y[:, g, m, :], T1[:, g, m, :], start=True,
                                      stop=True)
                        last.then_inc(S("xd_done"), 1)
                    for m in range(4):
                        last = mm(bank[2 + g][:, m * P:(m + 1) * P], T1[:, g, m, :], Y[:, g, m, :], start=True,
                                  stop=True)
                    last.then_inc(S("yd_done"), 1)

            def rwkv_solve_nv(l):
                pe.wait_ge(S("pair_taken"), l * 8 + 4)
                for g in range(2):
                    for m, (t, p) in enumerate(hm):
                        c = p * P + g * HD
                        last = mm(bank[4][:, t * T + c:t * T + c + HD], MT[:, g, m, :], tokm[:, 3, t, c:c + HD],
                                  start=True, stop=True)
                last.then_inc(S("nv_done"), 1)
                for g in range(2):
                    for m, (t, p) in enumerate(hm):
                        c = p * P + g * HD
                        last = mm(bank[5][g * HD:(g + 1) * HD, p * T + t * P:p * T + (t + 1) * P],
                                  tokm[:, 0, t, c:c + HD], Y[:, g, m, :], start=True, stop=True)
                last.then_inc(S("wt_done"), 1)

            def rwkv_solve_c(l):
                pe.wait_ge(S("nv_taken"), l + 1)
                for g in range(2):
                    for m, (t, p) in enumerate(hm):
                        c = p * P + g * HD
                        last = mm(bank[4][:, t * T + c:t * T + c + HD], Y[:, g, m, :], nv[:, t, c:c + HD],
                                  start=True, stop=True)
                last.then_inc(S("c_done"), 1)

            def rwkv_scan(l):
                ob = bank[5]
                pe.wait_ge(S("wt_taken"), l + 1)
                pe.wait_ge(S("c_taken"), l + 1)
                for n in range(NCH):
                    t, q = n // 2, n % 2
                    rows = slice(q * CH, (q + 1) * CH)
                    tk = slice(n * CH, (n + 1) * CH)
                    pe.wait_ge(S("state_ready"), l * (NCH + 1) + n + 1)
                    for p in range(RP):
                        last = mm(bank[4][rows, p * P:(p + 1) * P], wt[:, p, tk], st[:, p, :], start=True, stop=True)
                    last.then_inc(S("us_done"), 1)
                    for p in range(RP):
                        mm(ob[:, p * T + n * CH:p * T + (n + 1) * CH], st[:, p, :], ym[:, p, tk],
                           start=(n == 0 and p == 0), stop=False, skip_group_check=True)
                    pe.wait_ge(S("u_chunk"), l * NCH + n + 1)
                    for p in range(RP):
                        cc = slice(p * P, (p + 1) * P)
                        mm(bank[4][:, cc], tokm[rows, 1, t, cc], uu[rows, t, cc], start=True, stop=False)
                        last = mm(bank[4][:, cc], tokm[rows, 2, t, cc], tokm[rows, 3, t, cc], start=False, stop=True)
                    last.then_inc(S("ds_done"), 1)
                    out_block(l, n)
                pe.wait_ge(S("pair_taken"), l * 8 + 8)
                for g in range(2):
                    for m, (t, p) in enumerate(hm):
                        c = p * P + g * HD
                        o = ob[g * HD:(g + 1) * HD, p * T + t * P:p * T + (t + 1) * P]
                        mm(o, uu[:, t, c:c + HD], T1[:, g, m, :], start=False, stop=False, skip_group_check=True)
                        last = mm(o, tokm[:, 3, t, c:c + HD], X[:, g, m, :], start=False, stop=True,
                                  skip_group_check=True)
                last.then_inc(S("ro_done"), 1)

            def group_norm(l):
                head_sum("ro_taken", l + 1, "mean_done", 2, flat(tmpC))
                out_block(l, 4)
                head_sum("cen_ready", l + 1, "var_done", 3, flat(tmpB))
                out_block(l, 5)

            def rotary(l, i):
                pe.wait_ge(S("proj_taken"), l * NU + 5 + i)
                if i > 0:
                    pe.wait_ge(S("rot_taken"), l * 3 + i)
                for s in range(2):
                    last = mm(bank[6][:, s * T:(s + 1) * T], C("rot"), aqk[:, 2 * i + s, :], start=True, stop=True)
                last.then_inc(S("rot_done"), 1)

            def scores(l, h):
                p, g = h // 2, h % 2
                i = l * 6 + h
                r = slice(g * HD, (g + 1) * HD)
                pe.wait_ge(S("qk_ready"), 3 * l + 3)
                if h < 2:
                    pe.wait_ge(S("gg_ready"), l + 1)
                    if l == 1:
                        pe.wait_ge(S("v_gate"), 1)
                else:
                    pe.wait_ge(S("score_taken"), i - 1)
                for t in range(NT):
                    n = (t + 1) * P
                    last = mm(bank[4 + g][:, t * P:t * P + n], aqk[r, p, t * P:(t + 1) * P], aqk[r, 3 + p, 0:n],
                              start=True, stop=True)
                last.then_inc(S("score_done"), 1)

            def attend(l, h):
                p, g = h // 2, h % 2
                i = l * 6 + h
                pe.wait_ge(S("prob_ready"), i + 1)
                if h >= 1:
                    pe.wait_ge(S("pt_taken"), i)
                for b in range(3):
                    last = nc.tensor.transpose(bank[6][:, b * P:(b + 1) * P], sc[:, h % 2, b * P:(b + 1) * P], ident)
                last.then_inc(S("pt_done"), 1)
                pe.wait_ge(S("pt_taken"), i + 1)
                if g == 0 and h > 0:
                    pe.wait_ge(S("ao_taken"), l * 3 + p)
                r = slice(g * HD, (g + 1) * HD)
                v = slice(h * HD, (h + 1) * HD)
                mm(bank[7][r, 0:P], av[:, 0, v], pt[:, h % 2, 0:P], start=True, stop=True)
                mm(bank[7][r, P:T], av[:, 0, v], pt[:, h % 2, P:2 * P], start=True, stop=False)
                mm(bank[7][r, P:T], av[:, 1, v], pt[:, h % 2, 2 * P:3 * P], start=False, stop=True)\
                    .then_inc(S("ao_done"), 1)

            def gla_gates(l):
                pe.wait_ge(S("proj_taken"), l * NU + NU)
                for p in range(GP):
                    b = bank[p // 2]
                    last = mm(b[:, (p % 2) * T:(p % 2 + 1) * T], sml[:, l, 256 + p * P:256 + (p + 1) * P], gd[:, :],
                              start=True, stop=True)
                last.then_inc(S("gz_done"), 1)

            def gla_token_major(l):
                pe.wait_ge(S("gk_ready"), l + 1)
                pe.wait_ge(S("pt_taken"), 6 * l + 6)
                pe.wait_ge(S("ao_taken"), 3 * l + 3)
                for t in range(NT):
                    for p in range(GP):
                        last = nc.tensor.transpose(bank[6 + t][:, p * P:(p + 1) * P], gqk[:, 3 + p, t * P:(t + 1) * P],
                                                   ident)
                last.then_inc(S("ktok_done"), 1)

            def gla_pairwise(l, part_):
                if part_ == 0:
                    pe.wait_ge(S("ktok_taken"), l + 1)
                else:
                    pe.wait_ge(S("gatt_taken"), 2 * l + 1)
                for g in range(2):
                    r = slice(g * HD, (g + 1) * HD)
                    for m in (range(4), range(4, 6))[part_]:
                        t, p = m // 3, m % 3
                        last = mm(bank[6 + g][:, (m % 4) * P:(m % 4 + 1) * P], gqk[r, 3 + p, t * P:(t + 1) * P],
                                  gqk[r, p, t * P:(t + 1) * P], start=True, stop=True)
                last.then_inc(S("gatt_done"), 1)

            def gla_scan(l, n):
                t, q = n // 2, n % 2
                rows = slice(q * CH, (q + 1) * CH)
                if n == 0:
                    pe.wait_ge(S("gatt_taken"), 2 * l + 2)
                pe.wait_ge(S("gstate_ready"), l * (NCH + 1) + n + 1)
                for p in range(GP):
                    mm(bank[p // 2][:, (p % 2) * T + n * CH:(p % 2) * T + (n + 1) * CH], gst[:, p, :],
                       gqk[:, p, n * CH:(n + 1) * CH], start=(n == 0 and p != 1), stop=False,
                       skip_group_check=True)
                for p in range(GP):
                    cc = slice(p * P, (p + 1) * P)
                    last = mm(bank[6][:, cc], ktok[rows, t, cc], gv[rows, t, cc], start=True, stop=True)
                last.then_inc(S("gds_done"), 1)

            def gla_inside(l):
                for g in range(2):
                    for m in range(6):
                        t, p = m // 3, m % 3
                        c = p * P + g * HD
                        last = mm(bank[p // 2][g * HD:(g + 1) * HD, (p % 2) * T + t * P:(p % 2) * T + (t + 1) * P],
                                  gv[:, t, c:c + HD], gatt[:, g, m, :], start=False, stop=True, skip_group_check=True)
                last.then_inc(S("go_done"), 1)

            def gla_norm(l):
                pe.wait_ge(S("go_squared"), l + 1)
                pe.wait_ge(S("gstate_ready"), (l + 1) * (NCH + 1))
                mm(bank[6][:, :], blk, gU[:, 0:512], start=True, stop=True)
                mm(bank[7][:, 0:T], blk, gU[:, 512:768], start=True, stop=True).then_inc(S("gvar_done"), 1)

            def out_block(l, i):
                c, first = min(i // 3, 2), i % 3 == 0
                j = LAYER0[l] + NCI + c
                if first:
                    loaded(pe, j)
                    if c == 0:
                        pe.wait_ge(S("ao_taken"), 3 * l + 3)
                        pe.wait_ge(S("gstd_ready"), l + 1)
                    elif c == 1:
                        pe.wait_ge(S("gmix_ready"), l + 1)
                    else:
                        pe.wait_ge(S("rmix_ready"), l + 1)
                w = ring[:, j % RING, 0:OUT_K[c] * D].rearrange("p (k c) -> p k c", k=OUT_K[c])
                for m in range(KB):
                    last = mm(bank[OUT_BANKS[m // 2]][:, (m % 2) * T:(m % 2 + 1) * T], w[:, i - 3 * c,
                              m * P:(m + 1) * P], mixT[:, OUT_ORDER[i], :], start=(i == 0 and m % 2 == 0),
                              stop=(i == KB - 1), skip_group_check=True)
                if i in (2, 5, 7):
                    last.then_inc(S("wout_used"), 1)

            def gate_up(slot, par):
                w = gu_slot(slot)
                for m in range(2):
                    for k in range(KB):
                        last = mm(bank[4 + par][:, m * T:(m + 1) * T], w[:, m, k, :], uT[:, k, :], start=(k == 0),
                                  stop=(k == KB - 1))
                last.then_inc(S("gate_up_done"), 1)

            def down(slot, par, first):
                w = dn_slot(slot)
                for m in range(KB):
                    last = mm(bank[m // 2][:, (m % 2) * T:(m % 2 + 1) * T], w[:, m, :], hac[:, par, :],
                              start=(first and m % 2 == 0), stop=False, skip_group_check=True)
                last.then_inc(S("down_done"), 1)

            def channel_mixer(n_chunks, size, name, load0, base):
                first = load0 % size
                unroll = size * (1 + size % 2)
                rounds = (n_chunks - 2) // unroll

                def turn(c):
                    return 16 * ((load0 + c) // size + 1)

                pe.wait_ge(S(f"{name}{first}_loaded"), turn(0))
                if base:
                    pe.wait_ge(S("act_ready"), base)
                gate_up(first, 0)
                pe.wait_ge(S(f"{name}{(first + 1) % size}_loaded"), turn(1))
                gate_up((first + 1) % size, 1)
                pe.wait_ge(S("act_ready"), base + 1)
                down(first, 0, True)

                def pair(c, s, loads):
                    new, old = (first + 2 + s) % size, (first + 1 + s) % size
                    pe.wait_ge(S(f"{name}{new}_loaded"), loads)
                    pe.wait_ge(S("act_ready"), c + (base - 1))
                    gate_up(new, s % 2)
                    pe.wait_ge(S("act_ready"), c + base)
                    down(old, (s + 1) % 2, False)

                with pe.Fori(0, rounds) as it:
                    for s in range(unroll):
                        pair(it * unroll + (2 + s), s, it * (16 * unroll // size) + turn(2 + s))
                for c in range(2 + rounds * unroll, n_chunks):
                    pair(c, (c - 2) % unroll, turn(c))
                pe.wait_ge(S("act_ready"), base + n_chunks)
                down((first + n_chunks - 1) % size, (n_chunks - 1) % 2, False)

            def route():
                pe.wait_ge(S("u_ready"), 4)
                for t in range(NT):
                    for k in range(KB):
                        last = mm(bank[6][:, t * NE:(t + 1) * NE], uT[:, k, t * P:(t + 1) * P], rts[:, k, :],
                                  start=(k == 0), stop=(k == KB - 1))
                last.then_inc(S("logits_done"), 1)
                pe.wait_ge(S("sel_ready"), 1)
                mm(bank[7][:, 0:NE], C("before"), sel[:, 0, :], start=True, stop=True)
                mm(bank[7][:, NE:2 * NE], ones, sel[:, 0, :], start=True, stop=False)
                mm(bank[7][:, NE:2 * NE], C("before"), sel[:, 1, :], start=False, stop=True)
                mm(bank[7][:, 2 * NE:3 * NE], ones, sel[:, 0, :], start=True, stop=False)
                mm(bank[7][:, 2 * NE:3 * NE], ones, sel[:, 1, :], start=False, stop=True)\
                    .then_inc(S("queues_done"), 1)

            def spread_weights():
                pe.wait_ge(S("comb_ready"), 1)
                for t in range(NT):
                    last = nc.tensor.transpose(bank[7][0:NE, t * P:(t + 1) * P], lgt[:, t, :], ident)
                last.then_inc(S("combT_done"), 1)
                pe.wait_ge(S("combT_taken"), 1)
                for e in range(NE):
                    if e >= 2:
                        pe.wait_ge(S("combB_taken"), e - 1)
                    mm(bank[6 + e % 2][:, 0:T], ident[0:NE, e:e + 1].to_broadcast([NE, P]), cT[:, :], start=True,
                       stop=True).then_inc(S("combB_done"), 1)

            def gathered_experts():
                for t in range(NT):
                    for k in range(KB):
                        last = nc.tensor.transpose(bank[2 * t + k // 4][:, (k % 4) * P:(k % 4 + 1) * P],
                                                   uT[:, k, t * P:(t + 1) * P], ident)
                    last.then_inc(S("utok_done"), 1)
                for e in range(NE):
                    pe.wait_ge(S("pick_ready"), e + 1)
                    if e >= 2:
                        pe.wait_ge(S("gt_taken"), e - 1)
                    for t in range(NT):
                        last = nc.tensor.transpose(bank[6 + e % 2][0:CAP, t * P:(t + 1) * P], pickw[:, t, e, :], ident)
                    last.then_inc(S("gt_done"), 1)
                pe.wait_ge(S("utok_taken"), NT)
                pe.wait_ge(S("gt_taken"), NE)

                def gate_up_g(slot, par, parts):
                    for q in range(2):
                        pe.wait_ge(S("low_ready"), parts + q)
                        for k in range(4):
                            w = [x[:, k * 2 * P:(k + 1) * 2 * P] for x in (w_high[:, par, q, :],
                                                                          half(low_slot(slot), q))]
                            at = (4 * q + k) * CAP
                            for x, y in ((0, 0), (0, 1), (1, 0)):
                                last = mm(bank[4 + par][0:CAP, 0:2 * P], x_high[:, x, at:at + CAP], w[y],
                                          start=(q + k + x + y == 0), stop=(q == 1 and k == 3 and x == 1))
                    last.then_inc(S("gate_up_done"), 1)

                def down_g(slot, par, first):
                    w = dn_slot(slot)
                    for m in range(KB):
                        last = mm(bank[6 + m // 4][:, (m % 4) * CAP:(m % 4 + 1) * CAP], w[:, m, :], hcol[:, par, :],
                                  start=(first and m % 4 == 0), stop=False, skip_group_check=True)
                    last.then_inc(S("down_done"), 1)

                with pe.Fori(0, NE) as e:
                    for k in range(KB):
                        for t in range(NT):
                            last = mm(bank[k // 4][:, (k % 4) * CAP:(k % 4 + 1) * CAP],
                                      utok[:, t, k * P:(k + 1) * P],
                                      pick[:, t, bass.ds(e, 1), :].rearrange("p a s -> p (a s)"), start=(t == 0),
                                      stop=(t == NT - 1))
                        if k % 4 == 3:
                            last.then_inc(S("gather_done"), 1)
                    pe.wait_ge(S("x_low_ready"), e * 2 + 2)
                    for c in range(-1, ET + 1):
                        if c + 1 < ET:
                            pe.wait_ge(S("act_ready"), e * ET + (FT + c))
                            gate_up_g((c + 1) % MRING, (c + 1) % 2, e * 2 * ET + (2 * (c + 1) + 1))
                        if 0 <= c < ET:
                            pe.wait_ge(S("act_ready"), e * ET + (FT + c + 1))
                            if c >= 2:
                                pe.wait_ge(S("hcol_ready"), e * ET + (c - 1))
                            nc.tensor.transpose(bank[2 + c % 2][:, 0:CAP], hrow[0:CAP, c % 2, :],
                                                ident[0:CAP, 0:CAP]).then_inc(S("hcol_done"), 1)
                        if c >= 1:
                            pe.wait_ge(S("hcol_ready"), e * ET + c)
                            down_g((c - 1) % MRING, (c - 1) % 2, c == 1)
                    pe.wait_ge(S("ycol_ready"), e * 2 + 2)
                    for k in range(KB):
                        last = nc.tensor.transpose(bank[2 + k // 4][0:CAP, (k % 4) * P:(k % 4 + 1) * P],
                                                   ycol[:, k, :], ident)
                        if k % 4 == 3:
                            last.then_inc(S("yrow_done"), 1)
                    pe.wait_ge(S("yrow_ready"), e * 2 + 2)
                    for k in range(KB):
                        last = mm(bank[k // 2][:, (k % 2) * T:(k % 2 + 1) * T], yrow[0:CAP, k * P:(k + 1) * P],
                                  gT[0:CAP, bass.ds(e, 1), :].rearrange("p a t -> p (a t)"), start=True, stop=True)
                        if k % 2:
                            last.then_inc(S("scatter_done"), 1)
                    pe.wait_ge(S("h_added"), e * 4 + 2)

            pe.wait_ge(S("par_loaded"), 96)
            for l in range(2):
                norm(2 * l)
                for u in range(6):
                    project(l, u)
                rotary(l, 0)
                project(l, 6)
                rotary(l, 1)
                lora_up(l)
                rotary(l, 2)
                if l == 1:
                    value_residual()
                project(l, 7)
                pe.wait_ge(S("sw_ready"), l + 1)
                head_sum("kk2_ready", l + 1, "kksum_done", 2, flat(tmpA))
                for u in range(8, 11):
                    project(l, u)
                head_sum("rk_ready", l + 1, "rksum_done", 3, flat(bonus))
                project(l, 11)
                scores(l, 0)
                scores(l, 1)
                for h in range(5):
                    project(l, 12 + h)
                    attend(l, h)
                    if h < 4:
                        scores(l, h + 2)
                gla_gates(l)
                rwkv_products(l)
                attend(l, 5)
                pe.wait_ge(S("tok_taken"), 4 * l + 2)
                pairwise(l, 0, None, Bt, At)
                level0(l)
                invert_product(l, 1)
                invert_update(l, 1)
                invert_product(l, 2)
                gla_token_major(l)
                invert_update(l, 2)
                invert_product(l, 3)
                gla_pairwise(l, 0)
                invert_update(l, 3)
                invert_product(l, 4)
                gla_pairwise(l, 1)
                invert_update(l, 4)
                gla_scan(l, 0)
                invert_product(l, 5)
                gla_scan(l, 1)
                invert_update(l, 5)
                gla_scan(l, 2)
                pe.wait_ge(S("y_updated"), l * 10 + 10)
                pairwise(l, 1, None, Kt, At)
                gla_scan(l, 3)
                gla_inside(l)
                rwkv_solve_nv(l)
                pe.wait_ge(S("r_ready"), l + 1)
                pairwise(l, 2, None, Bt, ym)
                pairwise(l, 3, None, Kt, ym)
                gla_norm(l)
                rwkv_solve_c(l)
                rwkv_scan(l)
                group_norm(l)
                out_block(l, 6)
                out_block(l, 7)
                norm(2 * l + 1)
                if l == 0:
                    pe.wait_ge(S("u_ready"), 2)
                    channel_mixer(FT, RING, "slot", NCI + NCO, 0)
                else:
                    route()
                    pe.wait_ge(S("count_ready"), 1)
                    most = pe.value_load(countI[0:1, 0:1], min_val=0, max_val=T)
                    with pe.If(most < CAP + 1):
                        gathered_experts()
                    with pe.Else():
                        spread_weights()
                        channel_mixer(NM, MRING, "moe", 0, FT)
            norm(4)

        @block.scalar
        def _(act):
            a = nc.scalar.activation
            chain = [0]

            def link(ins):
                chain[0] += 1
                ins.then_inc(S("act_step"), 1)
                act.wait_ge(S("act_step"), chain[0])

            def norm_std(n):
                act.wait_ge(S("norm_summed"), n + 1)
                link(a(std[:, :], bank[7][:, 0:T], ACT.Ln, scale=1.0 / D, bias=epsr[:, 0:1]))
                a(rstd[:, :], std[:, :], ACT.Exp, scale=-0.5).then_inc(S("std_ready"), 1)

            def take(l, u):
                unit = UNITS[u]
                act.wait_ge(S("proj_done"), l * NU + u + 1)
                b = pb[u % 2]
                n = len(unit)
                two = b[:, 0:n * T].rearrange("p (a t) -> p a t", a=n) if unit[0] not in ("av", "gv") else None
                if u < 4:
                    dst, src = ypad[:, 2 * u:2 * u + n, 1:T + 1], two
                elif u < 7:
                    dst, src = aqk[:, 2 * (u - 4):2 * (u - 4) + 2, :], two
                elif u == 7:
                    dst, src = gd[:, :], b[0:16, 0:T]
                elif unit[0] == "av":
                    dst, src = av[:, unit[1], :], b[:, 0:AW]
                elif u < 13:
                    dst, src = gqk[:, 2 * (u - 10):2 * (u - 10) + 2, :], two
                elif unit[0] == "gv":
                    dst, src = gv[:, unit[1], :], b[:, 0:GW]
                else:
                    dst, src = og[:, 2 * (u - 15):2 * (u - 15) + n, :], two
                a(dst, src, ACT.Copy).then_inc(S("proj_taken"), 1)

            def use_ln_exp():
                nc.scalar.preload_act_table_set("natural_log_exp_and_others")

            use_ln_exp()
            act.wait_ge(S("par_loaded"), 96)
            act.wait_ge(S("eps_set"), 1)
            for l in range(2):
                norm_std(2 * l)
                for u in range(4):
                    take(l, u)
                act.wait_ge(S("wag_mixed"), l + 1)
                a(tw[64:128, :], ym[64:128, 6, :], ACT.Sigmoid)
                a(tw[0:32, :], ym[0:32, 6, :], ACT.Tanh)
                a(tw[32:64, :], ym[32:64, 6, :], ACT.Copy).then_inc(S("tw_ready"), 1)
                if l == 0:
                    act.wait_ge(S("angles_ready"), 1)
                    a(cosT[:, :], tmpB[:, 0, :], ACT.Sin)
                    a(sinT[:, :], tmpB[:, 1, :], ACT.Sin).then_inc(S("rope_ready"), 1)
                for u in range(4, 7):
                    take(l, u)
                act.wait_ge(S("lora_done"), 3 * l + 1)
                for p in range(RP):
                    last = a(sw[:, p, :], bank[2][:, p * T:(p + 1) * T], ACT.Sigmoid, bias=PR(l, "w0", p))
                last.then_inc(S("sw_ready"), 1)
                act.wait_ge(S("lora_done"), 3 * l + 2)
                for p in range(RP):
                    last = a(aa[:, p, :], bank[3][:, p * T:(p + 1) * T], ACT.Sigmoid, bias=PR(l, "a0", p))
                last.then_inc(S("aa_ready"), 1)
                if l == 1:
                    act.wait_ge(S("v2_done"), 1)
                    for p in range(RP):
                        last = a(tmpB[:, p, :], bank[5][:, p * T:(p + 1) * T], ACT.Sigmoid, bias=PR(l, "v0", p))
                    last.then_inc(S("v_gate"), 1)
                take(l, 7)
                use_ln_exp()
                act.wait_ge(S("cs_ready"), l + 1)
                a(flat(At), flat(sw), ACT.Exp, scale=-DECAY)
                a(flat(Kt), flat(tmpC), ACT.Exp, scale=DECAY)
                act.wait_ge(S("kksum_done"), l + 1)
                a(flat(tmpA), flat(tmpC), ACT.Exp, scale=-DECAY).then_inc(S("decay_ready"), 1)
                act.wait_ge(S("kk_floor"), l + 1)
                link(a(flat(tmpB), flat(tmpB), ACT.Ln, scale=65536.0))
                a(flat(tmpB), flat(tmpB), ACT.Exp, scale=-0.5, bias=epsr[:, 2:3]).then_inc(S("kk_norm"), 1)
                for u in range(8, 12):
                    take(l, u)

                def exponentials(h):
                    i = l * 6 + h
                    act.wait_ge(S("max_ready"), i + 1)
                    for t in range(NT):
                        n = (t + 1) * P
                        x = sc[:, h % 2, t * P:t * P + n]
                        last = a(x, x, ACT.Exp, bias=mxn[:, h % 2, t:t + 1], accum_out=den[:, h % 2, t:t + 1])
                    last.then_inc(S("exp_done"), 1)

                def take_head(h):
                    i = l * 6 + h
                    act.wait_ge(S("pt_done"), i + 1)
                    if h >= 2:
                        act.wait_ge(S("ao_done"), i - 1)
                    a(pt[:, h % 2, :], bank[6][:, 0:384], ACT.Copy).then_inc(S("pt_taken"), 1)
                    if h % 2:
                        act.wait_ge(S("ao_done"), i + 1)
                        a(mixT[:, RP + h // 2, :], bank[7][:, 0:T], ACT.Copy).then_inc(S("ao_taken"), 1)

                exponentials(0)
                exponentials(1)
                for h in range(5):
                    take(l, 12 + h)
                    take_head(h)
                    if h < 4:
                        exponentials(h + 2)
                act.wait_ge(S("gz_done"), l + 1)
                act.wait_ge(S("negb_ready"), l + 1)
                for p in range(GP):
                    z, c = bank[p // 2][:, (p % 2) * T:(p % 2 + 1) * T], slice(p * T, (p + 1) * T)
                    a(gE[:, c], z, ACT.Abs, bias=PR(l, "gb", p))
                    last = a(gEi[:, c], z, ACT.Relu, scale=-1.0, bias=negb[:, p:p + 1])
                link(last)
                for q in range(4):
                    act.wait_ge(S("tok_done"), 4 * l + q + 1)
                    a(tokm[:, q, :, :].rearrange("p t c -> p (t c)"), bank[2 + q][:, :], ACT.Copy)\
                        .then_inc(S("tok_taken"), 1)
                link(a(gE[:, :], gE[:, :], ACT.Exp, scale=-1.0))
                a(gE[:, :], gE[:, :], ACT.Ln, bias=1.0).then_inc(S("gln_ready"), 1)
                take_head(5)

                def take_product(lev):
                    for g in range(2):
                        i = l * 10 + (lev - 1) * 2 + g
                        act.wait_ge(S("t1_done"), i + 1)
                        if lev > 1:
                            act.wait_ge(S("yd_done"), i - 1)
                        a(T1[:, g, :, :].rearrange("p m c -> p (m c)"), bank[2 + g][:, :], ACT.Copy)\
                            .then_inc(S("t1_taken"), 1)

                take_product(1)
                act.wait_ge(S("gcs_ready"), l + 1)
                a(gE[:, :], gU[:, :], ACT.Exp, scale=1.0 / 16)
                a(gEi[:, :], gU[:, :], ACT.Exp, scale=-1.0 / 16).then_inc(S("gdecay_ready"), 1)
                take_product(2)
                act.wait_ge(S("ktok_done"), l + 1)
                for t in range(NT):
                    last = a(ktok[:, t, :], bank[6 + t][:, 0:384], ACT.Copy)
                last.then_inc(S("ktok_taken"), 1)
                for lev in range(3, 6):
                    take_product(lev)
                act.wait_ge(S("go_done"), l + 1)
                a(gS[:, 0:512], bank[0][:, :], ACT.Copy)
                a(gS[:, 512:768], bank[1][:, 0:T], ACT.Copy)
                a(gU[:, 0:512], bank[0][:, :], ACT.Square)
                a(gU[:, 512:768], bank[1][:, 0:T], ACT.Square).then_inc(S("go_squared"), 1)
                act.wait_ge(S("nv_done"), l + 1)
                a(flat(nv), bank[4][:, :], ACT.Copy).then_inc(S("nv_taken"), 1)
                act.wait_ge(S("wt_done"), l + 1)
                a(flat(wt), bank[5][:, :], ACT.Copy).then_inc(S("wt_taken"), 1)
                act.wait_ge(S("gvar_done"), l + 1)
                a(gE[:, 0:512], bank[6][:, :], ACT.Ln, scale=1.0 / HD, bias=epsr[:, 0:1])
                link(a(gE[:, 512:768], bank[7][:, 0:T], ACT.Ln, scale=1.0 / HD, bias=epsr[:, 0:1]))
                a(gE[:, :], gE[:, :], ACT.Exp, scale=-0.5).then_inc(S("gstd_ready"), 1)
                act.wait_ge(S("c_done"), l + 1)
                a(flat(c0), bank[4][:, :], ACT.Copy).then_inc(S("c_taken"), 1)
                a(og[:, :, :].rearrange("p a t -> p (a t)"), og[:, :, :].rearrange("p a t -> p (a t)"), ACT.Silu)\
                    .then_inc(S("og_ready"), 1)
                use_ln_exp()
                act.wait_ge(S("ro_done"), l + 1)
                a(flat(tmpC), bank[5][:, :], ACT.Copy).then_inc(S("ro_taken"), 1)
                act.wait_ge(S("var_done"), l + 1)
                link(a(flat(tmpA), bank[3][:, :], ACT.Ln, scale=1.0 / HD, bias=epsr[:, 1:2]))
                a(flat(tmpA), flat(tmpA), ACT.Exp, scale=-0.5).then_inc(S("gn_std"), 1)
                norm_std(2 * l + 1)

                def silu(c, par, guard=True):
                    act.wait_ge(S("gate_up_done"), c + 1)
                    if guard:
                        act.wait_ge(S("act_ready"), c - 1)
                    a(sil[:, par, :], bank[4 + par][:, 0:T], ACT.Silu).then_inc(S("silu_done"), 1)


                def all_tokens(base, n):
                    for c in range(2):
                        silu(base + c, c, base > 0)
                    with act.Fori(0, (n - 2) // RING) as it:
                        for s in range(RING):
                            silu(it * RING + (base + 2 + s), s % 2)
                    for c in range(2 + (n - 2) // RING * RING, n):
                        silu(base + c, c % 2)

                if l == 0:
                    all_tokens(0, FT)
                    use_ln_exp()
            act.wait_ge(S("logit_max"), 1)
            for t in range(NT):
                last = a(lgt[:, t, :], lgt[:, t, :], ACT.Exp, bias=nmax[:, t:t + 1])
            last.then_inc(S("logit_exp"), 1)
            act.wait_ge(S("count_ready"), 1)
            most = act.value_load(countI[0:1, 0:1], min_val=0, max_val=T)
            with act.If(most < CAP + 1):
                for t in range(NT):
                    act.wait_ge(S("utok_done"), t + 1)
                    for b in range(2):
                        last = a(utok[:, t, b * 512:(b + 1) * 512], bank[2 * t + b][:, :], ACT.Copy)
                    last.then_inc(S("utok_taken"), 1)
                for e in range(NE):
                    act.wait_ge(S("gt_done"), e + 1)
                    a(gT[0:CAP, e, :], bank[6 + e % 2][0:CAP, 0:T], ACT.Copy).then_inc(S("gt_taken"), 1)
                def round_weights(e, c):
                    act.wait_ge(S(f"moe{c % MRING}_loaded"), e * (16 * ET // MRING) + 16 * (c // MRING + 1))
                    if c >= 2:
                        act.wait_ge(S("gate_up_done"), e * ET + (FT + c - 1))
                    for q in range(2):
                        a(w_high[:, c % 2, q, :], half(slot(c % MRING), q), ACT.Copy).then_inc(S("high_ready"), 1)

                with act.Fori(0, NE) as e:
                    act.wait_ge(S("gate_up_done"), e * ET + FT)
                    round_weights(e, 0)
                    for b in range(2):
                        act.wait_ge(S("gather_done"), e * 2 + (b + 1))
                        a(x_high[:, 0, b * 4 * CAP:(b + 1) * 4 * CAP], bank[b][:, 0:4 * CAP], ACT.Copy)\
                            .then_inc(S("x_high_ready"), 1)
                    round_weights(e, 1)
                    for c in range(ET):
                        act.wait_ge(S("gate_up_done"), e * ET + (FT + c + 1))
                        act.wait_ge(S("act_ready"), e * ET + (FT + c - 1))
                        a(silg[0:CAP, c % 2, :], bank[4 + c % 2][0:CAP, 0:P], ACT.Silu).then_inc(S("silu_done"), 1)
                        if c + 2 < ET:
                            round_weights(e, c + 2)
                        act.wait_ge(S("hcol_done"), e * ET + (c + 1))
                        if c >= 2:
                            act.wait_ge(S("down_done"), e * ET + (FT + c - 1))
                        a(hcol[:, c % 2, :], bank[2 + c % 2][:, 0:CAP], ACT.Copy).then_inc(S("hcol_ready"), 1)
                    act.wait_ge(S("down_done"), e * ET + (FT + ET))
                    for b in range(2):
                        a(ycol[:, 4 * b:4 * b + 4, :].rearrange("p k s -> p (k s)"), bank[6 + b][:, 0:4 * CAP],
                          ACT.Copy).then_inc(S("ycol_ready"), 1)
            with act.Else():
                all_tokens(FT, NM)
            use_ln_exp()
            norm_std(4)

        @block.vector
        def _(dve):
            v = nc.vector
            tt, stt, ts = v.tensor_tensor, v.scalar_tensor_tensor, v.tensor_scalar
            chain = [0]

            def link(ins):
                chain[0] += 1
                ins.then_inc(S("dve_step"), 1)
                dve.wait_ge(S("dve_step"), chain[0])

            def tell(ins, name, val):
                ins.then_inc(S(name), 1)
                dve.wait_ge(S(name), val)

            def square(n):
                v.tensor_tensor(flat(uT), flat(hT), flat(hT), ALU.mult).then_inc(S("sq_ready"), 1)

            def scale_rows(n, g, l):
                dve.wait_ge(S("std_ready"), n + 1)
                for k in range(KB):
                    last = stt(uT[:, k, :], hT[:, k, :], PR(l, g, k), rstd[:, :], ALU.mult, ALU.mult)
                return last

            v.memset(epsr[:, 1:2], GN_EPS)
            v.memset(epsr[:, 2:3], LN256)
            v.memset(epsr[:, 0:1], RMS_EPS).then_inc(S("eps_set"), 1)
            dve.wait_ge(S("x_loaded"), 16)
            square(0)
            dve.wait_ge(S("pos_loaded"), 16)
            dve.wait_ge(S("par_loaded"), 96)

            def rotary_angles():
                link(v.tensor_copy(tmpA[:, 1, :], tmpA[:, 0, :].bitcast(I32)))
                link(ts(tmpA[:, 1, :], tmpA[:, 1, :], C("freq", 1), None, ALU.mult))
                both = [P, 2, T]
                r, k, x = tmpB[:, :, :], tmpC[:, :, :], tmpA[:, 1, :].unsqueeze(1).to_broadcast(both)
                for i, (turn, shift) in enumerate(((0.25, PI / 2), (0.0, 0.0))):
                    last = ts(tmpC[:, i, :], tmpA[:, 1, :], 1.0 / (2 * PI), turn, ALU.mult, ALU.add)
                link(last)
                link(ts(k, k, ROUND, -ROUND, ALU.add, ALU.add))
                link(stt(r, k, -C1, x, ALU.mult, ALU.add))
                link(stt(r, k, -C2, r, ALU.mult, ALU.add))
                link(stt(r, k, -C3, r, ALU.mult, ALU.add))
                link(ts(tmpB[:, 0, :], tmpB[:, 0, :], PI / 2, None, ALU.add))
                link(ts(k, r, PI, -2 * PI, ALU.is_gt, ALU.mult))
                link(tt(r, r, k, ALU.add))
                link(ts(k, r, -PI, 2 * PI, ALU.is_lt, ALU.mult))
                link(tt(r, r, k, ALU.add))
                ts(r, r, 3.1415925, -3.1415925, ALU.min, ALU.max).then_inc(S("angles_ready"), 1)

            for l in range(2):
                link(v.memset(ypad[:, :, 0:1], 0.0))
                scale_rows(2 * l, "mix_g", l).then_inc(S("u_ready"), 1)
                ts(negb[:, :], prm[:, l, PCOL["gb"]:PCOL["gb"] + GP], -1.0, None, ALU.mult)\
                    .then_inc(S("negb_ready"), 1)
                if l == 0:
                    rotary_angles()
                dve.wait_ge(S("proj_taken"), l * NU + 4)
                link(tt(ym[:, 6, :], ypad[:, 6, 0:T], ypad[:, 6, 1:T + 1], ALU.subtract))
                stt(ym[:, 6, :], ym[:, 6, :], PR(l, "mu", 6), ypad[:, 6, 1:T + 1], ALU.mult, ALU.add)\
                    .then_inc(S("wag_mixed"), 1)
                link(tt(ym[:, 0:6, :], ypad[:, 0:6, 0:T], ypad[:, 0:6, 1:T + 1], ALU.subtract))
                for i in range(6):
                    last = stt(ym[:, i, :], ym[:, i, :], PR(l, "mu", i), ypad[:, i, 1:T + 1], ALU.mult, ALU.add)
                tell(last, "v_mixed", l + 1)
                r_, k_, v_ = ym[:, 0:2, :], ym[:, 2:4, :], ym[:, 4:6, :]
                for p in range(RP):
                    last = ts(kk[:, p, :], k_[:, p, :], PR(l, "kk", p), None, ALU.mult)
                link(last)

                def rotate(i):
                    dve.wait_ge(S("rope_ready"), 1)
                    dve.wait_ge(S("rot_done"), 3 * l + i + 1)
                    x = aqk[:, 2 * i:2 * i + 2, :]
                    two = [P, 2, T]
                    tell(tt(rtmp, bank[6][:, :].rearrange("p (a t) -> p a t", a=2),
                            sinT[:, :].unsqueeze(1).to_broadcast(two), ALU.mult), "rot_taken", 3 * l + i + 1)
                    link(tt(x, x, cosT[:, :].unsqueeze(1).to_broadcast(two), ALU.mult))
                    tell(tt(x, x, rtmp, ALU.add), "qk_ready", 3 * l + i + 1)

                rotate(0)
                rotate(1)
                dve.wait_ge(S("sw_ready"), l + 1)
                link(v.tensor_tensor_scan(flat(tmpC), C("reset", 512), flat(sw), 0.0, ALU.mult, ALU.add))
                tt(flat(sw), flat(tmpC), flat(sw), ALU.subtract).then_inc(S("cs_ready"), 1)
                dve.wait_ge(S("lora_done"), 3 * l + 3)
                v.tensor_copy(flat(gg), bank[4][:, :]).then_inc(S("gg_ready"), 1)
                rotate(2)
                if l == 1:
                    dve.wait_ge(S("v1_done"), 1)
                    v.tensor_copy(tmpA[0:16, 0, :], bank[5][0:16, 0:T]).then_inc(S("v1_taken"), 1)
                    dve.wait_ge(S("v_gate"), 1)
                    link(tt(rtmp, vfirst[:, :, :], v_, ALU.subtract))
                    link(tt(rtmp, rtmp, tmpB[:, :, :], ALU.mult))
                    tell(tt(v_, v_, rtmp, ALU.add), "v_ready", 2)
                else:
                    tell(v.tensor_copy(vfirst[:, :, :], v_), "v_ready", 1)
                tt(tmpA[:, :, :], kk[:, :, :], kk[:, :, :], ALU.mult).then_inc(S("kk2_ready"), 1)
                dve.wait_ge(S("kksum_done"), l + 1)
                ts(flat(tmpB), bank[2][:, :], 1e-24, None, ALU.max).then_inc(S("kk_floor"), 1)
                dve.wait_ge(S("kk_norm"), l + 1)
                link(tt(flat(kk), flat(kk), flat(tmpB), ALU.mult))
                dve.wait_ge(S("aa_ready"), l + 1)
                for p in range(RP):
                    last = ts(tmpB[:, p, :], aa[:, p, :], -1.0, PR(l, "ka", p), ALU.add, ALU.mult)
                link(last)
                link(stt(flat(tmpB), flat(tmpB), 1.0, ym[:, 2:4, :].rearrange("p a t -> p (a t)"), ALU.add, ALU.mult))
                for p in range(RP):
                    last = stt(bonus[:, p, :], r_[:, p, :], PR(l, "rk", p), tmpB[:, p, :], ALU.mult, ALU.mult)
                last.then_inc(S("rk_ready"), 1)
                dve.wait_ge(S("decay_ready"), l + 1)
                link(tt(flat(aa), flat(aa), flat(kk), ALU.mult))
                stt(flat(At), flat(kk), -1.0, flat(At), ALU.mult, ALU.mult).then_inc(S("a_ready"), 1)
                tt(flat(Bt), flat(aa), flat(Kt), ALU.mult).then_inc(S("b_ready"), 1)
                tt(flat(Kt), flat(tmpB), flat(Kt), ALU.mult).then_inc(S("k_ready"), 1)
                v.tensor_copy(lc[:, :, :], tmpA[:, :, CH - 1::CH])
                tt(r_, r_, tmpA[:, :, :], ALU.mult).then_inc(S("r_ready"), 1)

                def soft_max(h):
                    i = l * 6 + h
                    b = h % 2
                    dve.wait_ge(S("score_done"), i + 1)
                    if h >= 2:
                        dve.wait_ge(S("pt_done"), i - 1)
                    tell(stt(sc[:, b, :], bank[4 + b][:, 0:384], 0.125, C("lnw", 384), ALU.mult, ALU.add),
                         "score_taken", i + 1)
                    for t in range(NT):
                        last = v.tensor_reduce(mxn[:, b, t:t + 1], sc[:, b, t * P:t * P + (t + 1) * P], AX.X, ALU.max,
                                               negate=True)
                    last.then_inc(S("max_ready"), 1)

                def soft_scale(h):
                    i = l * 6 + h
                    b = h % 2
                    dve.wait_ge(S("exp_done"), i + 1)
                    link(v.reciprocal(rden[:, b, :], den[:, b, :]))
                    for t in range(NT):
                        x = sc[:, b, t * P:t * P + (t + 1) * P]
                        last = ts(x, x, rden[:, b, t:t + 1], None, ALU.mult)
                    last.then_inc(S("prob_ready"), 1)

                soft_max(0)
                soft_max(1)
                dve.wait_ge(S("rksum_done"), l + 1)
                tt(bonus[:, :, :], bank[3][:, :].rearrange("p (a t) -> p a t", a=RP), v_, ALU.mult)\
                    .then_inc(S("bonus_ready"), 1)
                for h in range(6):
                    soft_scale(h)
                    if h < 4:
                        soft_max(h + 2)
                for g in range(2):
                    dve.wait_ge(S("pair_done"), l * 8 + g + 1)
                    b = bank[2 + g][:, :].rearrange("p (m c) -> p m c", m=4)
                    m4 = [P, 4, P]
                    dve.wait_ge(S("tok_taken"), 4 * l + 2)
                    tt(MT[:, g, :, :], b, C("strict").unsqueeze(1).to_broadcast(m4), ALU.mult)\
                        .then_inc(S("pair_taken"), 1)
                    dve.wait_ge(S("pair_taken"), l * 8 + g + 1)
                    tell(tt(T1[:, g, :, :], MT[:, g, :, :], C("lev").unsqueeze(1).to_broadcast(m4), ALU.mult),
                         "y0_ready", 2 * l + g + 1)
                    tt(Y[:, g, :, :], T1[:, g, :, :], ident.unsqueeze(1).to_broadcast(m4), ALU.add)\
                        .then_inc(S("mt_ready"), 1)
                dve.wait_ge(S("gln_ready"), l + 1)
                dve.wait_ge(S("ao_done"), 6 * l + 6)
                link(stt(gE[:, :], gEi[:, :], -1.0, gE[:, :], ALU.mult, ALU.subtract))
                v.tensor_tensor_scan(gU[:, :], C("reset", 768), gE[:, :], 0.0, ALU.mult, ALU.add)\
                    .then_inc(S("gcs_ready"), 1)
                for g in range(2):
                    dve.wait_ge(S("m0_done"), 2 * l + g + 1)
                    b = bank[4 + g][:, :].rearrange("p (m c) -> p m c", m=4)
                    tt(X[:, g, :, :], b, ident.unsqueeze(1).to_broadcast(m4), ALU.add).then_inc(S("x0_ready"), 1)

                def update_inverse(lev):
                    for g in range(2):
                        i = l * 10 + (lev - 1) * 2 + g
                        if lev < 5:
                            dve.wait_ge(S("xd_done"), l * 8 + (lev - 1) * 2 + g + 1)
                            b = bank[4 + g][:, :].rearrange("p (m c) -> p m c", m=4)
                            tt(X[:, g, :, :], b, X[:, g, :, :], ALU.add).then_inc(S("x_updated"), 1)
                        dve.wait_ge(S("yd_done"), i + 1)
                        b = bank[2 + g][:, :].rearrange("p (m c) -> p m c", m=4)
                        tt(Y[:, g, :, :], b, Y[:, g, :, :], ALU.add).then_inc(S("y_updated"), 1)

                def take_gla_pairs(i):
                    dve.wait_ge(S("gatt_done"), 2 * l + i + 1)
                    lo, hi = ((0, 4), (4, 6))[i]
                    for g in range(2):
                        last = v.copy_predicated(
                            gatt[:, g, lo:hi, :], C("incl").bitcast(I32).unsqueeze(1).to_broadcast([P, hi - lo, P]),
                            bank[6 + g][:, 0:(hi - lo) * P].rearrange("p (m c) -> p m c", m=hi - lo))
                    last.then_inc(S("gatt_taken"), 1)

                def gla_state(n):
                    dve.wait_ge(S("gds_done"), l * NCH + n + 1)
                    three = [P, GP, P]
                    link(tt(gtmp[:, :, :], bank[6][:, 0:384].rearrange("p (a c) -> p a c", a=GP),
                            blk.unsqueeze(1).to_broadcast(three), ALU.mult))
                    link(tt(gst[:, :, :], gst[:, :, :], gtmp[:, :, :], ALU.add))
                    tt(gst[:, :, :], gst[:, :, :], lgc[:, :, n].unsqueeze(2).to_broadcast(three), ALU.mult)\
                        .then_inc(S("gstate_ready"), 1)

                update_inverse(1)
                dve.wait_ge(S("gdecay_ready"), l + 1)
                q3 = gqk[:, 0:3, :].rearrange("p a t -> p (a t)")
                k3 = gqk[:, 3:6, :].rearrange("p a t -> p (a t)")
                tt(k3, k3, gEi[:, :], ALU.mult)
                stt(q3, q3, 0.125, gE[:, :], ALU.mult, ALU.mult).then_inc(S("gk_ready"), 1)
                v.memset(gst[:, :, :], 0.0)
                v.memset(qkf, 0.0)
                v.tensor_copy(lgc[:, :, :], gE[:, :].rearrange("p (a t) -> p a t", a=GP)[:, :, CH - 1::CH])\
                    .then_inc(S("gstate_ready"), 1)
                dve.wait_ge(S("gstate_ready"), l * (NCH + 1) + 1)
                update_inverse(2)
                take_gla_pairs(0)
                update_inverse(3)
                take_gla_pairs(1)
                update_inverse(4)
                gla_state(0)
                gla_state(1)
                update_inverse(5)
                gla_state(2)
                for n, (dst, mask) in ((1, (MT, "strict")), (2, (T1, "incl")), (3, (X, "incl"))):
                    for g in range(2):
                        dve.wait_ge(S("pair_done"), l * 8 + 2 * n + g + 1)
                        if n == 1:
                            dve.wait_ge(S("level_part"), l * 10 + 10)
                        b = bank[2 + g][:, :].rearrange("p (m c) -> p m c", m=4)
                        tt(dst[:, g, :, :], b, C(mask).unsqueeze(1).to_broadcast(m4), ALU.mult)\
                            .then_inc(S("pair_taken"), 1)
                    if n == 1:
                        gla_state(3)

                def gla_output():
                    dve.wait_ge(S("gstd_ready"), l + 1)
                    link(tt(gS[:, :], gS[:, :], gE[:, :], ALU.mult))
                    dve.wait_ge(S("og_ready"), l + 1)
                    stt(mixT[:, 5:8, :].rearrange("p a t -> p (a t)"), gS[:, :], PR(l, "gn"),
                        og[:, :, :].rearrange("p a t -> p (a t)"), ALU.mult, ALU.mult).then_inc(S("gmix_ready"), 1)

                v.memset(st[:, 0:RP, :], 0.0).then_inc(S("state_ready"), 1)
                dve.wait_ge(S("c_taken"), l + 1)
                for n in range(NCH):
                    t, q = n // 2, n % 2
                    rows = slice(q * CH, (q + 1) * CH)
                    dve.wait_ge(S("us_done"), l * NCH + n + 1)
                    tt(uu[rows, t, :], bank[4][rows, 0:T], c0[rows, t, :], ALU.add).then_inc(S("u_chunk"), 1)
                    dve.wait_ge(S("ds_done"), l * NCH + n + 1)
                    dve.wait_ge(S("state_ready"), l * (NCH + 1) + n + 1)
                    for p in range(RP):
                        last = stt(sttmp[:, p, :], bank[4][:, p * P:(p + 1) * P], lc[:, p, n:n + 1], blk, ALU.mult,
                                   ALU.mult)
                    link(last)
                    for p in range(RP):
                        last = stt(st[:, p, :], st[:, p, :], lc[:, p, n:n + 1], sttmp[:, p, :], ALU.mult, ALU.add)
                    last.then_inc(S("state_ready"), 1)
                    if n == 0:
                        gla_output()
                dve.wait_ge(S("mean_done"), l + 1)
                link(stt(flat(tmpC), bank[2][:, :], -1.0 / HD, flat(tmpC), ALU.mult, ALU.add))
                tt(flat(tmpB), flat(tmpC), flat(tmpC), ALU.mult).then_inc(S("cen_ready"), 1)
                dve.wait_ge(S("gn_std"), l + 1)
                link(tt(flat(tmpC), flat(tmpC), flat(tmpA), ALU.mult))
                for p in range(RP):
                    last = ts(tmpC[:, p, :], tmpC[:, p, :], PR(l, "lng", p), PR(l, "lnb", p), ALU.mult, ALU.add)
                link(last)
                link(tt(flat(tmpC), flat(tmpC), flat(bonus), ALU.add))
                tt(mixT[:, 0:RP, :], tmpC[:, :, :], gg[:, :, :], ALU.mult).then_inc(S("rmix_ready"), 1)
                def add_residual(name, val, banks=range(4)):
                    dve.wait_ge(S(name), val)
                    for i, b in enumerate(banks):
                        x = hT[:, 2 * i:2 * i + 2, :].rearrange("p a t -> p (a t)")
                        last = tt(x, bank[b][:, :], x, ALU.add)
                    link(last)

                add_residual("wout_used", NCO * (l + 1), OUT_BANKS)
                square(2 * l + 1)
                tell(scale_rows(2 * l + 1, "ffn_g", l), "u_ready", 2 * l + 2)

                def times_up(c, par, e=None, guard=True):
                    dve.wait_ge(S("silu_done"), c + 1)
                    if guard:
                        dve.wait_ge(S("down_done"), c - 1)
                    up = bank[4 + par][:, T:2 * T]
                    if l == 0:
                        tt(hac[:, par, :], up, sil[:, par, :], ALU.mult).then_inc(S("act_ready"), 1)
                    else:
                        tt(hraw[:, par, :], up, sil[:, par, :], ALU.mult).then_inc(S("raw_ready"), 1)
                        dve.wait_ge(S("raw_ready"), c - (FT - 1))
                        tt(hac[:, par, :], hraw[:, par, :], combB[:, e, :], ALU.mult).then_inc(S("act_ready"), 1)

                if l == 0:
                    for c in range(2):
                        times_up(c, c, guard=False)
                    with dve.Fori(0, (FT - 2) // RING) as it:
                        for s in range(RING):
                            times_up(it * RING + (2 + s), s % 2)
                    for c in range(2 + (FT - 2) // RING * RING, FT):
                        times_up(c, c % 2)
                    add_residual("down_done", FT)
                    square(2)
            dve.wait_ge(S("logits_done"), 1)
            for t in range(NT):
                lg, first = lgt[:, t, :], sel[:, t, :]
                link(v.tensor_copy(lg, bank[6][:, t * NE:(t + 1) * NE]))
                v.tensor_reduce(nmax[:, t:t + 1], lg, AX.X, ALU.max, negate=True)
                other = lg.unsqueeze(1).to_broadcast([P, NE, NE])
                own = lg.unsqueeze(2).to_broadcast([P, NE, NE])
                gt = rt[:, t, 0, :].rearrange("p (a b) -> p a b", a=NE)
                eq = rt[:, t, 1, :].rearrange("p (a b) -> p a b", a=NE)
                tt(gt, other, own, ALU.is_gt)
                link(tt(eq, other, own, ALU.is_equal))
                link(tt(eq, eq, C("tri8", 64).rearrange("p (a b) -> p a b", a=NE), ALU.mult))
                link(tt(gt, gt, eq, ALU.add))
                link(v.tensor_reduce(first, gt, AX.X, ALU.add))
                link(ts(first, first, 2.0, None, ALU.is_lt))
            v.memset(count[:, :], 0.0).then_inc(S("sel_ready"), 1)
            dve.wait_ge(S("sel_ready"), 1)
            v.memset(st[:, :, 0:1], 0.0).then_inc(S("logit_max"), 1)
            dve.wait_ge(S("queues_done"), 1)
            v.tensor_reduce(count[:, :], bank[7][:, 2 * NE:3 * NE], AX.X, ALU.max)
            link(v.tensor_copy(posn[:, :, :].rearrange("p t e -> p (t e)"), bank[7][:, 0:2 * NE]))
            v.tensor_copy(countI[:, :], count[:, :]).then_inc(S("count_ready"), 1)
            dve.wait_ge(S("logit_exp"), 1)
            for t in range(NT):
                w8 = lgt[:, t, :]
                link(tt(w8, w8, sel[:, t, :], ALU.mult))
                link(v.tensor_reduce(rsum[:, t:t + 1], w8, AX.X, ALU.add))
                link(v.reciprocal(rsum[:, t:t + 1], rsum[:, t:t + 1]))
                last = ts(w8, w8, rsum[:, t:t + 1], None, ALU.mult)
            tell(last, "comb_ready", 1)
            dve.wait_ge(S("count_ready"), 1)
            most = dve.value_load(countI[0:1, 0:1], min_val=0, max_val=T)
            with dve.If(most < CAP + 1):
                for e in range(NE):
                    for t in range(NT):
                        ts(pick[:, t, e, :], C("slot", CAP), posn[:, t, e:e + 1], sel[:, t, e:e + 1], ALU.is_equal,
                           ALU.mult)
                        last = ts(pickw[:, t, e, :], C("slot", CAP), posn[:, t, e:e + 1], lgt[:, t, e:e + 1],
                                  ALU.is_equal, ALU.mult)
                    last.then_inc(S("pick_ready"), 1)
                def rest_of_weights(e, c):
                    for q in range(2):
                        dve.wait_ge(S("high_ready"), e * 2 * ET + (2 * c + q + 1))
                        tt(half(low_slot(c % MRING), q), half(slot(c % MRING), q), w_high[:, c % 2, q, :],
                           ALU.subtract).then_inc(S("low_ready"), 1)

                with dve.Fori(0, NE) as e:
                    rest_of_weights(e, 0)
                    for b in range(2):
                        dve.wait_ge(S("x_high_ready"), e * 2 + (b + 1))
                        part_ = slice(b * 4 * CAP, (b + 1) * 4 * CAP)
                        tt(x_high[:, 1, part_], bank[b][:, 0:4 * CAP], x_high[:, 0, part_], ALU.subtract)\
                            .then_inc(S("x_low_ready"), 1)
                    rest_of_weights(e, 1)
                    for c in range(ET):
                        dve.wait_ge(S("silu_done"), e * ET + (FT + c + 1))
                        if c >= 2:
                            dve.wait_ge(S("hcol_done"), e * ET + (c - 1))
                        tt(hrow[0:CAP, c % 2, :], bank[4 + c % 2][0:CAP, P:2 * P], silg[0:CAP, c % 2, :], ALU.mult)\
                            .then_inc(S("act_ready"), 1)
                        if c + 2 < ET:
                            rest_of_weights(e, c + 2)
                    for b in range(2):
                        dve.wait_ge(S("yrow_done"), e * 2 + (b + 1))
                        v.tensor_copy(yrow[0:CAP, b * 512:(b + 1) * 512], bank[2 + b][0:CAP, :])\
                            .then_inc(S("yrow_ready"), 1)
                    for b in range(4):
                        dve.wait_ge(S("scatter_done"), e * 4 + (b + 1))
                        x = hT[:, 2 * b:2 * b + 2, :].rearrange("p a t -> p (a t)")
                        tt(x, bank[b][:, :], x, ALU.add).then_inc(S("h_added"), 1)
                dve.wait_ge(S("h_added"), 4 * NE)
            with dve.Else():
                dve.wait_ge(S("combT_done"), 1)
                v.tensor_copy(cT[:, :], bank[7][0:NE, 0:T]).then_inc(S("combT_taken"), 1)
                for e in range(NE):
                    dve.wait_ge(S("combB_done"), e + 1)
                    v.tensor_copy(combB[:, e, :], bank[6 + e % 2][:, 0:T]).then_inc(S("combB_taken"), 1)
                dve.wait_ge(S("combB_taken"), NE)
                with dve.Fori(0, NE) as e:
                    with dve.Fori(0, ET // RING) as it:
                        for s in range(RING):
                            times_up(e * ET + it * RING + (FT + s), s % 2, bass.ds(e, 1))
                dve.wait_ge(S("down_done"), FT + NM)
                for b in range(4):
                    x = hT[:, 2 * b:2 * b + 2, :].rearrange("p a t -> p (a t)")
                    last = tt(x, bank[b][:, :], x, ALU.add)
                last.then_inc(S("h_general"), 1)
                dve.wait_ge(S("h_general"), 1)
            square(4)
            scale_rows(4, "fin", 0).then_inc(S("final_ready"), 1)


def kernel(**inputs):
    import numpy as np
    import concourse.bacc as bacc
    from concourse.bass_utils import run_bass_kernel_spmd as run

    a = {k: np.asarray(x) for k, x in inputs.items()}

    def cols(x):
        return np.swapaxes(x.reshape(x.shape[:-1] + (-1, P)), -1, -2)

    def rows(x):
        return x.reshape((-1, P) + x.shape[1:]).transpose(1, 0, 2)

    par = np.concatenate([
        cols(a["mix_norm_g"]), cols(a["ffn_norm_g"]), cols(a["rwkv_mu"]), cols(a["rwkv_w0"]), cols(a["rwkv_a0"]),
        cols(a["rwkv_k_k"]), cols(a["rwkv_k_a"]), cols(a["rwkv_r_k"].reshape(2, -1)), cols(a["rwkv_ln_g"]),
        cols(a["rwkv_ln_b"]), cols(np.concatenate([a["rwkv_v0"], a["rwkv_v0"]])), cols(a["gla_gate_b"]),
        cols(np.concatenate([a["gla_norm_g"], a["gla_norm_g"]], axis=1)),
        cols(np.stack([a["final_norm_g"], a["final_norm_g"]]))], axis=2).transpose(1, 0, 2)
    lora = np.concatenate([a["rwkv_w2"], a["rwkv_a2"], a["rwkv_g2"]], axis=1).transpose(1, 0, 2)
    small = np.stack([np.concatenate([a["rwkv_v2"][0], a["gla_gate_up"][l]], axis=1) for l in range(2)], axis=1)
    start = {"wag": 768, "av": 1664, "gv": 2816, "gd": 3200}
    for n, at in (("r", 0), ("k", 256), ("v", 512), ("aq", 896), ("ak", 1280), ("gq", 2048), ("gk", 2432),
                  ("og", 3216)):
        for i in range(3):
            start[f"{n}{i}"] = at + i * P
    w_in = np.stack([np.concatenate([rows(np.concatenate(
        [a["w_in"][l][:, start[n]:start[n] + WIDTH.get(n, P)] for n in tiles], axis=1)).reshape(P, -1)
        for tiles in CHUNKS], axis=1) for l in range(2)])
    w_out = np.stack([rows(a["w_out"][l])[:, list(OUT_ORDER), :].reshape(P, -1) for l in range(2)])

    def mixer(g, u, d):
        n, _, f = g.shape
        gu = np.stack([x.reshape(n, KB, P, f // P, P).transpose(0, 3, 2, 1, 4) for x in (g, u)], axis=4)
        return np.concatenate([gu.reshape(n * f // P, P, 2 * D), d.reshape(n * f // P, P, D)], axis=2)

    arrays = {
        "in_x": rows(a["x"][0].T), "in_pos": a["positions"].reshape(-1), "in_const": constants(), "in_par": par,
        "in_lora": lora, "in_small": small, "in_v1": rows(a["rwkv_v1"][0]), "in_router": rows(a["moe_router"][0]),
        "in_w_in": w_in, "in_w_out": w_out,
        "in_ffn": mixer(a["ffn_w_gate"], a["ffn_w_up"], a["ffn_w_down"]),
        "in_moe": mixer(a["moe_w_gate"][0], a["moe_w_up"][0], a["moe_w_down"][0]),
    }
    arrays = {k: np.ascontiguousarray(x) for k, x in arrays.items()}
    nc = bacc.Bacc("TRN2", target_bir_lowering=False, num_devices=1)
    args = [nc.dram_tensor(k, x.shape, mybir.dt.from_np(x.dtype), kind="ExternalInput").ap()
            for k, x in arrays.items()]
    out = nc.dram_tensor("out_0", (P, KB, T), F32, kind="ExternalOutput").ap()
    build_trunk(nc, *args, out)
    r = run(nc, [arrays], core_ids=[0])
    o = r.results[0]["out_0"]
    return o.transpose(2, 1, 0).reshape(1, T, D)
```

```python
from contextlib import ExitStack

import concourse.bass as bass
from concourse import mybir

F32 = mybir.dt.float32
F32R = mybir.dt.float32r
I32 = mybir.dt.int32
ALU = mybir.AluOpType
ACT = mybir.ActivationFunctionType
AX = mybir.AxisListType

P = 128
D = 1024
KB = D // P
T = 256
NT = T // P
HD = 64
CH = 64
NCH = T // CH
RP, AP3, GP = 2, 3, 3
AW = GW = 384
FFN, FEXP, NE = 2816, 3584, 8
FT, ET = FFN // P, FEXP // P
NM = NE * ET
DECAY = 0.6065306597126334
RMS_EPS, GN_EPS = 1e-5, 64e-5
PI = 3.14159265358979
LN256 = 5.545177444479562
ROUND = 12582912.0
C1, C2, C3 = 6.28125, 1.9350051879882812e-03, 3.0198680390e-07

CAP = 96
RING = 4
MRING = 7
SLOT = 3072

CHUNKS = (("r0", "r1", "k0"), ("k1", "v0", "v1"), ("wag", "aq0", "aq1"), ("aq2", "ak0", "ak1"), ("ak2", "gd"),
          ("av",), ("gq0", "gq1", "gq2"), ("gk0", "gk1", "gk2"), ("gv",), ("og0", "og1", "og2"))
WIDTH = {"gd": 16, "av": AW, "gv": GW}
UNITS = (("r0", "r1"), ("k0", "k1"), ("v0", "v1"), ("wag",), ("aq0", "aq1"), ("aq2", "ak0"), ("ak1", "ak2"), ("gd",),
         ("av", 0), ("av", 1), ("gq0", "gq1"), ("gq2", "gk0"), ("gk1", "gk2"), ("gv", 0), ("gv", 1), ("og0", "og1"),
         ("og2",))
NU = len(UNITS)
CHUNK_OF, COL_OF, CHUNK_W = {}, {}, []
for _c, _tiles in enumerate(CHUNKS):
    _at = 0
    for _n in _tiles:
        CHUNK_OF[_n], COL_OF[_n] = _c, _at
        _at += WIDTH.get(_n, P)
    CHUNK_W.append(_at)
LAST_UNIT = [max(u for u, unit in enumerate(UNITS) if any(n in CHUNKS[c] for n in unit)) for c in range(len(CHUNKS))]
OUT_ORDER = (2, 3, 4, 5, 6, 7, 0, 1)
OUT_K = (3, 3, 2)
OUT_BANKS = (0, 1, 6, 7)
NCI, NCO = len(CHUNKS), len(OUT_K)
LAYER_LOADS = (NCI + NCO + FT, NCI + NCO)
LAYER0 = (0, LAYER_LOADS[0])
MOE0 = sum(LAYER_LOADS)
FFN0 = NCI + NCO
FFN_ROUNDS = (FT - 2) // RING - 1
assert MOE0 % RING == 0 and ET % (2 * MRING) == 0 and ET % RING == 0

PCOL, _at = {}, 0
for _n, _w in (("mix_g", 8), ("ffn_g", 8), ("mu", 7), ("w0", 2), ("a0", 2), ("kk", 2), ("ka", 2), ("rk", 2),
               ("lng", 2), ("lnb", 2), ("v0", 2), ("gb", 3), ("gn", 1), ("fin", 8)):
    PCOL[_n] = _at
    _at += _w
NPAR = _at
CCOL, _at = {}, 0
for _n, _w in (("ident", 128), ("ones", 128), ("strict", 128), ("incl", 128), ("lev", 6 * 128), ("rot", 128),
               ("blk", 128), ("lnw", 384), ("reset", 768), ("freq", 1), ("tri8", 64), ("before", 128),
               ("slot", CAP)):
    CCOL[_n] = _at
    _at += _w
NCON = _at


def constants():
    import numpy as np
    c = np.zeros((P, NCON), np.float32)

    def put(name, a):
        c[:a.shape[0], CCOL[name]:CCOL[name] + a.shape[1]] = a

    j, i = np.arange(P)[:, None], np.arange(P)[None, :]
    same = j // CH == i // CH
    put("ident", j == i)
    put("ones", np.ones((P, P)))
    put("strict", (j < i) & same)
    put("incl", (j <= i) & same)
    put("lev", np.concatenate([(j >> (n + 1) == i >> (n + 1)) & ((j >> n) % 2 == 0) & ((i >> n) % 2 == 1)
                               for n in range(6)], axis=1))
    dj, di = j % HD, i % HD
    head = j // HD == i // HD
    put("rot", head * (1.0 * ((di >= 8) & (di < 16) & (dj == di - 8)) - 1.0 * ((di < 8) & (dj == di + 8))))
    put("blk", head)
    w = np.zeros((T, T))
    qi, kj = np.arange(T)[:, None], np.arange(T)[None, :]
    for window, dil in ((128, 1), (512, 4), (2048, 16)):
        w += (qi >= kj) & (qi % dil == kj % dil) & (qi // dil - kj // dil <= window // dil)
    lw = np.where(w > 0, np.log(np.maximum(w, 1)), -1e30)
    put("lnw", np.concatenate([lw[:P, :P], lw[P:, :]], axis=1))
    put("reset", np.broadcast_to((np.arange(768) % CH != 0)[None, :], (P, 768)))
    half = 8
    inv = np.float32(500000.0) ** (-np.arange(half, dtype=np.float32) / np.float32(half))
    f = np.zeros((P, 1), np.float32)
    for p in range(P):
        if p % HD < 16:
            f[p] = inv[p % 8]
    put("freq", f)
    e = np.arange(8)
    put("before", j < i)
    put("slot", np.broadcast_to(np.arange(CAP)[None, :], (P, CAP)))
    put("tri8", np.broadcast_to((e[None, :] < e[:, None]).reshape(1, 64), (P, 64)))
    return c


def build_trunk(nc, xT, pos, con, par, lora, small, v1, router, w_in, w_out, w_ffn, w_moe, out):
    with ExitStack() as ctx:
        address = {}

        def sb(name, shape, dt=F32):
            address[name] = (nc.sbuf_base + 31) // 32 * 32
            return ctx.enter_context(nc.sbuf_tensor(name, shape, dt))

        sems = {}

        def S(name):
            if name not in sems:
                sems[name] = ctx.enter_context(nc.semaphore(name))
            return sems[name]

        def rounded(name, x, shape, at=0):
            return nc.alloc_sbuf_tensor_at(name, shape, F32R, offset=address[x] + 4 * at)

        ring = sb("ring", [P, RING, SLOT])
        hT = sb("hT", [P, KB, T])
        uT = sb("uT", [P, KB, T])
        mixT = sb("mixT", [P, KB, T])
        lent = sb("lent", [P, (MRING - RING) * SLOT])
        mats = sb("mats", [P, 5, 1024])
        vfirst = sb("vfirst", [P, RP, T])
        cst = sb("cst", [P, NCON])
        prm = sb("prm", [P, 2, NPAR])
        lor = sb("lor", [P, 2, 256])
        sml = sb("sml", [16, 2, 640])
        v1s = sb("v1s", [P, RP, 16])
        rts = sb("rts", [P, KB, NE])
        cosT = sb("cosT", [P, T])
        sinT = sb("sinT", [P, T])
        std = sb("std", [P, T])
        rstd = sb("rstd", [P, T])
        epsr = sb("epsr", [P, 3])
        sttmp = sb("sttmp", [P, RP, P])

        ypad = sb("ypad", [P, 7, T + 1])
        lent_at = [0]

        def part(n, *dims):
            at = lent_at[0]
            lent_at[0] += n
            x = lent[:, at:at + n]
            names = "abc"[:len(dims) + 1]
            if not dims:
                return x
            spec = " ".join(names)
            return x.rearrange(f"p ({spec}) -> p {spec}", **dict(zip(names, dims)))

        ym = part(7 * T, 7)
        aqk = sb("aqk", [P, 6, T])
        av = sb("av", [P, NT, AW])
        gqk = sb("gqk", [P, 6, T])
        gv = sb("gv", [P, NT, GW])
        gd = sb("gd", [16, T])
        og = sb("og", [P, 3, T])

        tw = part(T)
        sw, aa, gg, At, kk, Kt, Bt, bonus, wt = (part(RP * T, RP) for _ in range(9))
        tokm = part(4 * NT * 256, 4, NT)
        lc = sb("lc", [P, RP, NCH])
        tmps = sb("tmps", [P, 3, RP, T])
        tmpA, tmpB, tmpC = (tmps[:, i, :, :] for i in range(3))
        MT, X, ML, Y, T1 = (mats[:, i, :].rearrange("p (a b c) -> p a b c", a=2, b=4) for i in range(5))
        st = sb("st", [P, RP, P])

        bank = [ctx.enter_context(nc.psum_tensor(f"bank{i}", [P, 512], F32)) for i in range(8)]

        L_, Li, cs = tmpA, tmpB, tmpC
        nv, c0, uu = tmpA, tmpB, kk
        yp = ypad[:, :, :].rearrange("p a b -> p (a b)")
        qkf = aqk[:, :, :].rearrange("p a b -> p (a b)")
        combB = sb("combB", [P, NE, T])
        cbf = combB[:, :, :].rearrange("p a b -> p (a b)")
        sc = yp[:, 0:768].rearrange("p (b c) -> p b c", b=2)
        pt = yp[:, 768:1536].rearrange("p (b c) -> p b c", b=2)
        rtmp = yp[:, 0:512].rearrange("p (b c) -> p b c", b=2)
        gE, gEi, gU, gS = cbf[:, 0:768], cbf[:, 768:1536], yp[:, 0:768], yp[:, 768:1536]
        gatt = qkf.rearrange("p (g m c) -> p g m c", g=2, m=6)
        ktok = av
        gst = sb("gst", [P, GP, P])
        gtmp = sb("gtmp", [P, GP, P])
        lgc = sb("lgc", [P, GP, NCH])
        negb = sb("negb", [P, GP])
        mxn = sb("mxn", [P, 2, NT])
        den = sb("den", [P, 2, NT])
        rden = sb("rden", [P, 2, NT])
        sil = mats[:, 0, 0:512].rearrange("p (b t) -> p b t", b=2)
        hac = mats[:, 2, 0:512].rearrange("p (b t) -> p b t", b=2)
        hraw = mats[:, 4, 0:512].rearrange("p (b t) -> p b t", b=2)
        u_parts = rounded("u_parts", "mats", [P, 2, KB, T])
        f_high = rounded("f_high", "lent", [P, 2, 2, D])
        fd_high = rounded("fd_high", "lent", [P, 2, D], 4 * D)
        h_parts = rounded("h_parts", "lent", [P, 2, 2, T], 6 * D)
        fsil, fraw = (mats[:, 4, i * 512:(i + 1) * 512].rearrange("p (b t) -> p b t", b=2) for i in range(2))
        rt = sb("rt", [P, NT, 2, 64])
        lgt = sb("lgt", [P, NT, NE])
        sel = sb("sel", [P, NT, NE])
        posn = sb("posn", [P, NT, NE])
        nmax = sb("nmax", [P, NT])
        rsum = sb("rsum", [P, NT])
        count = sb("count", [P, 1])
        countI = sb("countI", [P, 1], I32)
        cT = cosT[0:NE, :]
        gT = combB
        yrow = tmps[:, 0:2, :, :].rearrange("p i a t -> p (i a t)")
        utok = mixT[:, :, :].rearrange("p k t -> p (k t)").rearrange("p (t d) -> p t d", t=NT)
        w_high = rounded("w_high", "mats", [P, 2, 2, D])
        ring_low = rounded("ring_low", "ring", [P, RING, SLOT])
        lent_low = rounded("lent_low", "lent", [P, MRING - RING, SLOT])
        x_high = rounded("x_high", "uT", [P, 2, KB * CAP])
        pick = gqk[:, :, :].rearrange("p a b -> p (a b)").rearrange("p (t e s) -> p t e s", t=NT, e=NE)
        pickw = ypad[:, :, :].rearrange("p a b -> p (a b)")[:, 0:NT * NE * CAP]\
            .rearrange("p (t e s) -> p t e s", t=NT, e=NE)
        silg = vfirst[:, 0, :].rearrange("p (b f) -> p b f", b=2)
        hrow = vfirst[:, 1, :].rearrange("p (b f) -> p b f", b=2)
        d_high = (rounded("down_even_high", "mats", [P, D], 4 * D), rounded("down_odd_high", "aqk", [P, D]))
        hcol = rounded("hcol", "aqk", [P, 2, 2, CAP], D)

        def C(name, n=P, at=0):
            return cst[:, CCOL[name] + at:CCOL[name] + at + n]

        def PR(l, name, i=0):
            a = PCOL[name] + i
            return prm[:, l, a:a + 1]

        ident, ones, blk = C("ident"), C("ones"), C("blk")

        def flat(a):
            return a[:, :, :].rearrange("p a b -> p (a b)")

        def loaded(eng, j):
            eng.wait_ge(S(f"slot{j % RING}_loaded"), 16 * (j // RING + 1))

        def wslot(j, w):
            return ring[:, j % RING, 0:KB * w].rearrange("p (k c) -> p k c", k=KB)

        def slot(s):
            return ring[:, s, :] if s < RING else lent[:, (s - RING) * SLOT:(s - RING + 1) * SLOT]

        def gu_slot(s):
            return slot(s)[:, 0:2 * D].rearrange("p (k m c) -> p m k c", m=2, k=KB)

        def half(x, q):
            return x[:, q * D:(q + 1) * D]

        def down_half(x):
            return x[:, 2 * D:3 * D]

        def low_slot(s):
            return ring_low[:, s, :] if s < RING else lent_low[:, s - RING, :]

        def dn_slot(s):
            return slot(s)[:, 2 * D:3 * D].rearrange("p (k c) -> p k c", k=KB)

        pb, bs = bank[0:2], bank
        hm = [(t, p) for t in range(NT) for p in range(RP)]
        block = ctx.enter_context(nc.Block())

        @block.sync
        def _(sp):
            sp.dma_start(hT[:, :, :], xT).then_inc(S("x_loaded"), 16)
            sp.dma_start(cst[:, :], con).then_inc(S("par_loaded"), 16)
            sp.dma_start(prm[:, :, :], par).then_inc(S("par_loaded"), 16)
            sp.dma_start(lor[:, :, :], lora).then_inc(S("par_loaded"), 16)
            sp.dma_start(sml[:, :, :], small).then_inc(S("par_loaded"), 16)
            sp.dma_start(v1s[:, :, :], v1).then_inc(S("par_loaded"), 16)
            sp.dma_start(rts[:, :, :], router).then_inc(S("par_loaded"), 16)

            def used(j):
                l = 0 if j < LAYER0[1] else 1
                i = j - LAYER0[l]
                if i < NCI:
                    sp.wait_ge(S("proj_done"), l * NU + LAST_UNIT[i] + 1)
                elif i < NCI + NCO:
                    sp.wait_ge(S("wout_used"), l * NCO + i - NCI + 1)
                else:
                    sp.wait_ge(S("down_done"), i - NCI - NCO + 1)

            def load(j, src, n):
                if j >= RING:
                    used(j - RING)
                sp.dma_start(ring[:, j % RING, 0:n], src).then_inc(S(f"slot{j % RING}_loaded"), 16)

            for l in range(2):
                at = 0
                for c in range(NCI):
                    load(LAYER0[l] + c, w_in[l, :, at:at + KB * CHUNK_W[c]], KB * CHUNK_W[c])
                    at += KB * CHUNK_W[c]
                at = 0
                for c in range(NCO):
                    load(LAYER0[l] + NCI + c, w_out[l, :, at:at + OUT_K[c] * D], OUT_K[c] * D)
                    at += OUT_K[c] * D
                if l == 0:
                    first = NCI + NCO
                    for c in range(RING):
                        load(first + c, w_ffn[c], SLOT)
                    with sp.Fori(0, FT // RING - 1) as it:
                        for s in range(RING):
                            sl = (first + s) % RING
                            sp.wait_ge(S("down_done"), it * RING + (s + 1))
                            sp.dma_start(ring[:, sl, :],
                                         w_ffn[bass.ds(it * RING + (RING + s), 1)].rearrange("a p n -> p (a n)"))\
                              .then_inc(S(f"slot{sl}_loaded"), 16)
                    for c in range(FT // RING * RING, FT):
                        load(first + c, w_ffn[c], SLOT)
            for c in range(MRING):
                if c < RING:
                    used(MOE0 - RING + c)
                elif c == RING:
                    sp.wait_ge(S("rmix_ready"), 2)
                    sp.wait_ge(S("gmix_ready"), 2)
                sp.dma_start(slot(c), w_moe[c]).then_inc(S(f"moe{c}_loaded"), 16)
            with sp.Fori(0, NM // MRING - 1) as it:
                for s in range(MRING):
                    sp.wait_ge(S("down_done"), it * MRING + (FT + s + 1))
                    sp.dma_start(slot(s), w_moe[bass.ds(it * MRING + (MRING + s), 1)].rearrange("a p n -> p (a n)"))\
                      .then_inc(S(f"moe{s}_loaded"), 16)
            sp.wait_ge(S("final_ready"), 1)
            sp.dma_start(out, uT[:, :, :]).then_inc(S("stored"), 16)
            sp.wait_ge(S("stored"), 16)

        @block.gpsimd
        def _(pool):
            pool.dma_start(tmpA[:, 0, :].bitcast(I32), pos.partition_broadcast(P)).then_inc(S("pos_loaded"), 16)
            pool.wait_ge(S("par_loaded"), 96)
            for l in range(2):
                for lev in range(1, 6):
                    for g in range(2):
                        if lev == 1:
                            pool.wait_ge(S("mt_ready"), 2 * l + g + 1)
                        else:
                            pool.wait_ge(S("t1_done"), l * 10 + (lev - 2) * 2 + g + 1)
                        for m in range(4):
                            last = nc.gpsimd.tensor_tensor(ML[:, g, m, :], MT[:, g, m, :], C("lev", P, lev * P),
                                                           ALU.mult)
                        last.then_inc(S("level_part"), 1)

        @block.tensor
        def _(pe):
            mm = nc.tensor.matmul

            def norm(n):
                pe.wait_ge(S("sq_ready"), n + 1)
                for k in range(KB):
                    last = mm(bank[7][:, 0:T], ones, uT[:, k, :], start=(k == 0), stop=(k == KB - 1))
                last.then_inc(S("norm_summed"), 1)

            def project(l, u):
                unit = UNITS[u]
                i = l * NU + u
                b = pb[u % 2]
                if u >= 2:
                    pe.wait_ge(S("proj_taken"), i - 1)
                if u == 0:
                    pe.wait_ge(S("u_ready"), 2 * l + 1)
                if unit[0] in ("av", "gv"):
                    c = CHUNK_OF[unit[0]]
                    loaded(pe, LAYER0[l] + c)
                    w = wslot(LAYER0[l] + c, AW)
                    t = unit[1]
                    for k in range(KB):
                        last = mm(b[:, 0:AW], uT[:, k, t * P:(t + 1) * P], w[:, k, :], start=(k == 0),
                                  stop=(k == KB - 1))
                else:
                    for i2, name in enumerate(unit):
                        c = CHUNK_OF[name]
                        loaded(pe, LAYER0[l] + c)
                        w = wslot(LAYER0[l] + c, CHUNK_W[c])
                        m = WIDTH.get(name, P)
                        for k in range(KB):
                            last = mm(b[0:m, i2 * T:(i2 + 1) * T], w[:, k, COL_OF[name]:COL_OF[name] + m], uT[:, k, :],
                                      start=(k == 0), stop=(k == KB - 1))
                last.then_inc(S("proj_done"), 1)

            def lora_up(l):
                pe.wait_ge(S("tw_ready"), l + 1)
                for b, (lo, hi) in ((2, (0, 32)), (3, (32, 64)), (4, (64, 128))):
                    for p in range(RP):
                        last = mm(bank[b][:, p * T:(p + 1) * T], lor[lo:hi, l, p * P:(p + 1) * P], tw[lo:hi, :],
                                  start=True, stop=True)
                    last.then_inc(S("lora_done"), 1)

            def value_residual():
                pe.wait_ge(S("v_mixed"), 2)
                for p in range(RP):
                    last = mm(bank[5][0:16, 0:T], v1s[:, p, :], ym[:, 4 + p, :], start=(p == 0), stop=(p == RP - 1))
                last.then_inc(S("v1_done"), 1)
                pe.wait_ge(S("v1_taken"), 1)
                for p in range(RP):
                    last = mm(bank[5][:, p * T:(p + 1) * T], sml[:, 1, p * P:(p + 1) * P], tmpA[0:16, 0, :],
                              start=True, stop=True)
                last.then_inc(S("v2_done"), 1)

            def head_sum(sig, val, done, b, src, n=512):
                pe.wait_ge(S(sig), val)
                mm(bank[b][:, 0:n], blk, src, start=True, stop=True).then_inc(S(done), 1)

            def rwkv_products(l):
                pe.wait_ge(S("score_taken"), 6 * l + 6)
                for q, (name, src) in enumerate((("a_ready", At), ("b_ready", Bt), ("k_ready", Kt), ("v_ready", ym))):
                    pe.wait_ge(S(name), l + 1)
                    if q == 0:
                        pe.wait_ge(S("sw_ready"), l + 1)
                        pe.wait_ge(S("bonus_ready"), l + 1)
                    if q == 2:
                        pe.wait_ge(S("gg_ready"), l + 1)
                    if q == 3 and l == 1:
                        pe.wait_ge(S("v_gate"), 1)
                    for t in range(NT):
                        for p in range(RP):
                            x = src[:, p, t * P:(t + 1) * P] if q < 3 else ym[:, 4 + p, t * P:(t + 1) * P]
                            last = nc.tensor.transpose(bank[2 + q][:, t * T + p * P:t * T + (p + 1) * P], x, ident)
                    last.then_inc(S("tok_done"), 1)

            def pairwise(l, n, sig, lhs, rhs):
                for g in range(2):
                    if n:
                        pe.wait_ge(S("pair_taken"), l * 8 + 2 * n + g - 1)
                    for m, (t, p) in enumerate(hm):
                        a = lhs[g * HD:(g + 1) * HD, p, t * P:(t + 1) * P]
                        b = rhs[g * HD:(g + 1) * HD, p, t * P:(t + 1) * P]
                        last = mm(bank[2 + g][:, m * P:(m + 1) * P], a, b, start=True, stop=True)
                    last.then_inc(S("pair_done"), 1)

            def level0(l):
                for g in range(2):
                    pe.wait_ge(S("y0_ready"), 2 * l + g + 1)
                    pe.wait_ge(S("tok_taken"), 4 * l + 4)
                    for m in range(4):
                        last = nc.tensor.transpose(bank[4 + g][:, m * P:(m + 1) * P], T1[:, g, m, :], ident)
                    last.then_inc(S("m0_done"), 1)

            def invert_product(l, lev):
                for g in range(2):
                    i = l * 10 + (lev - 1) * 2 + g
                    pe.wait_ge(S("level_part"), i + 1)
                    if lev == 1:
                        pe.wait_ge(S("x0_ready"), 2 * l + g + 1)
                    else:
                        pe.wait_ge(S("x_updated"), l * 8 + (lev - 2) * 2 + g + 1)
                        pe.wait_ge(S("y_updated"), i - 1)
                    for m in range(4):
                        last = mm(bank[2 + g][:, m * P:(m + 1) * P], ML[:, g, m, :], X[:, g, m, :], start=True,
                                  stop=True)
                    last.then_inc(S("t1_done"), 1)

            def invert_update(l, lev):
                for g in range(2):
                    i = l * 10 + (lev - 1) * 2 + g
                    pe.wait_ge(S("t1_taken"), i + 1)
                    if lev < 5:
                        for m in range(4):
                            last = mm(bank[4 + g][:, m * P:(m + 1) * P], Y[:, g, m, :], T1[:, g, m, :], start=True,
                                      stop=True)
                        last.then_inc(S("xd_done"), 1)
                    for m in range(4):
                        last = mm(bank[2 + g][:, m * P:(m + 1) * P], T1[:, g, m, :], Y[:, g, m, :], start=True,
                                  stop=True)
                    last.then_inc(S("yd_done"), 1)

            def rwkv_solve_nv(l):
                pe.wait_ge(S("pair_taken"), l * 8 + 4)
                for g in range(2):
                    for m, (t, p) in enumerate(hm):
                        c = p * P + g * HD
                        last = mm(bank[4][:, t * T + c:t * T + c + HD], MT[:, g, m, :], tokm[:, 3, t, c:c + HD],
                                  start=True, stop=True)
                last.then_inc(S("nv_done"), 1)
                for g in range(2):
                    for m, (t, p) in enumerate(hm):
                        c = p * P + g * HD
                        last = mm(bank[5][g * HD:(g + 1) * HD, p * T + t * P:p * T + (t + 1) * P],
                                  tokm[:, 0, t, c:c + HD], Y[:, g, m, :], start=True, stop=True)
                last.then_inc(S("wt_done"), 1)

            def rwkv_solve_c(l):
                pe.wait_ge(S("nv_taken"), l + 1)
                for g in range(2):
                    for m, (t, p) in enumerate(hm):
                        c = p * P + g * HD
                        last = mm(bank[4][:, t * T + c:t * T + c + HD], Y[:, g, m, :], nv[:, t, c:c + HD],
                                  start=True, stop=True)
                last.then_inc(S("c_done"), 1)

            def rwkv_scan(l):
                ob = bank[5]
                pe.wait_ge(S("wt_taken"), l + 1)
                pe.wait_ge(S("c_taken"), l + 1)
                for n in range(NCH):
                    t, q = n // 2, n % 2
                    rows = slice(q * CH, (q + 1) * CH)
                    tk = slice(n * CH, (n + 1) * CH)
                    pe.wait_ge(S("state_ready"), l * (NCH + 1) + n + 1)
                    for p in range(RP):
                        last = mm(bank[4][rows, p * P:(p + 1) * P], wt[:, p, tk], st[:, p, :], start=True, stop=True)
                    last.then_inc(S("us_done"), 1)
                    for p in range(RP):
                        mm(ob[:, p * T + n * CH:p * T + (n + 1) * CH], st[:, p, :], ym[:, p, tk],
                           start=(n == 0 and p == 0), stop=False, skip_group_check=True)
                    pe.wait_ge(S("u_chunk"), l * NCH + n + 1)
                    for p in range(RP):
                        cc = slice(p * P, (p + 1) * P)
                        mm(bank[4][:, cc], tokm[rows, 1, t, cc], uu[rows, t, cc], start=True, stop=False)
                        last = mm(bank[4][:, cc], tokm[rows, 2, t, cc], tokm[rows, 3, t, cc], start=False, stop=True)
                    last.then_inc(S("ds_done"), 1)
                    out_block(l, n)
                pe.wait_ge(S("pair_taken"), l * 8 + 8)
                for g in range(2):
                    for m, (t, p) in enumerate(hm):
                        c = p * P + g * HD
                        o = ob[g * HD:(g + 1) * HD, p * T + t * P:p * T + (t + 1) * P]
                        mm(o, uu[:, t, c:c + HD], T1[:, g, m, :], start=False, stop=False, skip_group_check=True)
                        last = mm(o, tokm[:, 3, t, c:c + HD], X[:, g, m, :], start=False, stop=True,
                                  skip_group_check=True)
                last.then_inc(S("ro_done"), 1)

            def group_norm(l):
                head_sum("ro_taken", l + 1, "mean_done", 2, flat(tmpC))
                out_block(l, 4)
                head_sum("cen_ready", l + 1, "var_done", 3, flat(tmpB))
                out_block(l, 5)

            def rotary(l, i):
                pe.wait_ge(S("proj_taken"), l * NU + 5 + i)
                if i > 0:
                    pe.wait_ge(S("rot_taken"), l * 3 + i)
                for s in range(2):
                    last = mm(bank[6][:, s * T:(s + 1) * T], C("rot"), aqk[:, 2 * i + s, :], start=True, stop=True)
                last.then_inc(S("rot_done"), 1)

            def scores(l, h):
                p, g = h // 2, h % 2
                i = l * 6 + h
                r = slice(g * HD, (g + 1) * HD)
                pe.wait_ge(S("qk_ready"), 3 * l + 3)
                if h < 2:
                    pe.wait_ge(S("gg_ready"), l + 1)
                    if l == 1:
                        pe.wait_ge(S("v_gate"), 1)
                else:
                    pe.wait_ge(S("score_taken"), i - 1)
                for t in range(NT):
                    n = (t + 1) * P
                    last = mm(bank[4 + g][:, t * P:t * P + n], aqk[r, p, t * P:(t + 1) * P], aqk[r, 3 + p, 0:n],
                              start=True, stop=True)
                last.then_inc(S("score_done"), 1)

            def attend(l, h):
                p, g = h // 2, h % 2
                i = l * 6 + h
                pe.wait_ge(S("prob_ready"), i + 1)
                if h >= 1:
                    pe.wait_ge(S("pt_taken"), i)
                for b in range(3):
                    last = nc.tensor.transpose(bank[6][:, b * P:(b + 1) * P], sc[:, h % 2, b * P:(b + 1) * P], ident)
                last.then_inc(S("pt_done"), 1)
                pe.wait_ge(S("pt_taken"), i + 1)
                if g == 0 and h > 0:
                    pe.wait_ge(S("ao_taken"), l * 3 + p)
                r = slice(g * HD, (g + 1) * HD)
                v = slice(h * HD, (h + 1) * HD)
                mm(bank[7][r, 0:P], av[:, 0, v], pt[:, h % 2, 0:P], start=True, stop=True)
                mm(bank[7][r, P:T], av[:, 0, v], pt[:, h % 2, P:2 * P], start=True, stop=False)
                mm(bank[7][r, P:T], av[:, 1, v], pt[:, h % 2, 2 * P:3 * P], start=False, stop=True)\
                    .then_inc(S("ao_done"), 1)

            def gla_gates(l):
                pe.wait_ge(S("proj_taken"), l * NU + NU)
                for p in range(GP):
                    b = bank[p // 2]
                    last = mm(b[:, (p % 2) * T:(p % 2 + 1) * T], sml[:, l, 256 + p * P:256 + (p + 1) * P], gd[:, :],
                              start=True, stop=True)
                last.then_inc(S("gz_done"), 1)

            def gla_token_major(l):
                pe.wait_ge(S("gk_ready"), l + 1)
                pe.wait_ge(S("pt_taken"), 6 * l + 6)
                pe.wait_ge(S("ao_taken"), 3 * l + 3)
                for t in range(NT):
                    for p in range(GP):
                        last = nc.tensor.transpose(bank[6 + t][:, p * P:(p + 1) * P], gqk[:, 3 + p, t * P:(t + 1) * P],
                                                   ident)
                last.then_inc(S("ktok_done"), 1)

            def gla_pairwise(l, part_):
                if part_ == 0:
                    pe.wait_ge(S("ktok_taken"), l + 1)
                else:
                    pe.wait_ge(S("gatt_taken"), 2 * l + 1)
                for g in range(2):
                    r = slice(g * HD, (g + 1) * HD)
                    for m in (range(4), range(4, 6))[part_]:
                        t, p = m // 3, m % 3
                        last = mm(bank[6 + g][:, (m % 4) * P:(m % 4 + 1) * P], gqk[r, 3 + p, t * P:(t + 1) * P],
                                  gqk[r, p, t * P:(t + 1) * P], start=True, stop=True)
                last.then_inc(S("gatt_done"), 1)

            def gla_scan(l, n):
                t, q = n // 2, n % 2
                rows = slice(q * CH, (q + 1) * CH)
                if n == 0:
                    pe.wait_ge(S("gatt_taken"), 2 * l + 2)
                pe.wait_ge(S("gstate_ready"), l * (NCH + 1) + n + 1)
                for p in range(GP):
                    mm(bank[p // 2][:, (p % 2) * T + n * CH:(p % 2) * T + (n + 1) * CH], gst[:, p, :],
                       gqk[:, p, n * CH:(n + 1) * CH], start=(n == 0 and p != 1), stop=False,
                       skip_group_check=True)
                for p in range(GP):
                    cc = slice(p * P, (p + 1) * P)
                    last = mm(bank[6][:, cc], ktok[rows, t, cc], gv[rows, t, cc], start=True, stop=True)
                last.then_inc(S("gds_done"), 1)

            def gla_inside(l):
                for g in range(2):
                    for m in range(6):
                        t, p = m // 3, m % 3
                        c = p * P + g * HD
                        last = mm(bank[p // 2][g * HD:(g + 1) * HD, (p % 2) * T + t * P:(p % 2) * T + (t + 1) * P],
                                  gv[:, t, c:c + HD], gatt[:, g, m, :], start=False, stop=True, skip_group_check=True)
                last.then_inc(S("go_done"), 1)

            def gla_norm(l):
                pe.wait_ge(S("go_squared"), l + 1)
                pe.wait_ge(S("gstate_ready"), (l + 1) * (NCH + 1))
                mm(bank[6][:, :], blk, gU[:, 0:512], start=True, stop=True)
                mm(bank[7][:, 0:T], blk, gU[:, 512:768], start=True, stop=True).then_inc(S("gvar_done"), 1)

            def out_block(l, i):
                c, first = min(i // 3, 2), i % 3 == 0
                j = LAYER0[l] + NCI + c
                if first:
                    loaded(pe, j)
                    if c == 0:
                        pe.wait_ge(S("ao_taken"), 3 * l + 3)
                        pe.wait_ge(S("gstd_ready"), l + 1)
                    elif c == 1:
                        pe.wait_ge(S("gmix_ready"), l + 1)
                    else:
                        pe.wait_ge(S("rmix_ready"), l + 1)
                w = ring[:, j % RING, 0:OUT_K[c] * D].rearrange("p (k c) -> p k c", k=OUT_K[c])
                for m in range(KB):
                    last = mm(bank[OUT_BANKS[m // 2]][:, (m % 2) * T:(m % 2 + 1) * T], w[:, i - 3 * c,
                              m * P:(m + 1) * P], mixT[:, OUT_ORDER[i], :], start=(i == 0 and m % 2 == 0),
                              stop=(i == KB - 1), skip_group_check=True)
                if i in (2, 5, 7):
                    last.then_inc(S("wout_used"), 1)

            def gate_up(slot, par):
                w = gu_slot(slot)
                for m in range(2):
                    for k in range(KB):
                        last = mm(bank[4 + par][:, m * T:(m + 1) * T], w[:, m, k, :], uT[:, k, :], start=(k == 0),
                                  stop=(k == KB - 1))
                last.then_inc(S("gate_up_done"), 1)

            def down(slot, par, first):
                w = dn_slot(slot)
                for m in range(KB):
                    last = mm(bank[m // 2][:, (m % 2) * T:(m % 2 + 1) * T], w[:, m, :], hac[:, par, :],
                              start=(first and m % 2 == 0), stop=False, skip_group_check=True)
                last.then_inc(S("down_done"), 1)

            def channel_mixer(n_chunks, size, name, load0, base):
                first = load0 % size
                unroll = size * (1 + size % 2)
                rounds = (n_chunks - 2) // unroll

                def turn(c):
                    return 16 * ((load0 + c) // size + 1)

                pe.wait_ge(S(f"{name}{first}_loaded"), turn(0))
                if base:
                    pe.wait_ge(S("act_ready"), base)
                gate_up(first, 0)
                pe.wait_ge(S(f"{name}{(first + 1) % size}_loaded"), turn(1))
                gate_up((first + 1) % size, 1)
                pe.wait_ge(S("act_ready"), base + 1)
                down(first, 0, True)

                def pair(c, s, loads):
                    new, old = (first + 2 + s) % size, (first + 1 + s) % size
                    pe.wait_ge(S(f"{name}{new}_loaded"), loads)
                    pe.wait_ge(S("act_ready"), c + (base - 1))
                    gate_up(new, s % 2)
                    pe.wait_ge(S("act_ready"), c + base)
                    down(old, (s + 1) % 2, False)

                with pe.Fori(0, rounds) as it:
                    for s in range(unroll):
                        pair(it * unroll + (2 + s), s, it * (16 * unroll // size) + turn(2 + s))
                for c in range(2 + rounds * unroll, n_chunks):
                    pair(c, (c - 2) % unroll, turn(c))
                pe.wait_ge(S("act_ready"), base + n_chunks)
                down((first + n_chunks - 1) % size, (n_chunks - 1) % 2, False)

            def dense_gate_up(c, n=0):
                s = (FFN0 + c) % RING
                for m in range(2):
                    for k in range(KB):
                        if m == 0 and k % 4 == 0:
                            pe.wait_ge(S("ffn_low_ready"), n * 2 + (2 * c + k // 4 + 1))
                            if c == 0:
                                pe.wait_ge(S("u_low_ready"), k // 4 + 1)
                        at = (k % 4 * 2 + m) * P
                        w = [x[:, at:at + P] for x in (f_high[:, c % 2, k // 4, :], half(ring_low[:, s, :], k // 4))]
                        for x, y in ((0, 0), (0, 1), (1, 0)):
                            last = mm(bank[4 + c % 2][:, m * T:(m + 1) * T], w[x], u_parts[:, y, k, :],
                                      start=(k + x + y == 0), stop=(k == KB - 1 and x == 1))
                last.then_inc(S("gate_up_done"), 1)

            def dense_down(c, n=0, first=False):
                s = (FFN0 + c) % RING
                pe.wait_ge(S("ffn_down_low_ready"), n + (c + 1))
                pe.wait_ge(S("act_ready"), n + (c + 1))
                w = fd_high[:, c % 2, :], down_half(ring_low[:, s, :])
                for m in range(KB):
                    for x, y in ((0, 0), (0, 1), (1, 0)):
                        last = mm(bank[m // 2][:, (m % 2) * T:(m % 2 + 1) * T], w[x][:, m * P:(m + 1) * P],
                                  h_parts[:, c % 2, y, :], start=(first and m % 2 + x + y == 0), stop=False,
                                  skip_group_check=True)
                last.then_inc(S("down_done"), 1)

            def dense_mixer():
                dense_gate_up(0)
                for c in range(2):
                    dense_gate_up(c + 1)
                    dense_down(c, first=(c == 0))
                with pe.Fori(0, FFN_ROUNDS) as it:
                    for c in range(2, 2 + RING):
                        pe.wait_ge(S("act_ready"), it * RING + c)
                        dense_gate_up(c + 1, it * RING)
                        dense_down(c, it * RING)
                for c in range(2 + FFN_ROUNDS * RING, FT):
                    if c + 1 < FT:
                        pe.wait_ge(S("act_ready"), c)
                        dense_gate_up(c + 1)
                    dense_down(c)

            def route():
                pe.wait_ge(S("u_ready"), 4)
                for t in range(NT):
                    for k in range(KB):
                        last = mm(bank[6][:, t * NE:(t + 1) * NE], uT[:, k, t * P:(t + 1) * P], rts[:, k, :],
                                  start=(k == 0), stop=(k == KB - 1))
                last.then_inc(S("logits_done"), 1)
                pe.wait_ge(S("sel_ready"), 1)
                mm(bank[7][:, 0:NE], C("before"), sel[:, 0, :], start=True, stop=True)
                mm(bank[7][:, NE:2 * NE], ones, sel[:, 0, :], start=True, stop=False)
                mm(bank[7][:, NE:2 * NE], C("before"), sel[:, 1, :], start=False, stop=True)
                mm(bank[7][:, 2 * NE:3 * NE], ones, sel[:, 0, :], start=True, stop=False)
                mm(bank[7][:, 2 * NE:3 * NE], ones, sel[:, 1, :], start=False, stop=True)\
                    .then_inc(S("queues_done"), 1)

            def spread_weights():
                pe.wait_ge(S("comb_ready"), 1)
                for t in range(NT):
                    last = nc.tensor.transpose(bank[7][0:NE, t * P:(t + 1) * P], lgt[:, t, :], ident)
                last.then_inc(S("combT_done"), 1)
                pe.wait_ge(S("combT_taken"), 1)
                for e in range(NE):
                    if e >= 2:
                        pe.wait_ge(S("combB_taken"), e - 1)
                    mm(bank[6 + e % 2][:, 0:T], ident[0:NE, e:e + 1].to_broadcast([NE, P]), cT[:, :], start=True,
                       stop=True).then_inc(S("combB_done"), 1)

            def gathered_experts():
                for t in range(NT):
                    for k in range(KB):
                        last = nc.tensor.transpose(bank[2 * t + k // 4][:, (k % 4) * P:(k % 4 + 1) * P],
                                                   uT[:, k, t * P:(t + 1) * P], ident)
                    last.then_inc(S("utok_done"), 1)
                for e in range(NE):
                    pe.wait_ge(S("pick_ready"), e + 1)
                    if e >= 2:
                        pe.wait_ge(S("gt_taken"), e - 1)
                    for t in range(NT):
                        last = nc.tensor.transpose(bank[6 + e % 2][0:CAP, t * P:(t + 1) * P], pickw[:, t, e, :], ident)
                    last.then_inc(S("gt_done"), 1)
                pe.wait_ge(S("utok_taken"), NT)
                pe.wait_ge(S("gt_taken"), NE)

                def gate_up_g(slot, par, parts):
                    for q in range(2):
                        pe.wait_ge(S("low_ready"), parts + q)
                        for k in range(4):
                            w = [x[:, k * 2 * P:(k + 1) * 2 * P] for x in (w_high[:, par, q, :],
                                                                          half(low_slot(slot), q))]
                            at = (4 * q + k) * CAP
                            for x, y in ((0, 0), (0, 1), (1, 0)):
                                last = mm(bank[4 + par][0:CAP, 0:2 * P], x_high[:, x, at:at + CAP], w[y],
                                          start=(q + k + x + y == 0), stop=(q == 1 and k == 3 and x == 1))
                    last.then_inc(S("gate_up_done"), 1)

                def down_g(slot, par, first):
                    w = d_high[par], down_half(low_slot(slot))
                    for b in range(2):
                        for x, y in ((0, 0), (0, 1), (1, 0)):
                            last = mm(bank[6 + b][0:CAP, :], hcol[:, par, x, :], w[y][:, b * 512:(b + 1) * 512],
                                      start=(first and x + y == 0), stop=False, skip_group_check=True)
                    last.then_inc(S("down_done"), 1)

                def gather(e):
                    for k in range(KB):
                        for t in range(NT):
                            last = mm(bank[k // 4][:, (k % 4) * CAP:(k % 4 + 1) * CAP],
                                      utok[:, t, k * P:(k + 1) * P],
                                      pick[:, t, bass.ds(e, 1), :].rearrange("p a s -> p (a s)"), start=(t == 0),
                                      stop=(t == NT - 1))
                        if k % 4 == 3:
                            last.then_inc(S("gather_done"), 1)

                def scatter(e, n):
                    for b in range(2):
                        if n:
                            pe.wait_ge(S("h_added"), e * 4 + (b + 1))
                        for i in range(2):
                            k = 4 * n + 2 * b + i
                            last = mm(bank[b][:, i * T:(i + 1) * T], yrow[0:CAP, k * P:(k + 1) * P],
                                      gT[0:CAP, bass.ds(e, 1), :].rearrange("p a t -> p (a t)"), start=True, stop=True)
                        last.then_inc(S("scatter_done"), 1)

                def step(e, c, last=False):
                    if c + 1 < ET or not last:
                        if c + 1 == ET:
                            pe.wait_ge(S("x_low_ready"), e * 2 + 4)
                        if c >= 1:
                            pe.wait_ge(S("act_ready"), e * ET + (FT + c))
                        gate_up_g((c + 1) % MRING, (c + 1) % 2, e * 2 * ET + (2 * (c + 1) + 1))
                    if c + 2 == ET and not last:
                        gather(e + 1)
                    if c == ET + 1:
                        pe.wait_ge(S("yrow_first"), e + 1)
                        pe.wait_ge(S("yrow_second"), e + 1)
                        scatter(e, 0)
                    pe.wait_ge(S("act_ready"), e * ET + (FT + c + 1))
                    if c >= 2:
                        pe.wait_ge(S("hcol_low_ready"), e * ET + (c - 1))
                    nc.tensor.transpose(bank[2 + c % 2][:, 0:CAP], hrow[0:CAP, c % 2, :],
                                        ident[0:CAP, 0:CAP]).then_inc(S("hcol_done"), 1)
                    if c >= 1:
                        down_after(e, c - 1)
                    if c == ET + 1:
                        scatter(e, 1)

                def down_after(e, c):
                    pe.wait_ge(S("down_low_ready"), e * ET + (c + 1))
                    pe.wait_ge(S("hcol_low_ready"), e * ET + (c + 1))
                    down_g(c % MRING, c % 2, c % ET == 0)

                gather(0)
                pe.wait_ge(S("x_low_ready"), 2)
                gate_up_g(0, 0, 1)
                for c in range(2):
                    step(0, c)
                with pe.Fori(0, NE - 1) as e:
                    for c in range(2, ET + 2):
                        step(e, c)
                for c in range(2, ET):
                    step(NE - 1, c, True)
                down_after(NE - 1, ET - 1)
                pe.wait_ge(S("yrow_first"), NE)
                pe.wait_ge(S("yrow_second"), NE)
                for n in range(2):
                    scatter(NE - 1, n)

            pe.wait_ge(S("par_loaded"), 96)
            for l in range(2):
                norm(2 * l)
                for u in range(6):
                    project(l, u)
                rotary(l, 0)
                project(l, 6)
                rotary(l, 1)
                lora_up(l)
                rotary(l, 2)
                if l == 1:
                    value_residual()
                project(l, 7)
                pe.wait_ge(S("sw_ready"), l + 1)
                head_sum("kk2_ready", l + 1, "kksum_done", 2, flat(tmpA))
                for u in range(8, 11):
                    project(l, u)
                head_sum("rk_ready", l + 1, "rksum_done", 3, flat(bonus))
                project(l, 11)
                scores(l, 0)
                scores(l, 1)
                for h in range(5):
                    project(l, 12 + h)
                    attend(l, h)
                    if h < 4:
                        scores(l, h + 2)
                gla_gates(l)
                rwkv_products(l)
                attend(l, 5)
                pe.wait_ge(S("tok_taken"), 4 * l + 2)
                pairwise(l, 0, None, Bt, At)
                level0(l)
                invert_product(l, 1)
                invert_update(l, 1)
                invert_product(l, 2)
                gla_token_major(l)
                invert_update(l, 2)
                invert_product(l, 3)
                gla_pairwise(l, 0)
                invert_update(l, 3)
                invert_product(l, 4)
                gla_pairwise(l, 1)
                invert_update(l, 4)
                gla_scan(l, 0)
                invert_product(l, 5)
                gla_scan(l, 1)
                invert_update(l, 5)
                gla_scan(l, 2)
                pe.wait_ge(S("y_updated"), l * 10 + 10)
                pairwise(l, 1, None, Kt, At)
                gla_scan(l, 3)
                gla_inside(l)
                rwkv_solve_nv(l)
                pe.wait_ge(S("r_ready"), l + 1)
                pairwise(l, 2, None, Bt, ym)
                pairwise(l, 3, None, Kt, ym)
                gla_norm(l)
                rwkv_solve_c(l)
                rwkv_scan(l)
                group_norm(l)
                out_block(l, 6)
                out_block(l, 7)
                norm(2 * l + 1)
                if l == 0:
                    dense_mixer()
                else:
                    route()
                    pe.wait_ge(S("count_ready"), 1)
                    most = pe.value_load(countI[0:1, 0:1], min_val=0, max_val=T)
                    with pe.If(most < CAP + 1):
                        gathered_experts()
                    with pe.Else():
                        spread_weights()
                        channel_mixer(NM, MRING, "moe", 0, FT)
            norm(4)

        @block.scalar
        def _(act):
            a = nc.scalar.activation
            chain = [0]

            def link(ins):
                chain[0] += 1
                ins.then_inc(S("act_step"), 1)
                act.wait_ge(S("act_step"), chain[0])

            def norm_std(n):
                act.wait_ge(S("norm_summed"), n + 1)
                link(a(std[:, :], bank[7][:, 0:T], ACT.Ln, scale=1.0 / D, bias=epsr[:, 0:1]))
                a(rstd[:, :], std[:, :], ACT.Exp, scale=-0.5).then_inc(S("std_ready"), 1)

            def take(l, u):
                unit = UNITS[u]
                act.wait_ge(S("proj_done"), l * NU + u + 1)
                b = pb[u % 2]
                n = len(unit)
                two = b[:, 0:n * T].rearrange("p (a t) -> p a t", a=n) if unit[0] not in ("av", "gv") else None
                if u < 4:
                    dst, src = ypad[:, 2 * u:2 * u + n, 1:T + 1], two
                elif u < 7:
                    dst, src = aqk[:, 2 * (u - 4):2 * (u - 4) + 2, :], two
                elif u == 7:
                    dst, src = gd[:, :], b[0:16, 0:T]
                elif unit[0] == "av":
                    dst, src = av[:, unit[1], :], b[:, 0:AW]
                elif u < 13:
                    dst, src = gqk[:, 2 * (u - 10):2 * (u - 10) + 2, :], two
                elif unit[0] == "gv":
                    dst, src = gv[:, unit[1], :], b[:, 0:GW]
                else:
                    dst, src = og[:, 2 * (u - 15):2 * (u - 15) + n, :], two
                a(dst, src, ACT.Copy).then_inc(S("proj_taken"), 1)

            def use_ln_exp():
                nc.scalar.preload_act_table_set("natural_log_exp_and_others")

            use_ln_exp()
            act.wait_ge(S("par_loaded"), 96)
            act.wait_ge(S("eps_set"), 1)
            for l in range(2):
                norm_std(2 * l)
                for u in range(4):
                    take(l, u)
                act.wait_ge(S("wag_mixed"), l + 1)
                a(tw[64:128, :], ym[64:128, 6, :], ACT.Sigmoid)
                a(tw[0:32, :], ym[0:32, 6, :], ACT.Tanh)
                a(tw[32:64, :], ym[32:64, 6, :], ACT.Copy).then_inc(S("tw_ready"), 1)
                if l == 0:
                    act.wait_ge(S("angles_ready"), 1)
                    a(cosT[:, :], tmpB[:, 0, :], ACT.Sin)
                    a(sinT[:, :], tmpB[:, 1, :], ACT.Sin).then_inc(S("rope_ready"), 1)
                for u in range(4, 7):
                    take(l, u)
                act.wait_ge(S("lora_done"), 3 * l + 1)
                for p in range(RP):
                    last = a(sw[:, p, :], bank[2][:, p * T:(p + 1) * T], ACT.Sigmoid, bias=PR(l, "w0", p))
                last.then_inc(S("sw_ready"), 1)
                act.wait_ge(S("lora_done"), 3 * l + 2)
                for p in range(RP):
                    last = a(aa[:, p, :], bank[3][:, p * T:(p + 1) * T], ACT.Sigmoid, bias=PR(l, "a0", p))
                last.then_inc(S("aa_ready"), 1)
                if l == 1:
                    act.wait_ge(S("v2_done"), 1)
                    for p in range(RP):
                        last = a(tmpB[:, p, :], bank[5][:, p * T:(p + 1) * T], ACT.Sigmoid, bias=PR(l, "v0", p))
                    last.then_inc(S("v_gate"), 1)
                take(l, 7)
                use_ln_exp()
                act.wait_ge(S("cs_ready"), l + 1)
                a(flat(At), flat(sw), ACT.Exp, scale=-DECAY)
                a(flat(Kt), flat(tmpC), ACT.Exp, scale=DECAY)
                act.wait_ge(S("kksum_done"), l + 1)
                a(flat(tmpA), flat(tmpC), ACT.Exp, scale=-DECAY).then_inc(S("decay_ready"), 1)
                act.wait_ge(S("kk_floor"), l + 1)
                link(a(flat(tmpB), flat(tmpB), ACT.Ln, scale=65536.0))
                a(flat(tmpB), flat(tmpB), ACT.Exp, scale=-0.5, bias=epsr[:, 2:3]).then_inc(S("kk_norm"), 1)
                for u in range(8, 12):
                    take(l, u)

                def exponentials(h):
                    i = l * 6 + h
                    act.wait_ge(S("max_ready"), i + 1)
                    for t in range(NT):
                        n = (t + 1) * P
                        x = sc[:, h % 2, t * P:t * P + n]
                        last = a(x, x, ACT.Exp, bias=mxn[:, h % 2, t:t + 1], accum_out=den[:, h % 2, t:t + 1])
                    last.then_inc(S("exp_done"), 1)

                def take_head(h):
                    i = l * 6 + h
                    act.wait_ge(S("pt_done"), i + 1)
                    if h >= 2:
                        act.wait_ge(S("ao_done"), i - 1)
                    a(pt[:, h % 2, :], bank[6][:, 0:384], ACT.Copy).then_inc(S("pt_taken"), 1)
                    if h % 2:
                        act.wait_ge(S("ao_done"), i + 1)
                        a(mixT[:, RP + h // 2, :], bank[7][:, 0:T], ACT.Copy).then_inc(S("ao_taken"), 1)

                exponentials(0)
                exponentials(1)
                for h in range(5):
                    take(l, 12 + h)
                    take_head(h)
                    if h < 4:
                        exponentials(h + 2)
                act.wait_ge(S("gz_done"), l + 1)
                act.wait_ge(S("negb_ready"), l + 1)
                for p in range(GP):
                    z, c = bank[p // 2][:, (p % 2) * T:(p % 2 + 1) * T], slice(p * T, (p + 1) * T)
                    a(gE[:, c], z, ACT.Abs, bias=PR(l, "gb", p))
                    last = a(gEi[:, c], z, ACT.Relu, scale=-1.0, bias=negb[:, p:p + 1])
                link(last)
                for q in range(4):
                    act.wait_ge(S("tok_done"), 4 * l + q + 1)
                    a(tokm[:, q, :, :].rearrange("p t c -> p (t c)"), bank[2 + q][:, :], ACT.Copy)\
                        .then_inc(S("tok_taken"), 1)
                link(a(gE[:, :], gE[:, :], ACT.Exp, scale=-1.0))
                a(gE[:, :], gE[:, :], ACT.Ln, bias=1.0).then_inc(S("gln_ready"), 1)
                take_head(5)

                def take_product(lev):
                    for g in range(2):
                        i = l * 10 + (lev - 1) * 2 + g
                        act.wait_ge(S("t1_done"), i + 1)
                        if lev > 1:
                            act.wait_ge(S("yd_done"), i - 1)
                        a(T1[:, g, :, :].rearrange("p m c -> p (m c)"), bank[2 + g][:, :], ACT.Copy)\
                            .then_inc(S("t1_taken"), 1)

                take_product(1)
                act.wait_ge(S("gcs_ready"), l + 1)
                a(gE[:, :], gU[:, :], ACT.Exp, scale=1.0 / 16)
                a(gEi[:, :], gU[:, :], ACT.Exp, scale=-1.0 / 16).then_inc(S("gdecay_ready"), 1)
                take_product(2)
                act.wait_ge(S("ktok_done"), l + 1)
                for t in range(NT):
                    last = a(ktok[:, t, :], bank[6 + t][:, 0:384], ACT.Copy)
                last.then_inc(S("ktok_taken"), 1)
                for lev in range(3, 6):
                    take_product(lev)
                act.wait_ge(S("go_done"), l + 1)
                a(gS[:, 0:512], bank[0][:, :], ACT.Copy)
                a(gS[:, 512:768], bank[1][:, 0:T], ACT.Copy)
                a(gU[:, 0:512], bank[0][:, :], ACT.Square)
                a(gU[:, 512:768], bank[1][:, 0:T], ACT.Square).then_inc(S("go_squared"), 1)
                act.wait_ge(S("nv_done"), l + 1)
                a(flat(nv), bank[4][:, :], ACT.Copy).then_inc(S("nv_taken"), 1)
                act.wait_ge(S("wt_done"), l + 1)
                a(flat(wt), bank[5][:, :], ACT.Copy).then_inc(S("wt_taken"), 1)
                act.wait_ge(S("gvar_done"), l + 1)
                a(gE[:, 0:512], bank[6][:, :], ACT.Ln, scale=1.0 / HD, bias=epsr[:, 0:1])
                link(a(gE[:, 512:768], bank[7][:, 0:T], ACT.Ln, scale=1.0 / HD, bias=epsr[:, 0:1]))
                a(gE[:, :], gE[:, :], ACT.Exp, scale=-0.5).then_inc(S("gstd_ready"), 1)
                act.wait_ge(S("c_done"), l + 1)
                a(flat(c0), bank[4][:, :], ACT.Copy).then_inc(S("c_taken"), 1)
                a(og[:, :, :].rearrange("p a t -> p (a t)"), og[:, :, :].rearrange("p a t -> p (a t)"), ACT.Silu)\
                    .then_inc(S("og_ready"), 1)
                use_ln_exp()
                act.wait_ge(S("ro_done"), l + 1)
                a(flat(tmpC), bank[5][:, :], ACT.Copy).then_inc(S("ro_taken"), 1)
                act.wait_ge(S("var_done"), l + 1)
                link(a(flat(tmpA), bank[3][:, :], ACT.Ln, scale=1.0 / HD, bias=epsr[:, 1:2]))
                a(flat(tmpA), flat(tmpA), ACT.Exp, scale=-0.5).then_inc(S("gn_std"), 1)
                norm_std(2 * l + 1)

                def silu(c, par, guard=True):
                    act.wait_ge(S("gate_up_done"), c + 1)
                    if guard:
                        act.wait_ge(S("act_ready"), c - 1)
                    a(sil[:, par, :], bank[4 + par][:, 0:T], ACT.Silu).then_inc(S("silu_done"), 1)


                def all_tokens(base, n):
                    for c in range(2):
                        silu(base + c, c, base > 0)
                    with act.Fori(0, (n - 2) // RING) as it:
                        for s in range(RING):
                            silu(it * RING + (base + 2 + s), s % 2)
                    for c in range(2 + (n - 2) // RING * RING, n):
                        silu(base + c, c % 2)

                def dense_round(c, n=0):
                    s = (FFN0 + c) % RING
                    act.wait_ge(S(f"slot{s}_loaded"), n * (16 // RING) + 16 * ((FFN0 + c) // RING + 1))
                    if c >= 2:
                        act.wait_ge(S("gate_up_done"), n + (c - 1))
                    for q in range(2):
                        a(f_high[:, c % 2, q, :], half(ring[:, s, :], q), ACT.Copy).then_inc(S("ffn_high_ready"), 1)

                def dense_round_down(c, n=0):
                    if c >= 2:
                        act.wait_ge(S("down_done"), n + (c - 1))
                    a(fd_high[:, c % 2, :], down_half(ring[:, (FFN0 + c) % RING, :]), ACT.Copy)\
                        .then_inc(S("ffn_down_high_ready"), 1)

                def dense_step(c, n=0):
                    act.wait_ge(S("gate_up_done"), n + (c + 1))
                    if c >= 2:
                        act.wait_ge(S("act_ready"), n + (c - 1))
                    a(fsil[:, c % 2, :], bank[4 + c % 2][:, 0:T], ACT.Silu).then_inc(S("silu_done"), 1)

                if l == 0:
                    dense_round(0)
                    act.wait_ge(S("u_ready"), 2)
                    for q in range(2):
                        a(u_parts[:, 0, 4 * q:4 * q + 4, :].rearrange("p k t -> p (k t)"),
                          uT[:, 4 * q:4 * q + 4, :].rearrange("p k t -> p (k t)"), ACT.Copy)\
                            .then_inc(S("u_high_ready"), 1)
                    dense_round(1)
                    dense_round_down(0)
                    for c in range(2):
                        dense_step(c)
                        dense_round(c + 2)
                        dense_round_down(c + 1)
                    with act.Fori(0, FFN_ROUNDS) as it:
                        for c in range(2, 2 + RING):
                            dense_step(c, it * RING)
                            dense_round(c + 2, it * RING)
                            dense_round_down(c + 1, it * RING)
                    for c in range(2 + FFN_ROUNDS * RING, FT):
                        dense_step(c)
                        if c + 2 < FT:
                            dense_round(c + 2)
                        if c + 1 < FT:
                            dense_round_down(c + 1)
                    use_ln_exp()
            act.wait_ge(S("logit_max"), 1)
            for t in range(NT):
                last = a(lgt[:, t, :], lgt[:, t, :], ACT.Exp, bias=nmax[:, t:t + 1])
            last.then_inc(S("logit_exp"), 1)
            act.wait_ge(S("count_ready"), 1)
            most = act.value_load(countI[0:1, 0:1], min_val=0, max_val=T)
            with act.If(most < CAP + 1):
                for t in range(NT):
                    act.wait_ge(S("utok_done"), t + 1)
                    for b in range(2):
                        last = a(utok[:, t, b * 512:(b + 1) * 512], bank[2 * t + b][:, :], ACT.Copy)
                    last.then_inc(S("utok_taken"), 1)
                for e in range(NE):
                    act.wait_ge(S("gt_done"), e + 1)
                    a(gT[0:CAP, e, :], bank[6 + e % 2][0:CAP, 0:T], ACT.Copy).then_inc(S("gt_taken"), 1)
                def round_weights(e, c):
                    act.wait_ge(S(f"moe{c % MRING}_loaded"), e * (16 * ET // MRING) + 16 * (c // MRING + 1))
                    if c >= 2:
                        act.wait_ge(S("gate_up_done"), e * ET + (FT + c - 1))
                    for q in range(2):
                        a(w_high[:, c % 2, q, :], half(slot(c % MRING), q), ACT.Copy).then_inc(S("high_ready"), 1)

                def round_tokens(e):
                    for b in range(2):
                        act.wait_ge(S("gather_done"), e * 2 + (b + 1))
                        a(x_high[:, 0, b * 4 * CAP:(b + 1) * 4 * CAP], bank[b][:, 0:4 * CAP], ACT.Copy)\
                            .then_inc(S("x_high_ready"), 1)

                def take_result(e):
                    act.wait_ge(S("down_done"), e * ET + (FT + ET))
                    a(yrow[0:CAP, 0:512], bank[6][0:CAP, :], ACT.Copy).then_inc(S("yrow_first"), 1)

                def step(e, c, last=False):
                    if c == ET + 1:
                        take_result(e)
                    act.wait_ge(S("gate_up_done"), e * ET + (FT + c + 1))
                    act.wait_ge(S("act_ready"), e * ET + (FT + c - 1))
                    a(silg[0:CAP, c % 2, :], bank[4 + c % 2][0:CAP, 0:P], ACT.Silu).then_inc(S("silu_done"), 1)
                    if c + 2 < ET or not last:
                        round_weights(e, c + 2)
                    if c + 1 == ET and not last:
                        round_tokens(e + 1)
                    if c >= 2:
                        act.wait_ge(S("down_done"), e * ET + (FT + c - 1))
                    a(d_high[c % 2][:, :], down_half(slot(c % MRING)), ACT.Copy).then_inc(S("down_high_ready"), 1)
                    act.wait_ge(S("hcol_done"), e * ET + (c + 1))
                    a(hcol[:, c % 2, 0, :], bank[2 + c % 2][:, 0:CAP], ACT.Copy).then_inc(S("hcol_high_ready"), 1)

                round_weights(0, 0)
                round_tokens(0)
                round_weights(0, 1)
                for c in range(2):
                    step(0, c)
                with act.Fori(0, NE - 1) as e:
                    for c in range(2, ET + 2):
                        step(e, c)
                for c in range(2, ET):
                    step(NE - 1, c, True)
                take_result(NE - 1)
            with act.Else():
                all_tokens(FT, NM)
            use_ln_exp()
            norm_std(4)

        @block.vector
        def _(dve):
            v = nc.vector
            tt, stt, ts = v.tensor_tensor, v.scalar_tensor_tensor, v.tensor_scalar
            chain = [0]

            def link(ins):
                chain[0] += 1
                ins.then_inc(S("dve_step"), 1)
                dve.wait_ge(S("dve_step"), chain[0])

            def tell(ins, name, val):
                ins.then_inc(S(name), 1)
                dve.wait_ge(S(name), val)

            def square(n):
                v.tensor_tensor(flat(uT), flat(hT), flat(hT), ALU.mult).then_inc(S("sq_ready"), 1)

            def scale_rows(n, g, l):
                dve.wait_ge(S("std_ready"), n + 1)
                for k in range(KB):
                    last = stt(uT[:, k, :], hT[:, k, :], PR(l, g, k), rstd[:, :], ALU.mult, ALU.mult)
                return last

            v.memset(epsr[:, 1:2], GN_EPS)
            v.memset(epsr[:, 2:3], LN256)
            v.memset(epsr[:, 0:1], RMS_EPS).then_inc(S("eps_set"), 1)
            dve.wait_ge(S("x_loaded"), 16)
            square(0)
            dve.wait_ge(S("pos_loaded"), 16)
            dve.wait_ge(S("par_loaded"), 96)

            def rotary_angles():
                link(v.tensor_copy(tmpA[:, 1, :], tmpA[:, 0, :].bitcast(I32)))
                link(ts(tmpA[:, 1, :], tmpA[:, 1, :], C("freq", 1), None, ALU.mult))
                both = [P, 2, T]
                r, k, x = tmpB[:, :, :], tmpC[:, :, :], tmpA[:, 1, :].unsqueeze(1).to_broadcast(both)
                for i, (turn, shift) in enumerate(((0.25, PI / 2), (0.0, 0.0))):
                    last = ts(tmpC[:, i, :], tmpA[:, 1, :], 1.0 / (2 * PI), turn, ALU.mult, ALU.add)
                link(last)
                link(ts(k, k, ROUND, -ROUND, ALU.add, ALU.add))
                link(stt(r, k, -C1, x, ALU.mult, ALU.add))
                link(stt(r, k, -C2, r, ALU.mult, ALU.add))
                link(stt(r, k, -C3, r, ALU.mult, ALU.add))
                link(ts(tmpB[:, 0, :], tmpB[:, 0, :], PI / 2, None, ALU.add))
                link(ts(k, r, PI, -2 * PI, ALU.is_gt, ALU.mult))
                link(tt(r, r, k, ALU.add))
                link(ts(k, r, -PI, 2 * PI, ALU.is_lt, ALU.mult))
                link(tt(r, r, k, ALU.add))
                ts(r, r, 3.1415925, -3.1415925, ALU.min, ALU.max).then_inc(S("angles_ready"), 1)

            for l in range(2):
                link(v.memset(ypad[:, :, 0:1], 0.0))
                scale_rows(2 * l, "mix_g", l).then_inc(S("u_ready"), 1)
                ts(negb[:, :], prm[:, l, PCOL["gb"]:PCOL["gb"] + GP], -1.0, None, ALU.mult)\
                    .then_inc(S("negb_ready"), 1)
                if l == 0:
                    rotary_angles()
                dve.wait_ge(S("proj_taken"), l * NU + 4)
                link(tt(ym[:, 6, :], ypad[:, 6, 0:T], ypad[:, 6, 1:T + 1], ALU.subtract))
                stt(ym[:, 6, :], ym[:, 6, :], PR(l, "mu", 6), ypad[:, 6, 1:T + 1], ALU.mult, ALU.add)\
                    .then_inc(S("wag_mixed"), 1)
                link(tt(ym[:, 0:6, :], ypad[:, 0:6, 0:T], ypad[:, 0:6, 1:T + 1], ALU.subtract))
                for i in range(6):
                    last = stt(ym[:, i, :], ym[:, i, :], PR(l, "mu", i), ypad[:, i, 1:T + 1], ALU.mult, ALU.add)
                tell(last, "v_mixed", l + 1)
                r_, k_, v_ = ym[:, 0:2, :], ym[:, 2:4, :], ym[:, 4:6, :]
                for p in range(RP):
                    last = ts(kk[:, p, :], k_[:, p, :], PR(l, "kk", p), None, ALU.mult)
                link(last)

                def rotate(i):
                    dve.wait_ge(S("rope_ready"), 1)
                    dve.wait_ge(S("rot_done"), 3 * l + i + 1)
                    x = aqk[:, 2 * i:2 * i + 2, :]
                    two = [P, 2, T]
                    tell(tt(rtmp, bank[6][:, :].rearrange("p (a t) -> p a t", a=2),
                            sinT[:, :].unsqueeze(1).to_broadcast(two), ALU.mult), "rot_taken", 3 * l + i + 1)
                    link(tt(x, x, cosT[:, :].unsqueeze(1).to_broadcast(two), ALU.mult))
                    tell(tt(x, x, rtmp, ALU.add), "qk_ready", 3 * l + i + 1)

                rotate(0)
                rotate(1)
                dve.wait_ge(S("sw_ready"), l + 1)
                link(v.tensor_tensor_scan(flat(tmpC), C("reset", 512), flat(sw), 0.0, ALU.mult, ALU.add))
                tt(flat(sw), flat(tmpC), flat(sw), ALU.subtract).then_inc(S("cs_ready"), 1)
                dve.wait_ge(S("lora_done"), 3 * l + 3)
                v.tensor_copy(flat(gg), bank[4][:, :]).then_inc(S("gg_ready"), 1)
                rotate(2)
                if l == 1:
                    dve.wait_ge(S("v1_done"), 1)
                    v.tensor_copy(tmpA[0:16, 0, :], bank[5][0:16, 0:T]).then_inc(S("v1_taken"), 1)
                    dve.wait_ge(S("v_gate"), 1)
                    link(tt(rtmp, vfirst[:, :, :], v_, ALU.subtract))
                    link(tt(rtmp, rtmp, tmpB[:, :, :], ALU.mult))
                    tell(tt(v_, v_, rtmp, ALU.add), "v_ready", 2)
                else:
                    tell(v.tensor_copy(vfirst[:, :, :], v_), "v_ready", 1)
                tt(tmpA[:, :, :], kk[:, :, :], kk[:, :, :], ALU.mult).then_inc(S("kk2_ready"), 1)
                dve.wait_ge(S("kksum_done"), l + 1)
                ts(flat(tmpB), bank[2][:, :], 1e-24, None, ALU.max).then_inc(S("kk_floor"), 1)
                dve.wait_ge(S("kk_norm"), l + 1)
                link(tt(flat(kk), flat(kk), flat(tmpB), ALU.mult))
                dve.wait_ge(S("aa_ready"), l + 1)
                for p in range(RP):
                    last = ts(tmpB[:, p, :], aa[:, p, :], -1.0, PR(l, "ka", p), ALU.add, ALU.mult)
                link(last)
                link(stt(flat(tmpB), flat(tmpB), 1.0, ym[:, 2:4, :].rearrange("p a t -> p (a t)"), ALU.add, ALU.mult))
                for p in range(RP):
                    last = stt(bonus[:, p, :], r_[:, p, :], PR(l, "rk", p), tmpB[:, p, :], ALU.mult, ALU.mult)
                last.then_inc(S("rk_ready"), 1)
                dve.wait_ge(S("decay_ready"), l + 1)
                link(tt(flat(aa), flat(aa), flat(kk), ALU.mult))
                stt(flat(At), flat(kk), -1.0, flat(At), ALU.mult, ALU.mult).then_inc(S("a_ready"), 1)
                tt(flat(Bt), flat(aa), flat(Kt), ALU.mult).then_inc(S("b_ready"), 1)
                tt(flat(Kt), flat(tmpB), flat(Kt), ALU.mult).then_inc(S("k_ready"), 1)
                v.tensor_copy(lc[:, :, :], tmpA[:, :, CH - 1::CH])
                tt(r_, r_, tmpA[:, :, :], ALU.mult).then_inc(S("r_ready"), 1)

                def soft_max(h):
                    i = l * 6 + h
                    b = h % 2
                    dve.wait_ge(S("score_done"), i + 1)
                    if h >= 2:
                        dve.wait_ge(S("pt_done"), i - 1)
                    tell(stt(sc[:, b, :], bank[4 + b][:, 0:384], 0.125, C("lnw", 384), ALU.mult, ALU.add),
                         "score_taken", i + 1)
                    for t in range(NT):
                        last = v.tensor_reduce(mxn[:, b, t:t + 1], sc[:, b, t * P:t * P + (t + 1) * P], AX.X, ALU.max,
                                               negate=True)
                    last.then_inc(S("max_ready"), 1)

                def soft_scale(h):
                    i = l * 6 + h
                    b = h % 2
                    dve.wait_ge(S("exp_done"), i + 1)
                    link(v.reciprocal(rden[:, b, :], den[:, b, :]))
                    for t in range(NT):
                        x = sc[:, b, t * P:t * P + (t + 1) * P]
                        last = ts(x, x, rden[:, b, t:t + 1], None, ALU.mult)
                    last.then_inc(S("prob_ready"), 1)

                soft_max(0)
                soft_max(1)
                dve.wait_ge(S("rksum_done"), l + 1)
                tt(bonus[:, :, :], bank[3][:, :].rearrange("p (a t) -> p a t", a=RP), v_, ALU.mult)\
                    .then_inc(S("bonus_ready"), 1)
                for h in range(6):
                    soft_scale(h)
                    if h < 4:
                        soft_max(h + 2)
                for g in range(2):
                    dve.wait_ge(S("pair_done"), l * 8 + g + 1)
                    b = bank[2 + g][:, :].rearrange("p (m c) -> p m c", m=4)
                    m4 = [P, 4, P]
                    dve.wait_ge(S("tok_taken"), 4 * l + 2)
                    tt(MT[:, g, :, :], b, C("strict").unsqueeze(1).to_broadcast(m4), ALU.mult)\
                        .then_inc(S("pair_taken"), 1)
                    dve.wait_ge(S("pair_taken"), l * 8 + g + 1)
                    tell(tt(T1[:, g, :, :], MT[:, g, :, :], C("lev").unsqueeze(1).to_broadcast(m4), ALU.mult),
                         "y0_ready", 2 * l + g + 1)
                    tt(Y[:, g, :, :], T1[:, g, :, :], ident.unsqueeze(1).to_broadcast(m4), ALU.add)\
                        .then_inc(S("mt_ready"), 1)
                dve.wait_ge(S("gln_ready"), l + 1)
                dve.wait_ge(S("ao_done"), 6 * l + 6)
                link(stt(gE[:, :], gEi[:, :], -1.0, gE[:, :], ALU.mult, ALU.subtract))
                v.tensor_tensor_scan(gU[:, :], C("reset", 768), gE[:, :], 0.0, ALU.mult, ALU.add)\
                    .then_inc(S("gcs_ready"), 1)
                for g in range(2):
                    dve.wait_ge(S("m0_done"), 2 * l + g + 1)
                    b = bank[4 + g][:, :].rearrange("p (m c) -> p m c", m=4)
                    tt(X[:, g, :, :], b, ident.unsqueeze(1).to_broadcast(m4), ALU.add).then_inc(S("x0_ready"), 1)

                def update_inverse(lev):
                    for g in range(2):
                        i = l * 10 + (lev - 1) * 2 + g
                        if lev < 5:
                            dve.wait_ge(S("xd_done"), l * 8 + (lev - 1) * 2 + g + 1)
                            b = bank[4 + g][:, :].rearrange("p (m c) -> p m c", m=4)
                            tt(X[:, g, :, :], b, X[:, g, :, :], ALU.add).then_inc(S("x_updated"), 1)
                        dve.wait_ge(S("yd_done"), i + 1)
                        b = bank[2 + g][:, :].rearrange("p (m c) -> p m c", m=4)
                        tt(Y[:, g, :, :], b, Y[:, g, :, :], ALU.add).then_inc(S("y_updated"), 1)

                def take_gla_pairs(i):
                    dve.wait_ge(S("gatt_done"), 2 * l + i + 1)
                    lo, hi = ((0, 4), (4, 6))[i]
                    for g in range(2):
                        last = v.copy_predicated(
                            gatt[:, g, lo:hi, :], C("incl").bitcast(I32).unsqueeze(1).to_broadcast([P, hi - lo, P]),
                            bank[6 + g][:, 0:(hi - lo) * P].rearrange("p (m c) -> p m c", m=hi - lo))
                    last.then_inc(S("gatt_taken"), 1)

                def gla_state(n):
                    dve.wait_ge(S("gds_done"), l * NCH + n + 1)
                    three = [P, GP, P]
                    link(tt(gtmp[:, :, :], bank[6][:, 0:384].rearrange("p (a c) -> p a c", a=GP),
                            blk.unsqueeze(1).to_broadcast(three), ALU.mult))
                    link(tt(gst[:, :, :], gst[:, :, :], gtmp[:, :, :], ALU.add))
                    tt(gst[:, :, :], gst[:, :, :], lgc[:, :, n].unsqueeze(2).to_broadcast(three), ALU.mult)\
                        .then_inc(S("gstate_ready"), 1)

                update_inverse(1)
                dve.wait_ge(S("gdecay_ready"), l + 1)
                q3 = gqk[:, 0:3, :].rearrange("p a t -> p (a t)")
                k3 = gqk[:, 3:6, :].rearrange("p a t -> p (a t)")
                tt(k3, k3, gEi[:, :], ALU.mult)
                stt(q3, q3, 0.125, gE[:, :], ALU.mult, ALU.mult).then_inc(S("gk_ready"), 1)
                v.memset(gst[:, :, :], 0.0)
                v.memset(qkf, 0.0)
                v.tensor_copy(lgc[:, :, :], gE[:, :].rearrange("p (a t) -> p a t", a=GP)[:, :, CH - 1::CH])\
                    .then_inc(S("gstate_ready"), 1)
                dve.wait_ge(S("gstate_ready"), l * (NCH + 1) + 1)
                update_inverse(2)
                take_gla_pairs(0)
                update_inverse(3)
                take_gla_pairs(1)
                update_inverse(4)
                gla_state(0)
                gla_state(1)
                update_inverse(5)
                gla_state(2)
                for n, (dst, mask) in ((1, (MT, "strict")), (2, (T1, "incl")), (3, (X, "incl"))):
                    for g in range(2):
                        dve.wait_ge(S("pair_done"), l * 8 + 2 * n + g + 1)
                        if n == 1:
                            dve.wait_ge(S("level_part"), l * 10 + 10)
                        b = bank[2 + g][:, :].rearrange("p (m c) -> p m c", m=4)
                        tt(dst[:, g, :, :], b, C(mask).unsqueeze(1).to_broadcast(m4), ALU.mult)\
                            .then_inc(S("pair_taken"), 1)
                    if n == 1:
                        gla_state(3)

                def gla_output():
                    dve.wait_ge(S("gstd_ready"), l + 1)
                    link(tt(gS[:, :], gS[:, :], gE[:, :], ALU.mult))
                    dve.wait_ge(S("og_ready"), l + 1)
                    stt(mixT[:, 5:8, :].rearrange("p a t -> p (a t)"), gS[:, :], PR(l, "gn"),
                        og[:, :, :].rearrange("p a t -> p (a t)"), ALU.mult, ALU.mult).then_inc(S("gmix_ready"), 1)

                v.memset(st[:, 0:RP, :], 0.0).then_inc(S("state_ready"), 1)
                dve.wait_ge(S("c_taken"), l + 1)
                for n in range(NCH):
                    t, q = n // 2, n % 2
                    rows = slice(q * CH, (q + 1) * CH)
                    dve.wait_ge(S("us_done"), l * NCH + n + 1)
                    tt(uu[rows, t, :], bank[4][rows, 0:T], c0[rows, t, :], ALU.add).then_inc(S("u_chunk"), 1)
                    dve.wait_ge(S("ds_done"), l * NCH + n + 1)
                    dve.wait_ge(S("state_ready"), l * (NCH + 1) + n + 1)
                    for p in range(RP):
                        last = stt(sttmp[:, p, :], bank[4][:, p * P:(p + 1) * P], lc[:, p, n:n + 1], blk, ALU.mult,
                                   ALU.mult)
                    link(last)
                    for p in range(RP):
                        last = stt(st[:, p, :], st[:, p, :], lc[:, p, n:n + 1], sttmp[:, p, :], ALU.mult, ALU.add)
                    last.then_inc(S("state_ready"), 1)
                    if n == 0:
                        gla_output()
                dve.wait_ge(S("mean_done"), l + 1)
                link(stt(flat(tmpC), bank[2][:, :], -1.0 / HD, flat(tmpC), ALU.mult, ALU.add))
                tt(flat(tmpB), flat(tmpC), flat(tmpC), ALU.mult).then_inc(S("cen_ready"), 1)
                dve.wait_ge(S("gn_std"), l + 1)
                link(tt(flat(tmpC), flat(tmpC), flat(tmpA), ALU.mult))
                for p in range(RP):
                    last = ts(tmpC[:, p, :], tmpC[:, p, :], PR(l, "lng", p), PR(l, "lnb", p), ALU.mult, ALU.add)
                link(last)
                link(tt(flat(tmpC), flat(tmpC), flat(bonus), ALU.add))
                tt(mixT[:, 0:RP, :], tmpC[:, :, :], gg[:, :, :], ALU.mult).then_inc(S("rmix_ready"), 1)
                def add_residual(name, val, banks=range(4)):
                    dve.wait_ge(S(name), val)
                    for i, b in enumerate(banks):
                        x = hT[:, 2 * i:2 * i + 2, :].rearrange("p a t -> p (a t)")
                        last = tt(x, bank[b][:, :], x, ALU.add)
                    link(last)

                add_residual("wout_used", NCO * (l + 1), OUT_BANKS)
                square(2 * l + 1)
                tell(scale_rows(2 * l + 1, "ffn_g", l), "u_ready", 2 * l + 2)

                def times_up(c, par, e):
                    dve.wait_ge(S("silu_done"), c + 1)
                    dve.wait_ge(S("down_done"), c - 1)
                    up = bank[4 + par][:, T:2 * T]
                    tt(hraw[:, par, :], up, sil[:, par, :], ALU.mult).then_inc(S("raw_ready"), 1)
                    dve.wait_ge(S("raw_ready"), c + 1)
                    tt(hac[:, par, :], hraw[:, par, :], combB[:, e, :], ALU.mult).then_inc(S("act_ready"), 1)

                def dense_rest(c, n=0):
                    x = (FFN0 + c) % RING
                    for q in range(2):
                        dve.wait_ge(S("ffn_high_ready"), n * 2 + (2 * c + q + 1))
                        tt(half(ring_low[:, x, :], q), half(ring[:, x, :], q), f_high[:, c % 2, q, :], ALU.subtract)\
                            .then_inc(S("ffn_low_ready"), 1)

                def dense_rest_down(c, n=0):
                    x = (FFN0 + c) % RING
                    dve.wait_ge(S("ffn_down_high_ready"), n + (c + 1))
                    tt(down_half(ring_low[:, x, :]), down_half(ring[:, x, :]), fd_high[:, c % 2, :], ALU.subtract)\
                        .then_inc(S("ffn_down_low_ready"), 1)

                def dense_activations(c, n=0):
                    par = c % 2
                    dve.wait_ge(S("silu_done"), n + (c + 1))
                    if c >= 2:
                        dve.wait_ge(S("down_done"), n + (c - 1))
                    tt(fraw[:, par, :], bank[4 + par][:, T:2 * T], fsil[:, par, :], ALU.mult)
                    tt(h_parts[:, par, 0, :], bank[4 + par][:, T:2 * T], fsil[:, par, :], ALU.mult)\
                        .then_inc(S("raw_ready"), 1)
                    dve.wait_ge(S("raw_ready"), n + (c + 1))
                    tt(h_parts[:, par, 1, :], fraw[:, par, :], h_parts[:, par, 0, :], ALU.subtract)\
                        .then_inc(S("act_ready"), 1)

                if l == 0:
                    dense_rest(0)
                    for q in range(2):
                        dve.wait_ge(S("u_high_ready"), q + 1)
                        tt(*(x[:, 4 * q:4 * q + 4, :].rearrange("p k t -> p (k t)")
                             for x in (u_parts[:, 1, :, :], uT[:, :, :], u_parts[:, 0, :, :])), ALU.subtract)\
                            .then_inc(S("u_low_ready"), 1)
                    dense_rest(1)
                    dense_rest_down(0)
                    for c in range(2):
                        dense_activations(c)
                        dense_rest(c + 2)
                        dense_rest_down(c + 1)
                    with dve.Fori(0, FFN_ROUNDS) as it:
                        for c in range(2, 2 + RING):
                            dense_activations(c, it * RING)
                            dense_rest(c + 2, it * RING)
                            dense_rest_down(c + 1, it * RING)
                    for c in range(2 + FFN_ROUNDS * RING, FT):
                        dense_activations(c)
                        if c + 2 < FT:
                            dense_rest(c + 2)
                        if c + 1 < FT:
                            dense_rest_down(c + 1)
                    add_residual("down_done", FT)
                    square(2)
            dve.wait_ge(S("logits_done"), 1)
            for t in range(NT):
                lg, first = lgt[:, t, :], sel[:, t, :]
                link(v.tensor_copy(lg, bank[6][:, t * NE:(t + 1) * NE]))
                v.tensor_reduce(nmax[:, t:t + 1], lg, AX.X, ALU.max, negate=True)
                other = lg.unsqueeze(1).to_broadcast([P, NE, NE])
                own = lg.unsqueeze(2).to_broadcast([P, NE, NE])
                gt = rt[:, t, 0, :].rearrange("p (a b) -> p a b", a=NE)
                eq = rt[:, t, 1, :].rearrange("p (a b) -> p a b", a=NE)
                tt(gt, other, own, ALU.is_gt)
                link(tt(eq, other, own, ALU.is_equal))
                link(tt(eq, eq, C("tri8", 64).rearrange("p (a b) -> p a b", a=NE), ALU.mult))
                link(tt(gt, gt, eq, ALU.add))
                link(v.tensor_reduce(first, gt, AX.X, ALU.add))
                link(ts(first, first, 2.0, None, ALU.is_lt))
            v.memset(count[:, :], 0.0).then_inc(S("sel_ready"), 1)
            dve.wait_ge(S("sel_ready"), 1)
            v.memset(st[:, :, 0:1], 0.0).then_inc(S("logit_max"), 1)
            dve.wait_ge(S("queues_done"), 1)
            v.tensor_reduce(count[:, :], bank[7][:, 2 * NE:3 * NE], AX.X, ALU.max)
            link(v.tensor_copy(posn[:, :, :].rearrange("p t e -> p (t e)"), bank[7][:, 0:2 * NE]))
            v.tensor_copy(countI[:, :], count[:, :]).then_inc(S("count_ready"), 1)
            dve.wait_ge(S("logit_exp"), 1)
            for t in range(NT):
                w8 = lgt[:, t, :]
                link(tt(w8, w8, sel[:, t, :], ALU.mult))
                link(v.tensor_reduce(rsum[:, t:t + 1], w8, AX.X, ALU.add))
                link(v.reciprocal(rsum[:, t:t + 1], rsum[:, t:t + 1]))
                last = ts(w8, w8, rsum[:, t:t + 1], None, ALU.mult)
            tell(last, "comb_ready", 1)
            dve.wait_ge(S("count_ready"), 1)
            most = dve.value_load(countI[0:1, 0:1], min_val=0, max_val=T)
            with dve.If(most < CAP + 1):
                for e in range(NE):
                    for t in range(NT):
                        ts(pick[:, t, e, :], C("slot", CAP), posn[:, t, e:e + 1], sel[:, t, e:e + 1], ALU.is_equal,
                           ALU.mult)
                        last = ts(pickw[:, t, e, :], C("slot", CAP), posn[:, t, e:e + 1], lgt[:, t, e:e + 1],
                                  ALU.is_equal, ALU.mult)
                    last.then_inc(S("pick_ready"), 1)
                def rest_of_weights(e, c):
                    for q in range(2):
                        dve.wait_ge(S("high_ready"), e * 2 * ET + (2 * c + q + 1))
                        tt(half(low_slot(c % MRING), q), half(slot(c % MRING), q), w_high[:, c % 2, q, :],
                           ALU.subtract).then_inc(S("low_ready"), 1)

                def rest_of_tokens(e):
                    for b in range(2):
                        dve.wait_ge(S("x_high_ready"), e * 2 + (b + 1))
                        part_ = slice(b * 4 * CAP, (b + 1) * 4 * CAP)
                        tt(x_high[:, 1, part_], bank[b][:, 0:4 * CAP], x_high[:, 0, part_], ALU.subtract)\
                            .then_inc(S("x_low_ready"), 1)

                def take_result(e):
                    dve.wait_ge(S("down_done"), e * ET + (FT + ET))
                    v.tensor_copy(yrow[0:CAP, 512:D], bank[7][0:CAP, :]).then_inc(S("yrow_second"), 1)

                def add_result(e, n):
                    for b in range(2):
                        dve.wait_ge(S("scatter_done"), e * 4 + (2 * n + b + 1))
                        k = 4 * n + 2 * b
                        x = hT[:, k:k + 2, :].rearrange("p a t -> p (a t)")
                        tt(x, bank[b][:, :], x, ALU.add).then_inc(S("h_added"), 1)

                def step(e, c, last=False):
                    if c == ET + 1:
                        take_result(e)
                    dve.wait_ge(S("silu_done"), e * ET + (FT + c + 1))
                    if c >= 2:
                        dve.wait_ge(S("hcol_done"), e * ET + (c - 1))
                    tt(hrow[0:CAP, c % 2, :], bank[4 + c % 2][0:CAP, P:2 * P], silg[0:CAP, c % 2, :], ALU.mult)\
                        .then_inc(S("act_ready"), 1)
                    if c + 2 < ET or not last:
                        rest_of_weights(e, c + 2)
                    if c + 1 == ET and not last:
                        rest_of_tokens(e + 1)
                    if c == ET + 1:
                        add_result(e, 0)
                    dve.wait_ge(S("down_high_ready"), e * ET + (c + 1))
                    tt(down_half(low_slot(c % MRING)), down_half(slot(c % MRING)), d_high[c % 2][:, :],
                       ALU.subtract).then_inc(S("down_low_ready"), 1)
                    dve.wait_ge(S("hcol_high_ready"), e * ET + (c + 1))
                    tt(hcol[:, c % 2, 1, :], bank[2 + c % 2][:, 0:CAP], hcol[:, c % 2, 0, :], ALU.subtract)\
                        .then_inc(S("hcol_low_ready"), 1)
                    if c == ET + 1:
                        add_result(e, 1)

                rest_of_weights(0, 0)
                rest_of_tokens(0)
                rest_of_weights(0, 1)
                for c in range(2):
                    step(0, c)
                with dve.Fori(0, NE - 1) as e:
                    for c in range(2, ET + 2):
                        step(e, c)
                for c in range(2, ET):
                    step(NE - 1, c, True)
                take_result(NE - 1)
                for n in range(2):
                    add_result(NE - 1, n)
                dve.wait_ge(S("h_added"), 4 * NE)
            with dve.Else():
                dve.wait_ge(S("combT_done"), 1)
                v.tensor_copy(cT[:, :], bank[7][0:NE, 0:T]).then_inc(S("combT_taken"), 1)
                for e in range(NE):
                    dve.wait_ge(S("combB_done"), e + 1)
                    v.tensor_copy(combB[:, e, :], bank[6 + e % 2][:, 0:T]).then_inc(S("combB_taken"), 1)
                dve.wait_ge(S("combB_taken"), NE)
                with dve.Fori(0, NE) as e:
                    with dve.Fori(0, ET // RING) as it:
                        for s in range(RING):
                            times_up(e * ET + it * RING + (FT + s), s % 2, bass.ds(e, 1))
                dve.wait_ge(S("down_done"), FT + NM)
                for b in range(4):
                    x = hT[:, 2 * b:2 * b + 2, :].rearrange("p a t -> p (a t)")
                    last = tt(x, bank[b][:, :], x, ALU.add)
                last.then_inc(S("h_general"), 1)
                dve.wait_ge(S("h_general"), 1)
            square(4)
            scale_rows(4, "fin", 0).then_inc(S("final_ready"), 1)


def kernel(**inputs):
    import numpy as np
    import concourse.bacc as bacc
    from concourse.bass_utils import run_bass_kernel_spmd as run

    a = {k: np.asarray(x) for k, x in inputs.items()}

    def cols(x):
        return np.swapaxes(x.reshape(x.shape[:-1] + (-1, P)), -1, -2)

    def rows(x):
        return x.reshape((-1, P) + x.shape[1:]).transpose(1, 0, 2)

    par = np.concatenate([
        cols(a["mix_norm_g"]), cols(a["ffn_norm_g"]), cols(a["rwkv_mu"]), cols(a["rwkv_w0"]), cols(a["rwkv_a0"]),
        cols(a["rwkv_k_k"]), cols(a["rwkv_k_a"]), cols(a["rwkv_r_k"].reshape(2, -1)), cols(a["rwkv_ln_g"]),
        cols(a["rwkv_ln_b"]), cols(np.concatenate([a["rwkv_v0"], a["rwkv_v0"]])), cols(a["gla_gate_b"]),
        cols(np.concatenate([a["gla_norm_g"], a["gla_norm_g"]], axis=1)),
        cols(np.stack([a["final_norm_g"], a["final_norm_g"]]))], axis=2).transpose(1, 0, 2)
    lora = np.concatenate([a["rwkv_w2"], a["rwkv_a2"], a["rwkv_g2"]], axis=1).transpose(1, 0, 2)
    small = np.stack([np.concatenate([a["rwkv_v2"][0], a["gla_gate_up"][l]], axis=1) for l in range(2)], axis=1)
    start = {"wag": 768, "av": 1664, "gv": 2816, "gd": 3200}
    for n, at in (("r", 0), ("k", 256), ("v", 512), ("aq", 896), ("ak", 1280), ("gq", 2048), ("gk", 2432),
                  ("og", 3216)):
        for i in range(3):
            start[f"{n}{i}"] = at + i * P
    w_in = np.stack([np.concatenate([rows(np.concatenate(
        [a["w_in"][l][:, start[n]:start[n] + WIDTH.get(n, P)] for n in tiles], axis=1)).reshape(P, -1)
        for tiles in CHUNKS], axis=1) for l in range(2)])
    w_out = np.stack([rows(a["w_out"][l])[:, list(OUT_ORDER), :].reshape(P, -1) for l in range(2)])

    def mixer(g, u, d):
        n, _, f = g.shape
        gu = np.stack([x.reshape(n, KB, P, f // P, P).transpose(0, 3, 2, 1, 4) for x in (g, u)], axis=4)
        return np.concatenate([gu.reshape(n * f // P, P, 2 * D), d.reshape(n * f // P, P, D)], axis=2)

    arrays = {
        "in_x": rows(a["x"][0].T), "in_pos": a["positions"].reshape(-1), "in_const": constants(), "in_par": par,
        "in_lora": lora, "in_small": small, "in_v1": rows(a["rwkv_v1"][0]), "in_router": rows(a["moe_router"][0]),
        "in_w_in": w_in, "in_w_out": w_out,
        "in_ffn": mixer(a["ffn_w_gate"], a["ffn_w_up"], a["ffn_w_down"]),
        "in_moe": mixer(a["moe_w_gate"][0], a["moe_w_up"][0], a["moe_w_down"][0]),
    }
    arrays = {k: np.ascontiguousarray(x) for k, x in arrays.items()}
    nc = bacc.Bacc("TRN2", target_bir_lowering=False, num_devices=1)
    args = [nc.dram_tensor(k, x.shape, mybir.dt.from_np(x.dtype), kind="ExternalInput").ap()
            for k, x in arrays.items()]
    out = nc.dram_tensor("out_0", (P, KB, T), F32, kind="ExternalOutput").ap()
    build_trunk(nc, *args, out)
    r = run(nc, [arrays], core_ids=[0])
    o = r.results[0]["out_0"]
    return o.transpose(2, 1, 0).reshape(1, T, D)
```
